# Optimizing a Trainium2 kernel written in Bass

```python
import math
import jax
import jax.numpy as jnp
from jax import lax
import numpy as np

D_MODEL = 1024
BATCH = 1
SEQ = 1024
DEPTH = 1

HEAD_DIM = 64
QBLK = 128
RMS_EPS = 1e-6
NEG = -1e30
FORCE = 1e30

A_HEADS = 4
A_QK = HEAD_DIM // 2
A_V = HEAD_DIM
B_HEADS = 4
B_KV = 2
B_WINDOW = 128
C_HEADS = 8
C_KV = 2
CMP_LEN = 32
CMP_STRIDE = 16
CMP_HID = 128
SLC_LEN = 64
SLC_TOPN = 8
SLC_QBLK = 64
C_WINDOW = 512

A_W = A_HEADS * A_V
B_W = B_HEADS * HEAD_DIM
C_W = C_HEADS * HEAD_DIM
D_MIX = A_W + B_W + C_W
KV_B = B_KV * HEAD_DIM
KV_C = C_KV * HEAD_DIM
N_GATES = 3 * C_HEADS
SPLIT_SIZES = (A_W, A_W, A_W, A_W, B_W, KV_B, KV_B, B_W, C_W, KV_C, KV_C, KV_C, KV_C, KV_C, KV_C, N_GATES, C_W)
IN_COLS = 4 * A_W + 2 * B_W + 2 * KV_B + 2 * C_W + 6 * KV_C + N_GATES

kernel_name = 'hybrid_diffattn_swa_nsa_parallel_heads'

def rmsnorm(x, w):
    xf = x.astype(jnp.float32)
    y = xf * lax.rsqrt(jnp.mean(xf * xf, axis=-1, keepdims=True) + RMS_EPS)
    return (y * w.astype(jnp.float32)).astype(x.dtype)

def alibi_slopes(n):
    return jnp.asarray(2.0 ** (-8.0 * np.arange(1, n + 1) / n), dtype=jnp.float32)

def diff_attention(q1, q2, k1, k2, v, lam, slopes):
    b, s, h, dq = q1.shape
    nb = s // QBLK
    scale = dq ** -0.5
    kpos = jnp.arange(s)

    def one_block(args):
        qi, q1b, q2b = args
        t = qi * QBLK + jnp.arange(QBLK)
        dist = t[:, None] - kpos[None, :]
        valid = dist >= 0
        bias = -slopes[:, None, None] * dist.astype(jnp.float32)

        def probs(qb, kk):
            sc = jnp.einsum('bqhd,bkhd->bhqk', qb, kk).astype(jnp.float32) * scale + bias
            return jax.nn.softmax(jnp.where(valid, sc, NEG), axis=-1)

        a = probs(q1b, k1) - lam * probs(q2b, k2)
        return jnp.einsum('bhqk,bkhd->bqhd', a.astype(v.dtype), v)

    q1s = q1.reshape(b, nb, QBLK, h, dq).swapaxes(0, 1)
    q2s = q2.reshape(b, nb, QBLK, h, dq).swapaxes(0, 1)
    out = lax.map(one_block, (jnp.arange(nb), q1s, q2s))
    return out.swapaxes(0, 1).reshape(b, s, h, v.shape[-1])

def banded_attention(q, k, v, window, slopes, sinks=None):
    b, s, g, r, d = q.shape
    nb = s // QBLK
    npv = -(-window // QBLK)
    nk = (npv + 1) * QBLK

    def band(x):
        xp = jnp.pad(x, ((0, 0), (npv * QBLK, 0), (0, 0), (0, 0))).reshape(b, nb + npv, QBLK, g, d)
        return jnp.concatenate([xp[:, o:o + nb] for o in range(npv + 1)], axis=2)

    kb = band(k)
    vb = band(v)
    qb = q.reshape(b, nb, QBLK, g, r, d)
    sc = jnp.einsum('bnqgrd,bnkgd->bngrqk', qb, kb).astype(jnp.float32) * d ** -0.5
    qi = np.arange(QBLK)[:, None]
    kj = np.arange(nk)[None, :]
    dist = qi + npv * QBLK - kj
    kpos = np.arange(nb)[:, None, None] * QBLK - npv * QBLK + kj[None]
    valid = (dist[None] >= 0) & (dist[None] < window) & (kpos >= 0)
    sc = sc - slopes[:, :, None, None] * jnp.asarray(dist, dtype=jnp.float32)
    sc = jnp.where(valid[:, None, None], sc, NEG)
    if sinks is None:
        p = jax.nn.softmax(sc, axis=-1)
    else:
        sink = jnp.broadcast_to(sinks.astype(jnp.float32)[:, :, None, None], (b, nb, g, r, QBLK, 1))
        p = jax.nn.softmax(jnp.concatenate([sc, sink], axis=-1), axis=-1)[..., :nk]
    o = jnp.einsum('bngrqk,bnkgd->bnqgrd', p.astype(v.dtype), vb)
    return o.reshape(b, s, g, r, d)

def overlap_matrix(n_cmp, n_slc):
    cs = np.arange(n_cmp)[:, None] * CMP_STRIDE
    ss = np.arange(n_slc)[None, :] * SLC_LEN
    ov = np.minimum(cs + CMP_LEN, ss + SLC_LEN) - np.maximum(cs, ss)
    return jnp.asarray(np.maximum(ov, 0) / CMP_LEN, dtype=jnp.float32)

def compress(x, pe, w1, w2):
    b, s, g, d = x.shape
    nch = s // CMP_STRIDE
    ratio = CMP_LEN // CMP_STRIDE
    ncmp = nch - ratio + 1
    ch = x.reshape(b, nch, CMP_STRIDE, g, d)
    blocks = jnp.concatenate([ch[:, o:o + ncmp] for o in range(ratio)], axis=2)
    blocks = blocks + pe[:, None, :]
    flat = blocks.transpose(0, 1, 3, 2, 4).reshape(b, ncmp, g, CMP_LEN * d)
    return jax.nn.silu(flat @ w1) @ w2

def nsa_attention(q, kc, vc, ks, vs, kw, vw, gates, slopes, pe_k, pe_v, wk1, wk2, wv1, wv2):
    b, s, g, r, d = q.shape
    scale = d ** -0.5
    kcmp = compress(kc, pe_k, wk1, wk2)
    vcmp = compress(vc, pe_v, wv1, wv2)
    ncmp = kcmp.shape[1]
    t = jnp.arange(s)
    cend = jnp.arange(ncmp) * CMP_STRIDE + CMP_LEN - 1
    dist_c = t[:, None] - cend[None, :]
    valid_c = dist_c >= 0
    sc = jnp.einsum('bsgrd,bcgd->bgrsc', q, kcmp).astype(jnp.float32) * scale
    sc = sc - slopes[:, :, None, None] * dist_c.astype(jnp.float32)
    p_cmp = jax.nn.softmax(jnp.where(valid_c, sc, NEG), axis=-1) * valid_c
    o_cmp = jnp.einsum('bgrsc,bcgd->bsgrd', p_cmp.astype(vcmp.dtype), vcmp)
    n_slc = s // SLC_LEN
    topn = min(SLC_TOPN, n_slc)
    imp = jnp.einsum('bgrsc,cj->bsgj', p_cmp, overlap_matrix(ncmp, n_slc))
    blk = jnp.arange(n_slc)[None, :]
    cur = (t // SLC_LEN)[:, None]
    causal = blk * SLC_LEN <= t[:, None]
    forced = (blk == 0) | (blk == cur) | (blk == cur - 1)
    score = jnp.where(causal[:, None, :], jnp.where(forced[:, None, :], FORCE, imp), NEG)
    _, idx = lax.top_k(score, topn)
    ksb = ks.reshape(b, n_slc, SLC_LEN, g, d).transpose(0, 3, 1, 2, 4)
    vsb = vs.reshape(b, n_slc, SLC_LEN, g, d).transpose(0, 3, 1, 2, 4)
    nq = s // SLC_QBLK
    bi = jnp.arange(b)[:, None, None, None]
    gi = jnp.arange(g)[None, None, :, None]

    def one_block(args):
        qi, qb, ib = args
        kg = ksb[bi, gi, ib].reshape(b, SLC_QBLK, g, topn * SLC_LEN, d)
        vg = vsb[bi, gi, ib].reshape(b, SLC_QBLK, g, topn * SLC_LEN, d)
        tq = qi * SLC_QBLK + jnp.arange(SLC_QBLK)
        kpos = (ib[..., None] * SLC_LEN + jnp.arange(SLC_LEN)).reshape(b, SLC_QBLK, g, topn * SLC_LEN)
        dist = (tq[None, :, None, None] - kpos)[:, :, :, None, :]
        scs = jnp.einsum('bqgrd,bqgkd->bqgrk', qb, kg).astype(jnp.float32) * scale
        scs = scs - slopes[None, None, :, :, None] * dist.astype(jnp.float32)
        p = jax.nn.softmax(jnp.where(dist >= 0, scs, NEG), axis=-1)
        return jnp.einsum('bqgrk,bqgkd->bqgrd', p.astype(vg.dtype), vg)

    qs = q.reshape(b, nq, SLC_QBLK, g, r, d).swapaxes(0, 1)
    ids = idx.reshape(b, nq, SLC_QBLK, g, topn).swapaxes(0, 1)
    o_slc = lax.map(one_block, (jnp.arange(nq), qs, ids)).swapaxes(0, 1).reshape(b, s, g, r, d)
    o_win = banded_attention(q, kw, vw, C_WINDOW, slopes)
    return gates[..., 0:1] * o_cmp + gates[..., 1:2] * o_slc + gates[..., 2:3] * o_win

def hybrid_layer(x, layer_idx, norm_w, w_in, w_out, lq1, lk1, lq2, lk2, subln_w, sinks,
                 pe_k, pe_v, wk1, wk2, wv1, wv2):
    b, s, _ = x.shape
    h = rmsnorm(x, norm_w) @ w_in
    offsets = np.cumsum(SPLIT_SIZES)[:-1].tolist()
    (qa, ka, va, ga, qb, kb, vb, gb, qc, kc, vc, ks, vs, kw, vw, gl, gc) = jnp.split(h, offsets, axis=-1)
    lam_init = 0.8 - 0.6 * math.exp(-0.3 * layer_idx)
    lam = (jnp.exp(jnp.sum(lq1.astype(jnp.float32) * lk1.astype(jnp.float32)))
           - jnp.exp(jnp.sum(lq2.astype(jnp.float32) * lk2.astype(jnp.float32))) + lam_init)
    qa = qa.reshape(b, s, A_HEADS, 2, A_QK)
    ka = ka.reshape(b, s, A_HEADS, 2, A_QK)
    oa = diff_attention(qa[..., 0, :], qa[..., 1, :], ka[..., 0, :], ka[..., 1, :],
                        va.reshape(b, s, A_HEADS, A_V), lam, alibi_slopes(A_HEADS))
    oa = rmsnorm(oa, subln_w) * (1.0 - lam_init)
    ya = oa.reshape(b, s, A_W) * jax.nn.silu(ga)
    rb = B_HEADS // B_KV
    ob = banded_attention(qb.reshape(b, s, B_KV, rb, HEAD_DIM), kb.reshape(b, s, B_KV, HEAD_DIM),
                          vb.reshape(b, s, B_KV, HEAD_DIM), B_WINDOW,
                          alibi_slopes(B_HEADS).reshape(B_KV, rb), sinks.reshape(B_KV, rb))
    yb = ob.reshape(b, s, B_W) * jax.nn.silu(gb)
    rc = C_HEADS // C_KV
    kvs = (b, s, C_KV, HEAD_DIM)
    gates = jax.nn.sigmoid(gl.reshape(b, s, C_KV, rc, 3))
    oc = nsa_attention(qc.reshape(b, s, C_KV, rc, HEAD_DIM), kc.reshape(kvs), vc.reshape(kvs),
                       ks.reshape(kvs), vs.reshape(kvs), kw.reshape(kvs), vw.reshape(kvs), gates,
                       alibi_slopes(C_HEADS).reshape(C_KV, rc), pe_k, pe_v, wk1, wk2, wv1, wv2)
    yc = oc.reshape(b, s, C_W) * jax.nn.silu(gc)
    return x + jnp.concatenate([ya, yb, yc], axis=-1) @ w_out

def setup_inputs(seed: int = 0) -> dict:
    key = jax.random.key(seed)
    ks = jax.random.split(key, 17)
    f32 = jnp.float32
    nrm = lambda k, shape, sc: jax.random.normal(k, shape, dtype=f32) * sc
    return {
        'x': nrm(ks[0], (BATCH, SEQ, D_MODEL), 1.0),
        'norm_w': 1.0 + nrm(ks[1], (DEPTH, D_MODEL), 0.02),
        'w_in': nrm(ks[2], (DEPTH, D_MODEL, IN_COLS), D_MODEL ** -0.5),
        'w_out': nrm(ks[3], (DEPTH, D_MIX, D_MODEL), D_MIX ** -0.5),
        'diff_lq1': nrm(ks[4], (DEPTH, A_QK), 0.1),
        'diff_lk1': nrm(ks[5], (DEPTH, A_QK), 0.1),
        'diff_lq2': nrm(ks[6], (DEPTH, A_QK), 0.1),
        'diff_lk2': nrm(ks[7], (DEPTH, A_QK), 0.1),
        'diff_subln': 1.0 + nrm(ks[8], (DEPTH, A_V), 0.02),
        'sinks': nrm(ks[9], (DEPTH, B_HEADS), 1.0),
        'cmp_pe_k': nrm(ks[10], (DEPTH, CMP_LEN, HEAD_DIM), 0.1),
        'cmp_pe_v': nrm(ks[11], (DEPTH, CMP_LEN, HEAD_DIM), 0.1),
        'cmp_wk1': nrm(ks[12], (DEPTH, CMP_LEN * HEAD_DIM, CMP_HID), (CMP_LEN * HEAD_DIM) ** -0.5),
        'cmp_wk2': nrm(ks[13], (DEPTH, CMP_HID, HEAD_DIM), CMP_HID ** -0.5),
        'cmp_wv1': nrm(ks[14], (DEPTH, CMP_LEN * HEAD_DIM, CMP_HID), (CMP_LEN * HEAD_DIM) ** -0.5),
        'cmp_wv2': nrm(ks[15], (DEPTH, CMP_HID, HEAD_DIM), CMP_HID ** -0.5),
        'final_norm': 1.0 + nrm(ks[16], (D_MODEL,), 0.02),
    }

def reference(x, norm_w, w_in, w_out, diff_lq1, diff_lk1, diff_lq2, diff_lk2, diff_subln, sinks,
              cmp_pe_k, cmp_pe_v, cmp_wk1, cmp_wk2, cmp_wv1, cmp_wv2, final_norm):
    for l in range(DEPTH):
        x = hybrid_layer(x, l, norm_w[l], w_in[l], w_out[l], diff_lq1[l], diff_lk1[l], diff_lq2[l],
                         diff_lk2[l], diff_subln[l], sinks[l], cmp_pe_k[l], cmp_pe_v[l],
                         cmp_wk1[l], cmp_wk2[l], cmp_wv1[l], cmp_wv2[l])
    return rmsnorm(x, final_norm)


_drawn_inputs = setup_inputs


def setup_inputs(seed=0):
    import zlib

    import numpy as np

    out = dict(_drawn_inputs(seed))
    spreads = {}
    factors = {'norm_w': 4.959,
     'diff_lq1': 4.69,
     'diff_lk1': 5.856,
     'diff_lq2': 8.0,
     'diff_lk2': 8.0,
     'diff_subln': 8.0,
     'sinks': 8.0,
     'cmp_pe_k': 8.0,
     'cmp_pe_v': 4.816,
     'cmp_wk1': 3.094,
     'cmp_wk2': 3.08,
     'final_norm': 2.86}
    for name, (base, spread) in spreads.items():
        noise = np.random.default_rng([zlib.crc32(name.encode()), seed]).standard_normal(out[name].shape)
        drawn = base * np.exp(spread * noise) if base else spread * noise
        out[name] = jnp.asarray(drawn.astype(out[name].dtype))
    for name, factor in factors.items():
        out[name] = (out[name] * factor).astype(out[name].dtype)
    return out
```

```python
from contextlib import ExitStack

import numpy as np

import concourse.bass as bass
from concourse import mybir

F32 = mybir.dt.float32
F32R = mybir.dt.float32r
F16 = mybir.dt.float16
BF16 = mybir.dt.bfloat16
ALU = mybir.AluOpType
ACT = mybir.ActivationFunctionType
AX = mybir.AxisListType

P = 128
D = 1024
S = 1024
KT = D // P
NT = S // P
HD = 64
A_QK = 32
EPS = 1e-6
NEG = -1e30
BIG = 3e38
TINY = 2.0 ** -126
PSCALE = 2.0 ** 14
A_H, B_H, C_H, KV = 4, 4, 8, 2
RC = C_H // KV
TC = 15
VH = A_H + 3 * KV
LAM_INIT = 0.2
CW = 640
BW = 256
NCMP = 63
SEL_T = 4
NSLC = 16
CPL = 16


def score_layout(n_tiles):
    w = n_tiles * P
    if w <= 512:
        return 0, [(0, 0, w)]
    at = P if w == 640 else 0
    return at, [(at, 0, 512 - at), (512, 512 - at, w - 512 + at)]


def chunks_of(tiles):
    return [tiles[i:i + 4] for i in range(0, len(tiles), 4)]


def norm_phase(nc, x, norm_row, ident, hT, xh, xl):
    xin = hT[:, 0:2, :]
    xs = hT[:, 2:4, :]
    nw = hT[:, 4, :]
    junk = hT[:, 5, :]
    with ExitStack() as ctx:
        ss = ctx.enter_context(nc.sbuf_tensor("x_square_sums", [P, NT], F32))
        rs = ctx.enter_context(nc.sbuf_tensor("x_rstd", [P, NT], F32))
        ms = ctx.enter_context(nc.sbuf_tensor("x_mean_squares", [P, NT], F32))
        nt = ctx.enter_context(nc.sbuf_tensor("x_newton", [P, NT], F32))
        epsc = ctx.enter_context(nc.sbuf_tensor("norm_eps", [P, 1], F32))
        tp = [ctx.enter_context(nc.psum_tensor(f"x_transposed{i}", [P, 4, P], F32)) for i in range(4)]
        x_in = [ctx.enter_context(nc.semaphore(f"x_in{i}")) for i in range(2)]
        nw_in = ctx.enter_context(nc.semaphore("nw_in"))
        eps_set = ctx.enter_context(nc.semaphore("eps_set"))
        squares = ctx.enter_context(nc.semaphore("squares_summed"))
        roots = ctx.enter_context(nc.semaphore("roots_taken"))
        inverted = ctx.enter_context(nc.semaphore("roots_inverted"))
        scaled = ctx.enter_context(nc.semaphore("x_scaled"))
        turned = ctx.enter_context(nc.semaphore("x_turned"))
        high = ctx.enter_context(nc.semaphore("x_high_written"))
        low = ctx.enter_context(nc.semaphore("x_low_written"))
        block = ctx.enter_context(nc.Block())

        @block.sync
        def _(sp):
            sp.dma_start(nw, norm_row.partition_broadcast(P)).then_inc(nw_in, 16)
            for i in range(NT):
                if i >= 2:
                    sp.wait_ge(scaled, i - 1)
                sp.dma_start(xin[:, i % 2, :], x[i * P:(i + 1) * P, :]).then_inc(x_in[i % 2], 16)

        @block.scalar
        def _(act):
            act.wait_ge(eps_set, 1)

            def high_part(i):
                for h in range(2):
                    act.wait_ge(turned, 2 * i + h + 1)
                    nc.scalar.copy(xh[:, 4 * h:4 * h + 4, i * P:(i + 1) * P], tp[(2 * i + h) % 4][:, :, :]).then_inc(high, 1)

            for i in range(NT):
                act.wait_ge(x_in[i % 2], 16 * (i // 2 + 1))
                nc.scalar.activation(junk, xin[:, i % 2, :], ACT.Square, accum_out=ss[:, i:i + 1]).then_inc(squares, 1)
                act.wait_ge(squares, i + 1)
                nc.scalar.activation(rs[:, i:i + 1], ss[:, i:i + 1], ACT.Sqrt, scale=1.0 / D,
                                     bias=epsc[:, 0:1]).then_inc(roots, 1)
                if i >= 1:
                    high_part(i - 1)
            high_part(NT - 1)

        @block.vector
        def _(dve):
            nc.vector.memset(epsc[:, :], EPS).then_inc(eps_set, 1)
            dve.wait_ge(nw_in, 16)

            def low_part(i):
                for h in range(2):
                    dve.wait_ge(high, 2 * i + h + 1)
                    nc.vector.tensor_tensor(xl[:, 4 * h:4 * h + 4, i * P:(i + 1) * P], tp[(2 * i + h) % 4][:, :, :],
                                            xh[:, 4 * h:4 * h + 4, i * P:(i + 1) * P].bitcast(F32),
                                            ALU.subtract).then_inc(low, 1)

            steps = Chain(dve, inverted)
            for i in range(NT):
                dve.wait_ge(roots, i + 1)
                r, v, t = rs[:, i:i + 1], ms[:, i:i + 1], nt[:, i:i + 1]
                steps.link(nc.vector.tensor_scalar(v, ss[:, i:i + 1], 1.0 / D, EPS, ALU.mult, ALU.add))
                steps.link(nc.vector.reciprocal(r, r))
                steps.link(nc.vector.tensor_tensor(t, r, r, ALU.mult))
                steps.link(nc.vector.tensor_tensor(t, t, v, ALU.mult))
                steps.link(nc.vector.tensor_scalar(t, t, -0.5, 1.5, ALU.mult, ALU.add))
                steps.link(nc.vector.tensor_tensor(r, r, t, ALU.mult))
                if i >= 2:
                    dve.wait_ge(turned, 2 * i - 2)
                nc.vector.scalar_tensor_tensor(out=xs[:, i % 2, :], in0=xin[:, i % 2, :], scalar=rs[:, i:i + 1],
                                               in1=nw, op0=ALU.mult, op1=ALU.mult).then_inc(scaled, 1)
                if i >= 1:
                    low_part(i - 1)
            low_part(NT - 1)

        @block.tensor
        def _(pe):
            for i in range(NT):
                pe.wait_ge(scaled, i + 1)
                for h in range(2):
                    if 2 * i + h >= 4:
                        pe.wait_ge(low, 2 * i + h - 3)
                    for k in range(4):
                        mm = nc.tensor.transpose(tp[(2 * i + h) % 4][:, k, :],
                                                 xs[:, i % 2, (4 * h + k) * P:(4 * h + k + 1) * P], ident[:, :])
                    mm.then_inc(turned, 1)


def values_phase(nc, w_val, w_gate, gate_dram, hT, xh, xl, wr, wh, wl, v3, glog):
    rest = hT[:, 0, 0:512].rearrange("p (s n) -> p s n", s=2)
    e = hT[:, 1, 0:512].rearrange("p (s n) -> p s n", s=2)
    sg = hT[:, 2, :].rearrange("p (s n) -> p s n", s=4)
    NS, W = 3 + 4, 256
    with ExitStack() as ctx:
        acc = [ctx.enter_context(nc.psum_tensor(f"nat{i}", [P, 512], F32)) for i in range(4)]
        w_in = [ctx.enter_context(nc.semaphore(f"slab_in{i}")) for i in range(2)]
        high = ctx.enter_context(nc.semaphore("slab_high"))
        low = ctx.enter_context(nc.semaphore("slab_low"))
        done = ctx.enter_context(nc.semaphore("nat_done"))
        glog_copied = ctx.enter_context(nc.semaphore("gate_logits_copied"))
        v_first = ctx.enter_context(nc.semaphore("v_first_part"))
        v_rest = ctx.enter_context(nc.semaphore("v_rest"))
        v_second = ctx.enter_context(nc.semaphore("v_second_part"))
        v_third = ctx.enter_context(nc.semaphore("v_third_part"))
        g_exp = ctx.enter_context(nc.semaphore("gate_exp"))
        g_chain = ctx.enter_context(nc.semaphore("gate_chain"))
        g_ready = ctx.enter_context(nc.semaphore("gate_ready"))
        g_out = [ctx.enter_context(nc.semaphore(f"gate_out{i}")) for i in range(4)]
        block = ctx.enter_context(nc.Block())

        def slab(t, s):
            return t[:, 2 * (s % 2):2 * (s % 2) + 2, :].rearrange("p a n -> p (a n)").rearrange("p (k n) -> p k n", k=KT)

        def heads(s):
            return 4 if s < 2 else 2

        def first_head(s):
            return 4 * s

        def store(sp, s):
            if s < 3:
                return
            for i in range(NT):
                n = (s - 3) * NT + i
                sp.wait_ge(g_ready, n + 1)
                sp.dma_start(gate_dram[i * P:(i + 1) * P, (s - 3) * W:(s - 2) * W], sg[:, n % 4, :]).then_inc(g_out[n % 4], 16)

        @block.sync
        def _(sp):
            for s in range(NS):
                if s >= 2:
                    sp.wait_ge(low, s - 1)
                src = w_val[s] if s < 3 else w_gate[s - 3]
                sp.dma_start(slab(wr, s), src).then_inc(w_in[s % 2], 16)
                if s >= 3:
                    store(sp, s - 1)
            store(sp, NS - 1)
            for i in range(4):
                sp.wait_ge(g_out[i], 16 * 8)

        @block.scalar
        def _(act):
            def split(s):
                act.wait_ge(w_in[s % 2], 16 * (s // 2 + 1))
                if s >= 2:
                    act.wait_ge(done, NT * (s - 1))
                nc.scalar.copy(slab(wh, s), slab(wr, s)).then_inc(high, 1)

            split(0)
            split(1)
            for s in range(NS):
                for i in range(NT):
                    n = s * NT + i
                    act.wait_ge(done, n + 1)
                    if s < 3:
                        nh = heads(s)
                        ins = nc.scalar.copy(v3[:, i, first_head(s):first_head(s) + nh, 0, :],
                                             acc[n % 4][:, 0:nh * HD].rearrange("p (h d) -> p h d", d=HD))
                        ins.then_inc(v_first, 1)
                    else:
                        if n - 3 * NT >= 2:
                            act.wait_ge(g_ready, n - 3 * NT - 1)
                        nc.scalar.activation(e[:, n % 2, :], acc[n % 4][:, 0:W], ACT.Exp, scale=-1.0).then_inc(g_exp, 1)
                if s + 2 < NS:
                    split(s + 2)

        @block.vector
        def _(dve):
            def split(s):
                dve.wait_ge(high, s + 1)
                nc.vector.tensor_tensor(slab(wl, s), slab(wr, s), slab(wh, s).bitcast(F32), ALU.subtract).then_inc(low, 1)

            split(0)
            split(1)
            chain = 0
            for s in range(NS):
                for i in range(NT):
                    n = s * NT + i
                    if s < 3:
                        nh = heads(s)
                        dve.wait_ge(v_first, n + 1)
                        if n >= 2:
                            dve.wait_ge(v_third, n - 1)
                        ins = nc.vector.tensor_tensor(rest[:, n % 2, 0:nh * HD].rearrange("p (h d) -> p h d", d=HD),
                                                      acc[n % 4][:, 0:nh * HD].rearrange("p (h d) -> p h d", d=HD),
                                                      v3[:, i, first_head(s):first_head(s) + nh, 0, :], ALU.subtract)
                        ins.then_inc(v_rest, 1)
                        if s == 2:
                            ins = nc.vector.tensor_copy(glog[:, i, :], acc[n % 4][:, P:P + 3 * C_H])
                            ins.then_inc(glog_copied, 1)
                    else:
                        dve.wait_ge(g_exp, n - 3 * NT + 1)
                        nc.vector.tensor_scalar(e[:, n % 2, :], e[:, n % 2, :], 1.0, None, ALU.add).then_inc(g_chain, 1)
                        chain += 1
                        dve.wait_ge(g_chain, chain)
                        nc.vector.reciprocal(e[:, n % 2, :], e[:, n % 2, :]).then_inc(g_chain, 1)
                        chain += 1
                        dve.wait_ge(g_chain, chain)
                        m = n - 3 * NT
                        if m >= 4:
                            dve.wait_ge(g_out[n % 4], 16 * (m // 4))
                        nc.vector.tensor_tensor(sg[:, n % 4, :], acc[n % 4][:, 0:W], e[:, n % 2, :],
                                                ALU.mult).then_inc(g_ready, 1)
                if s + 2 < NS:
                    split(s + 2)

        @block.gpsimd
        def _(pool):
            for s in range(3):
                nh = heads(s)
                for i in range(NT):
                    n = s * NT + i
                    r = rest[:, n % 2, 0:nh * HD].rearrange("p (h d) -> p h d", d=HD)
                    vh = v3[:, i, first_head(s):first_head(s) + nh, :, :]
                    pool.wait_ge(v_rest, n + 1)
                    nc.gpsimd.tensor_copy(vh[:, :, 1, :], r).then_inc(v_second, 1)
                    pool.wait_ge(v_second, n + 1)
                    nc.gpsimd.tensor_tensor(vh[:, :, 2, :], r, vh[:, :, 1, :], ALU.subtract).then_inc(v_third, 1)

        @block.tensor
        def _(pe):
            for s in range(NS):
                pe.wait_ge(low, s + 1)
                a, b = slab(wh, s), slab(wl, s)
                n_cols = W if s != 2 else 192
                for i in range(NT):
                    n = s * NT + i
                    if n >= 4:
                        m = n - 4
                        if m < 3 * NT:
                            pe.wait_ge(v_rest, m + 1)
                            if m >= 2 * NT:
                                pe.wait_ge(glog_copied, m - 2 * NT + 1)
                        else:
                            pe.wait_ge(g_ready, m - 3 * NT + 1)
                    for k in range(KT):
                        rows = slice(i * P, (i + 1) * P)
                        nc.tensor.matmul(acc[n % 4][:, 0:n_cols], xh[:, k, rows], a[:, k, 0:n_cols], start=(k == 0), stop=False)
                        nc.tensor.matmul(acc[n % 4][:, 0:n_cols], xh[:, k, rows], b[:, k, 0:n_cols], start=False, stop=False)
                        mm = nc.tensor.matmul(acc[n % 4][:, 0:n_cols], xl[:, k, rows], a[:, k, 0:n_cols],
                                              start=False, stop=(k == KT - 1))
                    mm.then_inc(done, 1)


def queries_phase(nc, w_feat, hT, xh, xl, wr, wh, wl):
    U = 3
    TURNS = TC // U
    with ExitStack() as ctx:
        acc = [ctx.enter_context(nc.psum_tensor(f"feat{i}", [P, 512], F32)) for i in range(2 * U)]
        w_in = [ctx.enter_context(nc.semaphore(f"chunk_in{i}")) for i in range(U)]
        high = ctx.enter_context(nc.semaphore("chunk_high"))
        low = ctx.enter_context(nc.semaphore("chunk_low"))
        done = ctx.enter_context(nc.semaphore("feat_done"))
        left = ctx.enter_context(nc.semaphore("feat_left_copied"))
        right = ctx.enter_context(nc.semaphore("feat_right_copied"))
        block = ctx.enter_context(nc.Block())

        def chunk(t, j):
            return t[:, j, :].rearrange("p (k n) -> p k n", k=KT)

        @block.sync
        def _(sp):
            for j in range(U):
                sp.dma_start(chunk(wr, j), w_feat[j]).then_inc(w_in[j], 16)
            with sp.Fori(0, TURNS - 1) as it:
                for j in range(U):
                    sp.wait_ge(low, U * it + j + 1)
                    sp.dma_start(chunk(wr, j), w_feat[U * it + (j + U)]).then_inc(w_in[j], 16)

        @block.scalar
        def _(act):
            def split(j):
                nc.scalar.copy(chunk(wh, j), chunk(wr, j)).then_inc(high, 1)

            def evacuate(it, j):
                act.wait_ge(done, 2 * U * it + (2 * j + 1))
                nc.scalar.copy(hT[:, U * it + j, 0:512], acc[2 * j][:, :]).then_inc(left, 1)

            for j in range(U):
                act.wait_ge(w_in[j], 16)
                split(j)
            with act.Fori(0, TURNS - 1) as it:
                for j in range(U):
                    evacuate(it, j)
                    act.wait_ge(w_in[j], 16 * it + 32)
                    act.wait_ge(done, 2 * U * it + (2 * j + 2))
                    split(j)
            for j in range(U):
                evacuate(TURNS - 1, j)

        @block.vector
        def _(dve):
            def split(it, j):
                dve.wait_ge(high, U * it + (j + 1))
                nc.vector.tensor_tensor(chunk(wl, j), chunk(wr, j), chunk(wh, j).bitcast(F32),
                                        ALU.subtract).then_inc(low, 1)

            def evacuate(it, j):
                dve.wait_ge(done, 2 * U * it + (2 * j + 2))
                nc.vector.tensor_copy(hT[:, U * it + j, 512:1024], acc[2 * j + 1][:, :]).then_inc(right, 1)

            for j in range(U):
                split(0, j)
            with dve.Fori(0, TURNS - 1) as it:
                for j in range(U):
                    evacuate(it, j)
                    split(it + 1, j)
            for j in range(U):
                evacuate(TURNS - 1, j)

        @block.tensor
        def _(pe):
            def products(it, j, first):
                pe.wait_ge(low, U * it + (j + 1))
                a, b = chunk(wh, j), chunk(wl, j)
                for h, copied in ((0, left), (1, right)):
                    if not first:
                        pe.wait_ge(copied, U * it + (j + 1 - U))
                    cols = slice(512 * h, 512 * h + 512)
                    for k in range(KT):
                        nc.tensor.matmul(acc[2 * j + h][:, :], a[:, k, :], xh[:, k, cols], start=(k == 0), stop=False)
                        nc.tensor.matmul(acc[2 * j + h][:, :], a[:, k, :], xl[:, k, cols], start=False, stop=False)
                        mm = nc.tensor.matmul(acc[2 * j + h][:, :], b[:, k, :], xh[:, k, cols],
                                              start=False, stop=(k == KT - 1))
                    mm.then_inc(done, 1)

            for j in range(U):
                products(0, j, True)
            with pe.Fori(1, TURNS) as it:
                for j in range(U):
                    products(it, j, False)


def after(eng, sem, value):
    if value > 0:
        eng.wait_ge(sem, value)


class Chain:

    def __init__(self, eng, sem, start=0):
        self.eng, self.sem, self.start, self.n = eng, sem, start, 0

    def link(self, ins):
        ins.then_inc(self.sem, 1)
        self.n += 1
        self.eng.wait_ge(self.sem, self.start + self.n)


def softmax_chunks(tiles_of_unit):
    runs = [chunks_of(t) for t in tiles_of_unit]
    before = [0]
    for r in runs:
        before.append(before[-1] + len(r))
    return runs, before


def transpose_run(pe, nc, dst, src, run, first, ident):
    for j, kt in enumerate(run):
        c = (kt - first) * P
        mm = nc.tensor.transpose(dst[:, j, :], src[:, c:c + P], ident[:, :])
    return mm


def values_run(nc, out, ph, pl, run, v_of_tile, opens, closes):
    for j, kt in enumerate(run):
        v = v_of_tile(kt)
        o, c = opens and j == 0, closes and j == len(run) - 1
        if c and not o:
            nc.tensor.matmul(out[:, 0:2 * HD], pl[:, j, :], v[:, 0:2 * HD], start=False, stop=False)
            mm = nc.tensor.matmul(out[:, :], ph[:, j, :], v, start=False, stop=True)
        elif c:
            nc.tensor.matmul(out[:, :], ph[:, j, :], v, start=True, stop=False)
            mm = nc.tensor.matmul(out[:, 0:2 * HD], pl[:, j, :], v[:, 0:2 * HD], start=False, stop=True)
        else:
            nc.tensor.matmul(out[:, :], ph[:, j, :], v, start=o, stop=False)
            mm = nc.tensor.matmul(out[:, 0:2 * HD], pl[:, j, :], v[:, 0:2 * HD], start=False, stop=False)
    return mm


def diff_phase(nc, hT, v3, y, ident, bias_full, lams, lam_size):
    HT = A_H // 2
    UN = 2 * NT
    tiles = [list(range(n % NT + 1)) for n in range(UN)]
    runs, before = softmax_chunks(tiles)
    R = before[-1]
    LOADS = 8
    CH = 3
    with ExitStack() as ctx:
        def sb(name, shape, dt):
            return ctx.enter_context(nc.sbuf_tensor(name, shape, dt))

        def sem(name):
            return ctx.enter_context(nc.semaphore(name))

        raw = sb("a_raw", [P, 2, S], F32)
        qs = sb("a_queries", [P, 4, S], F32R)
        ks = sb("a_keys", [P, 4, S], F32R)
        bias = sb("a_bias", [P, 2, S], F32)
        pr = sb("a_probs", [P, 4, S], F32)
        pth = sb("a_probsT_high", [P, 4, 4, P], F16)
        ptl = sb("a_probsT_low", [P, 4, 4, P], F16)
        nmax = sb("a_negated_max", [P, 4], F32)
        sums = sb("a_sums", [P, 4], F32)
        lam_in = sb("a_lam_vectors", [P, 4, A_QK], F32)
        lam = sb("a_lam", [P, 8], F32)
        coef = lam[:, 6:8]
        sc = [ctx.enter_context(nc.psum_tensor(f"a_scores{i}", [P, S], F32)) for i in range(2)]
        tp = [ctx.enter_context(nc.psum_tensor(f"a_turned{i}", [P, 4, P], F32)) for i in range(2)]
        ov = [ctx.enter_context(nc.psum_tensor(f"a_out{i}", [P, 512], F32)) for i in range(2)]

        lam_loaded, lam_chain, lam_exp, lam_ready = sem("lam_loaded"), sem("lam_chain"), sem("lam_exp"), sem("lam_ready")
        raw_in = [sem(f"a_raw_in{i}") for i in range(2)]
        bias_in = [sem(f"a_bias_in{i}") for i in range(2)]
        stack_high, stack_ready = sem("a_stack_high"), sem("a_stack_ready")
        scored, biased, exped = sem("a_scored"), sem("a_biased"), sem("a_exped")
        chain, mixed = sem("a_mix_chain"), sem("a_mixed")
        turned, t_high, t_low = sem("a_turned"), sem("a_turned_high"), sem("a_turned_low")
        valued, summed = sem("a_valued"), sem("a_summed")
        block = ctx.enter_context(nc.Block())

        @block.sync
        def _(sp):
            for i in range(4):
                sp.dma_start(lam_in[:, i, :], lams[i:i + 1, :].partition_broadcast(P)).then_inc(lam_loaded, 16)
            for c in range(HT):
                for hh in range(2):
                    after(sp, biased, 2 * UN * c)
                    sp.dma_start(bias[:, hh, :], bias_full[4 * c + (2 * hh + 1)]).then_inc(bias_in[hh], 16)
                    for m in range(2):
                        for kind in range(2):
                            j = 4 * hh + 2 * m + kind
                            after(sp, stack_ready, LOADS * c + max(j - 1, 0))
                            src = hT[HD * hh + A_QK * m:HD * hh + A_QK * (m + 1), c + 2 * kind, :]
                            for band in range(4):
                                sp.dma_start(raw[A_QK * band:A_QK * (band + 1), j % 2, :], src).then_inc(raw_in[j % 2], 16)

        @block.scalar
        def _(act):
            act.wait_ge(lam_ready, 1)
            nc.scalar.activation(lam[:, 2:4], lam[:, 0:2], ACT.Exp).then_inc(lam_exp, 1)

            def stack(c, hh):
                for m in range(2):
                    for kind in range(2):
                        j = 4 * hh + 2 * m + kind
                        act.wait_ge(raw_in[j % 2], 256 * c + 64 * (j // 2 + 1))
                        dst = (qs, ks)[kind]
                        nc.scalar.activation(dst[:, 2 * hh + m, :], raw[:, j % 2, :], ACT.Copy,
                                             scale=A_QK ** -0.5 if kind == 0 else 1.0).then_inc(stack_high, 1)

            def exponentials(c, n):
                w = len(tiles[n]) * P
                for m in range(2):
                    act.wait_ge(biased, 2 * UN * c + (2 * n + m + 1))
                    s = 2 * (n % 2) + m
                    nc.scalar.activation(pr[:, s, 0:w], pr[:, s, 0:w], ACT.Exp, scale=-1.0, bias=nmax[:, s:s + 1],
                                         accum_out=sums[:, s:s + 1]).then_inc(exped, 1)

            def high_part(c, n):
                for r, run in enumerate(runs[n]):
                    g = before[n] + r
                    act.wait_ge(turned, R * c + (g + 1))
                    after(act, valued, R * c + max(g - 3, 0))
                    k = len(run)
                    nc.scalar.activation(pth[:, g % 4, 0:k, :], tp[g % 2][:, 0:k, :], ACT.Copy,
                                         scale=PSCALE).then_inc(t_high, 1)

            for c in range(HT):
                after(act, scored, 2 * UN * c)
                stack(c, 0)
                exponentials(c, 0)
                for n in range(UN):
                    if n == 1:
                        stack(c, 1)
                    if n + 1 < UN:
                        exponentials(c, n + 1)
                    high_part(c, n)

        @block.vector
        def _(dve):
            lc = Chain(dve, lam_chain)
            dve.wait_ge(lam_loaded, 64)
            for i in range(2):
                lc.link(nc.vector.tensor_tensor_reduce(out=lam_in[:, 2 * i, :], in0=lam_in[:, 2 * i, :],
                                                       in1=lam_in[:, 2 * i + 1, :], scale=1.0, scalar=0.0,
                                                       op0=ALU.mult, op1=ALU.add, accum_out=lam[:, i:i + 1]))
            nc.vector.tensor_copy(lam[:, 4:5], lam[:, 0:1]).then_inc(lam_ready, 1)
            dve.wait_ge(lam_exp, 1)
            lc.link(nc.vector.tensor_tensor(lam[:, 4:5], lam[:, 2:3], lam[:, 3:4], ALU.subtract))
            lc.link(nc.vector.tensor_scalar(lam[:, 4:5], lam[:, 4:5], LAM_INIT, None, ALU.add))
            lc.link(nc.vector.tensor_scalar(lam[:, 5:6], lam[:, 4:5], -1.0, None, ALU.mult))
            lc.link(nc.vector.tensor_tensor(lam[:, 5:6], lam[:, 5:6], lam[:, 4:5], ALU.max))
            lc.link(nc.vector.tensor_scalar(lam[:, 5:6], lam[:, 5:6], 1.0, None, ALU.add))
            lc.link(nc.vector.tensor_copy(lam_size[:, :], lam[:, 5:6]))
            lc.link(nc.vector.reciprocal(coef[:, 0:1], lam[:, 5:6]))
            lc.link(nc.vector.scalar_tensor_tensor(out=coef[:, 1:2], in0=lam[:, 4:5], scalar=-1.0, in1=coef[:, 0:1],
                                                   op0=ALU.mult, op1=ALU.mult))

            def stack(c, hh):
                for m in range(2):
                    for kind in range(2):
                        j = 4 * hh + 2 * m + kind
                        dve.wait_ge(stack_high, LOADS * c + (j + 1))
                        s = 2 * hh + m
                        if kind == 0:
                            low = qs[2 * A_QK:4 * A_QK, s, :]
                            ins = nc.vector.scalar_tensor_tensor(
                                out=low, in0=raw[2 * A_QK:4 * A_QK, j % 2, :], scalar=A_QK ** -0.5,
                                in1=low.bitcast(F32), op0=ALU.mult, op1=ALU.subtract)
                        else:
                            for band in (1, 2):
                                rows = slice(A_QK * band, A_QK * (band + 1))
                                ins = nc.vector.tensor_tensor(ks[rows, s, :], raw[rows, j % 2, :],
                                                              ks[rows, s, :].bitcast(F32), ALU.subtract)
                        ins.then_inc(stack_ready, 1)

            def add_bias(c, n):
                w = len(tiles[n]) * P
                at = score_layout(len(tiles[n]))[0]
                hh, qt = n // NT, n % NT
                if qt == 0:
                    dve.wait_ge(bias_in[hh], 16 * c + 16)
                after(dve, turned, R * c + before[max(n - 1, 0)])
                for m in range(2):
                    dve.wait_ge(scored, 2 * UN * c + (2 * n + m + 1))
                    s = 2 * (n % 2) + m
                    nc.vector.tensor_tensor_reduce(out=pr[:, s, 0:w], in0=sc[m][:, at:at + w], in1=bias[:, hh, S - w:S],
                                                   scale=-1.0, scalar=BIG, op0=ALU.add, op1=ALU.min,
                                                   accum_out=nmax[:, s:s + 1]).then_inc(biased, 1)

            def mix(c, n):
                w = len(tiles[n]) * P
                s = 2 * (n % 2)
                dve.wait_ge(exped, 2 * UN * c + (2 * n + 2))
                ch = Chain(dve, chain, CH * UN * c + CH * n)
                ch.link(nc.vector.reciprocal(sums[:, s:s + 2], sums[:, s:s + 2]))
                ch.link(nc.vector.tensor_tensor(sums[:, s:s + 2], sums[:, s:s + 2], coef, ALU.mult))
                ch.link(nc.vector.tensor_scalar(pr[:, s + 1, 0:w], pr[:, s + 1, 0:w], sums[:, s + 1:s + 2], None, ALU.mult))
                nc.vector.scalar_tensor_tensor(out=pr[:, s, 0:w], in0=pr[:, s, 0:w], scalar=sums[:, s:s + 1],
                                               in1=pr[:, s + 1, 0:w], op0=ALU.mult, op1=ALU.add).then_inc(mixed, 1)

            def low_part(c, n):
                for r, run in enumerate(runs[n]):
                    g = before[n] + r
                    dve.wait_ge(t_high, R * c + (g + 1))
                    k = len(run)
                    nc.vector.scalar_tensor_tensor(out=ptl[:, g % 4, 0:k, :], in0=tp[g % 2][:, 0:k, :], scalar=PSCALE,
                                                   in1=pth[:, g % 4, 0:k, :], op0=ALU.mult,
                                                   op1=ALU.subtract).then_inc(t_low, 1)

            def write_out(c, n):
                hh, qt = n // NT, n % NT
                dve.wait_ge(valued, R * c + before[n + 1])
                nc.vector.tensor_reduce(y[:, qt, bass.ds(2 * HD * c + HD * hh, HD)],
                                        ov[n % 2][:, 0:3 * HD].rearrange("p (t d) -> p d t", t=3),
                                        AX.X, ALU.add).then_inc(summed, 1)

            for c in range(HT):
                stack(c, 0)
                add_bias(c, 0)
                mix(c, 0)
                for n in range(UN):
                    if n == 1:
                        stack(c, 1)
                    if n + 1 < UN:
                        add_bias(c, n + 1)
                    low_part(c, n)
                    if n + 1 < UN:
                        mix(c, n + 1)
                    if n >= 1:
                        write_out(c, n - 1)
                write_out(c, UN - 1)

        @block.tensor
        def _(pe):
            def scores(c, n):
                hh, qt = n // NT, n % NT
                if qt == 0:
                    pe.wait_ge(stack_ready, LOADS * c + 4 * (hh + 1))
                after(pe, biased, 2 * UN * c + 2 * n)
                for m in range(2):
                    s = 2 * hh + m
                    for at, key, w in score_layout(max(qt + 1, 2))[1]:
                        mm = nc.tensor.matmul(sc[m][:, at:at + w], qs[:, s, qt * P:(qt + 1) * P], ks[:, s, key:key + w],
                                              start=True, stop=True)
                    mm.then_inc(scored, 1)

            def turn(c, n):
                pe.wait_ge(mixed, UN * c + (n + 1))
                for r, run in enumerate(runs[n]):
                    g = before[n] + r
                    after(pe, t_low, R * c + max(g - 1, 0))
                    transpose_run(pe, nc, tp[g % 2], pr[:, 2 * (n % 2), :], run, 0, ident).then_inc(turned, 1)

            def values(c, n):
                hh = n // NT
                after(pe, summed, UN * c + max(n - 1, 0))
                for r, run in enumerate(runs[n]):
                    g = before[n] + r
                    pe.wait_ge(t_low, R * c + (g + 1))
                    values_run(nc, ov[n % 2][:, 0:3 * HD], pth[:, g % 4], ptl[:, g % 4], run,
                               lambda kt: v3[:, kt, bass.ds(2 * c + hh, 1), :, :].rearrange("p a t d -> p (a t d)"),
                               r == 0, r == len(runs[n]) - 1).then_inc(valued, 1)

            for c in range(HT):
                scores(c, 0)
                for n in range(UN):
                    if n + 1 < UN:
                        scores(c, n + 1)
                    turn(c, n)
                    if n >= 1:
                        values(c, n - 1)
                values(c, UN - 1)


def swa_phase(nc, hT, v3, y, ident, bias_swa, sinks):
    UN = 2 * NT
    tiles = [list(range(max(n % NT - 1, 0), n % NT + 1)) for n in range(UN)]
    LOADS = 3
    CH = 1 + 2 * 3
    with ExitStack() as ctx:
        def sb(name, shape, dt):
            return ctx.enter_context(nc.sbuf_tensor(name, shape, dt))

        def sem(name):
            return ctx.enter_context(nc.semaphore(name))

        raw = sb("b_raw", [P, 3, S], F32)
        qs = sb("b_queries", [P, 2, S], F32R)
        kh = sb("b_keys_high", [P, S], F32R)
        kl = sb("b_keys_low", [P, S], F32R)
        bias = sb("b_bias", [P, 2, BW], F32)
        pr = sb("b_probs", [P, 4, BW], F32)
        pth = sb("b_probsT_high", [P, 4, 2, P], F16)
        ptl = sb("b_probsT_low", [P, 4, 2, P], F16)
        nmax = sb("b_negated_max", [P, 2, NT], F32)
        sums = sb("b_sums", [P, 2, NT], F32)
        sink_exp = sb("b_sink_exp", [P, 2, NT], F32)
        sink = sb("b_sink", [P, 2], F32)
        nsink = sb("b_negated_sink", [P, 2], F32)
        red = sb("b_out", [P, 2, NT, HD], F32)
        sc = [ctx.enter_context(nc.psum_tensor(f"b_scores{i}", [P, 512], F32)) for i in range(4)]
        tp = [ctx.enter_context(nc.psum_tensor(f"b_turned{i}", [P, 4, P], F32)) for i in range(2)]
        ov = [ctx.enter_context(nc.psum_tensor(f"b_out{i}", [P, 512], F32)) for i in range(2)]

        raw_in = [sem(f"b_raw_in{i}") for i in range(LOADS)]
        bias_in, sink_in = sem("b_bias_in"), sem("b_sink_in")
        stack_high, stack_ready = sem("b_stack_high"), sem("b_stack_ready")
        scored, biased, exped, sink_exped = sem("b_scored"), sem("b_biased"), sem("b_exped"), sem("b_sink_exped")
        turned, t_high, t_low = sem("b_turned"), sem("b_turned_high"), sem("b_turned_low")
        valued, summed, chain, headed = sem("b_valued"), sem("b_summed"), sem("b_chain"), sem("b_headed")
        block = ctx.enter_context(nc.Block())

        @block.sync
        def _(sp):
            for c in range(KV):
                after(sp, headed, 2 * c)
                sp.dma_start(bias[:, :, :], bias_swa[c]).then_inc(bias_in, 16)
                sp.dma_start(sink[:, :], sinks[c].partition_broadcast(P)).then_inc(sink_in, 16)
                after(sp, stack_ready, LOADS * c)
                for j in range(LOADS):
                    src = hT[0:HD, c + 6, :] if j == 0 else hT[HD * (j - 1):HD * j, c + 4, :]
                    for band in range(2):
                        sp.dma_start(raw[HD * band:HD * (band + 1), j, :], src).then_inc(raw_in[j], 16)

        @block.scalar
        def _(act):
            def exponentials(c, n):
                w = len(tiles[n]) * P
                hh, qt = n // NT, n % NT
                act.wait_ge(biased, UN * c + (n + 1))
                nc.scalar.activation(pr[:, n % 4, 0:w], pr[:, n % 4, 0:w], ACT.Exp, scale=-1.0,
                                     bias=nmax[:, hh, qt:qt + 1], accum_out=sums[:, hh, qt:qt + 1]).then_inc(exped, 1)
                if qt == NT - 1:
                    nc.scalar.activation(sink_exp[:, hh, :], nmax[:, hh, :], ACT.Exp,
                                         bias=sink[:, hh:hh + 1]).then_inc(sink_exped, 1)

            def high_part(c, n):
                act.wait_ge(turned, UN * c + (n + 1))
                after(act, valued, UN * c + max(n - 3, 0))
                k = len(tiles[n])
                nc.scalar.activation(pth[:, n % 4, 0:k, :], tp[n % 2][:, 0:k, :], ACT.Copy,
                                     scale=PSCALE).then_inc(t_high, 1)

            for c in range(KV):
                after(act, scored, UN * c)
                for j in range(LOADS):
                    act.wait_ge(raw_in[j], 32 * c + 32)
                    if j == 0:
                        nc.scalar.copy(kh[:, :], raw[:, j, :]).then_inc(stack_high, 1)
                    else:
                        nc.scalar.activation(qs[:, j - 1, :], raw[:, j, :], ACT.Copy,
                                             scale=HD ** -0.5).then_inc(stack_high, 1)
                exponentials(c, 0)
                exponentials(c, 1)
                for n in range(UN):
                    if n + 2 < UN:
                        exponentials(c, n + 2)
                    high_part(c, n)

        @block.vector
        def _(dve):
            def add_bias(c, n):
                w = len(tiles[n]) * P
                hh, qt = n // NT, n % NT
                after(dve, turned, UN * c + max(n - 3, 0))
                dve.wait_ge(scored, UN * c + (n + 1))
                nc.vector.tensor_tensor_reduce(out=pr[:, n % 4, 0:w], in0=sc[n % 4][:, 0:w], in1=bias[:, hh, BW - w:BW],
                                               scale=-1.0, scalar=nsink[:, hh:hh + 1], op0=ALU.add, op1=ALU.min,
                                               accum_out=nmax[:, hh, qt:qt + 1]).then_inc(biased, 1)

            def low_part(c, n):
                dve.wait_ge(t_high, UN * c + (n + 1))
                k = len(tiles[n])
                nc.vector.scalar_tensor_tensor(out=ptl[:, n % 4, 0:k, :], in0=tp[n % 2][:, 0:k, :], scalar=PSCALE,
                                               in1=pth[:, n % 4, 0:k, :], op0=ALU.mult,
                                               op1=ALU.subtract).then_inc(t_low, 1)

            def write_out(c, n, ch):
                hh, qt = n // NT, n % NT
                dve.wait_ge(valued, UN * c + (n + 1))
                nc.vector.tensor_reduce(red[:, hh, qt, :], ov[n % 2][:, 0:3 * HD].rearrange("p (t d) -> p d t", t=3),
                                        AX.X, ALU.add).then_inc(summed, 1)
                if qt < NT - 1:
                    return
                dve.wait_ge(sink_exped, 2 * c + (hh + 1))
                s = sums[:, hh, :]
                ch.link(nc.vector.tensor_tensor(s, s, sink_exp[:, hh, :], ALU.add))
                ch.link(nc.vector.tensor_scalar(s, s, PSCALE, None, ALU.mult))
                ch.link(nc.vector.reciprocal(s, s))
                dve.wait_ge(summed, UN * c + (n + 1))
                nc.vector.tensor_tensor(y[:, :, bass.ds(2 * HD * c + (A_H * HD + HD * hh), HD)], red[:, hh, :, :],
                                        s.unsqueeze(2).broadcast_to([P, NT, HD]), ALU.mult).then_inc(headed, 1)

            for c in range(KV):
                ch = Chain(dve, chain, CH * c)
                for j in range(LOADS):
                    dve.wait_ge(stack_high, LOADS * c + (j + 1))
                    if j == 0:
                        ins = nc.vector.tensor_tensor(kl[:, :], raw[:, j, :], kh[:, :].bitcast(F32), ALU.subtract)
                    else:
                        low = qs[HD:P, j - 1, :]
                        ins = nc.vector.scalar_tensor_tensor(out=low, in0=raw[HD:P, j, :], scalar=HD ** -0.5,
                                                             in1=low.bitcast(F32), op0=ALU.mult, op1=ALU.subtract)
                    ins.then_inc(stack_ready, 1)
                dve.wait_ge(sink_in, 16 * c + 16)
                ch.link(nc.vector.tensor_scalar(nsink[:, :], sink[:, :], -1.0, None, ALU.mult))
                dve.wait_ge(bias_in, 16 * c + 16)
                add_bias(c, 0)
                add_bias(c, 1)
                for n in range(UN):
                    if n + 2 < UN:
                        add_bias(c, n + 2)
                    low_part(c, n)
                    if n >= 1:
                        write_out(c, n - 1, ch)
                write_out(c, UN - 1, ch)
                assert ch.n == CH

        @block.tensor
        def _(pe):
            def scores(c, n):
                hh, qt = n // NT, n % NT
                if qt == 0:
                    pe.wait_ge(stack_ready, LOADS * c + (hh + 2))
                after(pe, biased, UN * c + max(n - 3, 0))
                q = qs[:, hh, qt * P:(qt + 1) * P]
                key = max(qt - 1, 0) * P
                nc.tensor.matmul(sc[n % 4][:, 0:BW], q, kh[:, key:key + BW], start=True, stop=False)
                nc.tensor.matmul(sc[n % 4][:, 0:BW], q, kl[:, key:key + BW], start=False, stop=True).then_inc(scored, 1)

            def turn(c, n):
                pe.wait_ge(exped, UN * c + (n + 1))
                after(pe, t_low, UN * c + max(n - 1, 0))
                transpose_run(pe, nc, tp[n % 2], pr[:, n % 4, :], tiles[n], tiles[n][0], ident).then_inc(turned, 1)

            def values(c, n):
                after(pe, summed, UN * c + max(n - 1, 0))
                pe.wait_ge(t_low, UN * c + (n + 1))
                values_run(nc, ov[n % 2][:, 0:3 * HD], pth[:, n % 4], ptl[:, n % 4], tiles[n],
                           lambda kt: v3[:, kt, bass.ds(c + A_H, 1), :, :].rearrange("p a t d -> p (a t d)"),
                           True, True).then_inc(valued, 1)

            for c in range(KV):
                scores(c, 0)
                scores(c, 1)
                for n in range(UN):
                    if n + 2 < UN:
                        scores(c, n + 2)
                    turn(c, n)
                    if n >= 1:
                        values(c, n - 1)
                values(c, UN - 1)


def compress_phase(nc, hT, w1, w2k, w2v, pe_pairs, kch, kcl, vc3):
    NC2 = KV * NCMP
    with ExitStack() as ctx:
        def sb(name, shape, dt):
            return ctx.enter_context(nc.sbuf_tensor(name, shape, dt))

        def sem(name):
            return ctx.enter_context(nc.semaphore(name))

        cc = sb("c_pairs", [P, 2, KV + 1, S], F32)
        w1s = sb("c_w1", [P, 2, CPL, P], F32)
        w2ks = sb("c_w2k", [P, P], F32)
        w2vs = sb("c_w2v", [P, HD], F32)
        pes = sb("c_pe", [P, 2, CPL], F32)
        z = sb("c_hidden", [P, 2, NC2], F32)
        e = sb("c_hidden_exp", [P, 2, NC2], F32)
        rest = sb("c_value_rest", [P, KV, HD], F32)
        hid = [ctx.enter_context(nc.psum_tensor(f"c_hid{i}", [P, 512], F32)) for i in range(2)]
        kp = ctx.enter_context(nc.psum_tensor("c_key", [P, 512], F32))
        vp = [ctx.enter_context(nc.psum_tensor(f"c_value{g}", [P, 512], F32)) for g in range(KV)]
        w_in, w2_in, pe_in, cc_in = sem("c_w1_in"), sem("c_w2_in"), sem("c_pe_in"), [sem(f"c_pairs_in{i}") for i in range(2)]
        zeroed, placed, hidden, biased, exped = sem("c_zeroed"), sem("c_pe_placed"), sem("c_hidden_done"), sem("c_hid_biased"), sem("c_hid_exp")
        chain, act_ready, keyed, valued = sem("c_chain"), sem("c_silu"), sem("c_keyed"), sem("c_value_done")
        key_high, first = sem("c_key_high"), sem("c_value_first")
        block = ctx.enter_context(nc.Block())

        @block.sync
        def _(sp):
            sp.dma_start(w1s[:, :, :, :], w1).then_inc(w_in, 16)
            sp.dma_start(pes[:, :, :], pe_pairs).then_inc(pe_in, 16)
            for kv in range(2):
                for g in range(KV):
                    src = hT[HD:P, 8 + g, :] if kv == 0 else hT[HD * g:HD * (g + 1), 14, :]
                    sp.dma_start(cc[0:HD, kv, g, :], src).then_inc(cc_in[kv], 16)
                    sp.dma_start(cc[HD:P, kv, g, 0:S - 1], src[:, 1:S]).then_inc(cc_in[kv], 16)
            sp.dma_start(w2ks[:, :], w2k).then_inc(w2_in, 16)
            sp.dma_start(w2vs[:, :], w2v).then_inc(w2_in, 16)

        @block.scalar
        def _(act):
            for kv in range(2):
                act.wait_ge(biased, kv + 1)
                nc.scalar.activation(e[:, kv, :], z[:, kv, :], ACT.Exp, scale=-1.0).then_inc(exped, 1)
            act.wait_ge(keyed, 1)
            act.wait_ge(zeroed, 3)
            nc.scalar.copy(kch[:, :, 0:NCMP], kp[:, 0:NC2].rearrange("p (g n) -> p g n", g=KV)).then_inc(key_high, 1)
            for g in range(KV):
                act.wait_ge(valued, g + 1)
                for half in range(2):
                    rows = slice(HD * half, HD * half + NCMP)
                    nc.scalar.copy(vc3[rows, g, 0, :], vp[g][rows, 0:HD]).then_inc(first, 1)

        @block.vector
        def _(dve):
            nc.vector.memset(cc[:, :, KV, :], 0.0).then_inc(chain, 1)
            nc.vector.memset(kch[:, :, NCMP:HD].bitcast(F32), 0.0).then_inc(zeroed, 1)
            nc.vector.memset(kcl[:, :, NCMP:HD].bitcast(F32), 0.0).then_inc(zeroed, 1)
            nc.vector.memset(vc3[:, :, :, :], 0.0).then_inc(zeroed, 1)
            dve.wait_ge(chain, 1)
            ch = Chain(dve, chain, 1)
            dve.wait_ge(pe_in, 16)
            nc.vector.tensor_copy(cc[:, :, KV, 0:2 * CPL:2], pes[:, :, :]).then_inc(placed, 1)
            for kv in range(2):
                dve.wait_ge(hidden, kv + 1)
                nc.vector.tensor_scalar(z[:, kv, :], hid[kv][:, 0:NC2], hid[kv][:, NC2:NC2 + 1], None,
                                        ALU.add).then_inc(biased, 1)
            for kv in range(2):
                dve.wait_ge(exped, kv + 1)
                ch.link(nc.vector.tensor_scalar(e[:, kv, :], e[:, kv, :], 1.0, None, ALU.add))
                ch.link(nc.vector.reciprocal(e[:, kv, :], e[:, kv, :]))
                nc.vector.tensor_tensor(z[:, kv, :], z[:, kv, :], e[:, kv, :], ALU.mult).then_inc(act_ready, 1)
            dve.wait_ge(key_high, 1)
            ch.link(nc.vector.tensor_tensor(kcl[:, :, 0:NCMP], kp[:, 0:NC2].rearrange("p (g n) -> p g n", g=KV),
                                            kch[:, :, 0:NCMP].bitcast(F32), ALU.subtract))
            for g in range(KV):
                dve.wait_ge(first, 2 * g + 2)
                for half in range(2):
                    rows = slice(HD * half, HD * half + NCMP)
                    ch.link(nc.vector.tensor_tensor(rest[rows, g, :], vp[g][rows, 0:HD], vc3[rows, g, 0, :], ALU.subtract))
                    ch.link(nc.vector.tensor_copy(vc3[rows, g, 1, :], rest[rows, g, :]))
                    ch.link(nc.vector.tensor_tensor(vc3[rows, g, 2, :], rest[rows, g, :], vc3[rows, g, 1, :], ALU.subtract))

        @block.tensor
        def _(pe):
            pe.wait_ge(w_in, 16)
            pe.wait_ge(placed, 1)
            for kv in range(2):
                pe.wait_ge(cc_in[kv], 64)
                out = hid[kv][:, 0:(KV + 1) * NCMP].rearrange("p (g n) -> p g n", g=KV + 1)
                for lp in range(CPL):
                    mm = nc.tensor.matmul(out, w1s[:, kv, lp, :], cc[:, kv, :, 2 * lp:2 * lp + 16 * (NCMP - 1) + 1:16],
                                          start=(lp == 0), stop=(lp == CPL - 1))
                mm.then_inc(hidden, 1)
            pe.wait_ge(w2_in, 32)
            pe.wait_ge(act_ready, 1)
            nc.tensor.matmul(kp[:, 0:NC2], w2ks[:, :], z[:, 0, :], start=True, stop=True).then_inc(keyed, 1)
            pe.wait_ge(act_ready, 2)
            for g in range(KV):
                for half in range(2):
                    mm = nc.tensor.matmul(vp[g][HD * half:HD * half + NCMP, 0:HD], z[:, 1, NCMP * g:NCMP * (g + 1)],
                                          w2vs[:, :], start=True, stop=True)
                mm.then_inc(valued, 1)


def nsa_phase(nc, hT, v3, y, ident, kch, kcl, vc3, glog, bias_full, bias_win, bias_cmp, row_valid, force, blocks):
    HU = 2 * NT
    UN = RC * HU
    tiles = []
    for n in range(UN):
        qt = n % NT
        tiles.append(list(range(qt + 1)) if n % HU < NT else list(range(max(qt - 4, 0), qt + 1)))
    runs, before = softmax_chunks(tiles)
    R = before[-1]
    LOADS = RC + 2
    PAIRS = NT // 2
    ROUNDS = 2
    CH = 8 * RC - 1 + 7 + 2 + 3 * 2 * RC
    with ExitStack() as ctx:
        def sb(name, shape, dt):
            return ctx.enter_context(nc.sbuf_tensor(name, shape, dt))

        def sem(name):
            return ctx.enter_context(nc.semaphore(name))

        raw = hT[:, 0:2, :]
        bf = hT[:, 2:4, :]
        blk_in = hT[:, 4, :]
        qs = sb("s_queries", [P, RC, S], F32R)
        kh = sb("s_keys_high", [P, 2, S], F32R)
        kl = sb("s_keys_low", [P, 2, S], F32R)
        ck = sb("s_cmp_keys", [P, 2, HD], F32R)
        cv = sb("s_cmp_values", [P, 3 * HD], BF16)
        bw = sb("s_bias_window", [P, 2, CW], F32)
        bc = sb("s_bias_cmp", [P, 2, NT * HD], F32)
        pr = sb("s_probs", [P, 2, S], F32)
        pth = sb("s_probsT_high", [P, 4, 4, P], F16)
        ptl = sb("s_probsT_low", [P, 4, 4, P], F16)
        nmax = sb("s_negated_max", [P, 2, NT], F32)
        sums = sb("s_sums", [P, 2, 2, NT], F32)
        red = sb("s_out", [P, 2, NT, HD], F32)
        cmax = sb("s_cmp_max", [P, RC, NT], F32)
        csum = sb("s_cmp_sums", [P, RC, NT], F32)
        pbar = sb("s_cmp_probs_sum", [P, 2, SEL_T * HD], F32)
        imp = sb("s_importance", [P, SEL_T, NSLC], F32)
        tail = sb("s_importance_tail", [P, SEL_T, NSLC], F32)
        left = sb("s_not_chosen_scores", [P, SEL_T, NSLC], F32)
        top8 = sb("s_top8", [P, SEL_T, 8], F32)
        unsel = sb("s_not_chosen", [P, SEL_T, 32], F32)
        unselT = sb("s_not_chosenT", [P, P], BF16)
        valid0 = sb("s_row_valid", [P, NT], F32)
        forced = sb("s_forced", [P, SEL_T, NSLC], F32)
        blk = sb("s_blocks", [P, S], BF16)
        gate = sb("s_gates", [P, NT, 3 * C_H], F32)
        sc = [ctx.enter_context(nc.psum_tensor(f"s_scores{i}", [P, S], F32)) for i in range(2)]
        tp = [ctx.enter_context(nc.psum_tensor(f"s_turned{i}", [P, 4, P], F32)) for i in range(2)]
        ov = [ctx.enter_context(nc.psum_tensor(f"s_out{i}", [P, 512], F32)) for i in range(2)]

        const_in, gate_exp, gate_chain = sem("s_const_in"), sem("s_gate_exp"), sem("s_gate_chain")
        raw_in = [sem(f"s_raw_in{i}") for i in range(2)]
        bc_in = [sem(f"s_bias_cmp_in{i}") for i in range(2)]
        bf_in = [sem(f"s_bias_full_in{i}") for i in range(2)]
        bw_in = [sem(f"s_bias_window_in{i}") for i in range(2)]
        stack_high, stack_ready, cmp_copied = sem("s_stack_high"), sem("s_stack_ready"), sem("s_cmp_copied")
        c_scored, c_shifted, c_exped, c_normed = sem("c_scored"), sem("c_shifted"), sem("c_exped"), sem("c_normed")
        c_turned, c_high, c_low, c_valued, c_summed = sem("c_turned"), sem("c_high"), sem("c_low"), sem("c_valued"), sem("c_summed")
        chosen, chosen_turned, mask_ready = sem("s_chosen"), sem("s_chosen_turned"), sem("s_mask_ready")
        scored, biased, exped = sem("s_scored"), sem("s_biased"), sem("s_exped")
        turned, t_high, t_low = sem("s_turned"), sem("s_turned_high"), sem("s_turned_low")
        valued, summed, chain, headed = sem("s_valued"), sem("s_summed"), sem("s_chain"), sem("s_headed")
        block = ctx.enter_context(nc.Block())

        @block.sync
        def _(sp):
            sp.dma_start(valid0[:, :], row_valid).then_inc(const_in, 16)
            sp.dma_start(forced[:, :, :], force).then_inc(const_in, 16)
            sp.dma_start(blk_in, blocks).then_inc(const_in, 16)
            for c in range(KV):
                for j in range(LOADS):
                    after(sp, stack_ready, LOADS * c + max(j - 1, 0))
                    if j < RC:
                        src = hT[HD * (j % 2):HD * (j % 2 + 1), 2 * c + (10 + j // 2), :]
                    else:
                        src = hT[HD:P, c + 6, :] if j == RC else hT[0:HD, c + 8, :]
                    for band in range(2):
                        sp.dma_start(raw[HD * band:HD * (band + 1), j % 2, :], src).then_inc(raw_in[j % 2], 16)
                    if j < RC:
                        after(sp, c_shifted, RC * c + max(j - 1, 0))
                        sp.dma_start(bc[:, j % 2, :], bias_cmp[RC * c + j]).then_inc(bc_in[j % 2], 16)
                for r in range(RC):
                    after(sp, biased, UN * c + max(r - 1, 0) * HU)
                    sp.dma_start(bf[:, r % 2, :], bias_full[RC * c + r]).then_inc(bf_in[r % 2], 16)
                    sp.dma_start(bw[:, r % 2, :], bias_win[RC * c + r]).then_inc(bw_in[r % 2], 16)

        @block.scalar
        def _(act):
            nc.scalar.activation(gate[:, :, :], glog[:, :, :], ACT.Exp, scale=-1.0).then_inc(gate_exp, 1)

            def stack(c, j):
                act.wait_ge(raw_in[j % 2], 96 * c + 32 * (j // 2 + 1))
                if j < RC:
                    nc.scalar.activation(qs[:, j, :], raw[:, j % 2, :], ACT.Copy, scale=HD ** -0.5).then_inc(stack_high, 1)
                else:
                    nc.scalar.copy(kh[:, j - RC, :], raw[:, j % 2, :]).then_inc(stack_high, 1)

            def exponentials(c, n):
                w = len(tiles[n]) * P
                r, br, qt = n // HU, n % HU // NT, n % NT
                act.wait_ge(biased, UN * c + (n + 1))
                nc.scalar.activation(pr[:, n % 2, 0:w], pr[:, n % 2, 0:w], ACT.Exp, scale=-1.0,
                                     bias=nmax[:, br, qt:qt + 1],
                                     accum_out=sums[:, r % 2, br, qt:qt + 1]).then_inc(exped, 1)

            def high_part(c, n):
                for i, run in enumerate(runs[n]):
                    g = before[n] + i
                    act.wait_ge(turned, R * c + (g + 1))
                    after(act, valued, R * c + max(g - 3, 0))
                    k = len(run)
                    nc.scalar.activation(pth[:, g % 4, 0:k, :], tp[g % 2][:, 0:k, :], ACT.Copy,
                                         scale=PSCALE).then_inc(t_high, 1)

            for c in range(KV):
                after(act, scored, UN * c)
                after(act, c_valued, RC * ROUNDS * c)
                nc.scalar.copy(ck[:, 0, :], kch[:, bass.ds(c, 1), :].rearrange("p a n -> p (a n)").bitcast(F32)).then_inc(cmp_copied, 1)
                nc.scalar.copy(ck[:, 1, :], kcl[:, bass.ds(c, 1), :].rearrange("p a n -> p (a n)").bitcast(F32)).then_inc(cmp_copied, 1)
                nc.scalar.copy(cv[:, :], vc3[:, bass.ds(c, 1), :, :].rearrange("p a t d -> p (a t d)")).then_inc(cmp_copied, 1)
                stack(c, 0)
                for r in range(RC):
                    stack(c, r + 1)
                    act.wait_ge(c_shifted, RC * c + (r + 1))
                    nc.scalar.activation(pr[:, r % 2, 0:NT * HD], pr[:, r % 2, 0:NT * HD], ACT.Exp).then_inc(c_exped, 1)
                    act.wait_ge(c_turned, RC * c + (r + 1))
                    after(act, valued, R * c)
                    if r >= 2:
                        after(act, c_valued, RC * ROUNDS * c + ROUNDS * (r - 1))
                    nc.scalar.activation(pth[:, r % 2, :, :], tp[r % 2][:, :, :], ACT.Copy, scale=PSCALE).then_inc(c_high, 1)
                stack(c, RC + 1)
                if c == 0:
                    act.wait_ge(const_in, 48)
                    nc.scalar.copy(blk[:, :], blk_in).then_inc(mask_ready, 1)
                act.wait_ge(chosen_turned, c + 1)
                nc.scalar.copy(unselT[:, :], tp[0][:, 0, :]).then_inc(mask_ready, 1)
                exponentials(c, 0)
                act.wait_ge(c_valued, RC * ROUNDS * (c + 1))
                for n in range(UN):
                    if n + 1 < UN:
                        exponentials(c, n + 1)
                    high_part(c, n)

        @block.vector
        def _(dve):
            gc = Chain(dve, gate_chain)
            dve.wait_ge(gate_exp, 1)
            gc.link(nc.vector.tensor_scalar(gate[:, :, :], gate[:, :, :], 1.0, PSCALE, ALU.add, ALU.mult))
            gc.link(nc.vector.reciprocal(gate[:, :, :], gate[:, :, :]))
            gc.link(nc.vector.memset(unsel[:, :, :], 0.0))
            dve.wait_ge(const_in, 48)

            def gate_of(c, r, br):
                return gate[:, :, bass.ds(3 * RC * c + (3 * r + br), 1)]

            def y_of(c, r):
                return y[:, :, bass.ds(RC * HD * c + ((A_H + B_H) * HD + HD * r), HD)]

            def stack(c, j):
                dve.wait_ge(stack_high, LOADS * c + (j + 1))
                if j < RC:
                    low = qs[HD:P, j, :]
                    ins = nc.vector.scalar_tensor_tensor(out=low, in0=raw[HD:P, j % 2, :], scalar=HD ** -0.5,
                                                         in1=low.bitcast(F32), op0=ALU.mult, op1=ALU.subtract)
                else:
                    ins = nc.vector.tensor_tensor(kl[:, j - RC, :], raw[:, j % 2, :], kh[:, j - RC, :].bitcast(F32),
                                                  ALU.subtract)
                ins.then_inc(stack_ready, 1)

            def by_tile(r):
                return pr[:, r % 2, 0:NT * HD].rearrange("p (t n) -> p t n", t=NT)

            def over_blocks(v):
                return v.unsqueeze(2).broadcast_to([P, NT, HD])

            def shift(c, r, ch):
                dve.wait_ge(bc_in[r % 2], 32 * c + 16 * (r // 2 + 1))
                dve.wait_ge(c_scored, RC * c + (r + 1))
                after(dve, turned, R * c)
                if r >= 2:
                    dve.wait_ge(c_turned, RC * c + (r - 1))
                x = by_tile(r)
                ch.link(nc.vector.tensor_tensor(pr[:, r % 2, 0:NT * HD], sc[r % 2][:, 0:NT * HD], bc[:, r % 2, :], ALU.add))
                ch.link(nc.vector.tensor_reduce(cmax[:, r, :], x, AX.X, ALU.max))
                nc.vector.tensor_tensor(x, x, over_blocks(cmax[:, r, :]), ALU.subtract).then_inc(c_shifted, 1)

            def norm(c, r, ch):
                x = by_tile(r)
                dve.wait_ge(c_exped, RC * c + (r + 1))
                ch.link(nc.vector.tensor_reduce(csum[:, r, :], x, AX.X, ALU.add))
                ch.link(nc.vector.reciprocal(csum[:, r, :], csum[:, r, :]))
                ch.link(nc.vector.tensor_tensor(csum[:, r, :], csum[:, r, :], valid0[:, :], ALU.mult))
                nc.vector.tensor_tensor(x, x, over_blocks(csum[:, r, :]), ALU.mult).then_inc(c_normed, 1)
                dve.wait_ge(c_normed, RC * c + (r + 1))
                late = pr[:, r % 2, SEL_T * HD:NT * HD]
                flushed = pbar[:, 0, :] if r == 0 else pbar[:, 1, :]
                ch.link(nc.vector.scalar_tensor_tensor(out=flushed, in0=late, scalar=TINY, in1=late, op0=ALU.is_ge,
                                                       op1=ALU.mult))
                if r > 0:
                    ch.link(nc.vector.tensor_tensor(pbar[:, 0, :], pbar[:, 0, :], pbar[:, 1, :], ALU.add))

            def weigh(c, r, ch):
                dve.wait_ge(c_high, RC * c + (r + 1))
                nc.vector.scalar_tensor_tensor(out=ptl[:, r % 2, :, :], in0=tp[r % 2][:, :, :], scalar=PSCALE,
                                               in1=pth[:, r % 2, :, :], op0=ALU.mult, op1=ALU.subtract).then_inc(c_low, 1)
                for k in range(ROUNDS):
                    dve.wait_ge(c_valued, RC * ROUNDS * c + (ROUNDS * r + k + 1))
                    for half in range(2):
                        ins = nc.vector.tensor_reduce(red[:, 0, 4 * k + half:4 * k + half + 3:2, :],
                                                      ov[half][:, 0:2 * 3 * HD].rearrange("p (q t d) -> p q d t", q=2, t=3),
                                                      AX.X, ALU.add)
                    ins.then_inc(c_summed, 1)
                dve.wait_ge(c_summed, RC * ROUNDS * c + ROUNDS * (r + 1))
                ch.link(nc.vector.tensor_tensor(y_of(c, r), red[:, 0, :, :], gate_of(c, r, 0).broadcast_to([P, NT, HD]),
                                                ALU.mult))

            def choose(c, ch):
                p4 = pbar[:, 0, :].rearrange("p (t j k) -> p t j k", t=SEL_T, k=4)
                ch.link(nc.vector.tensor_tensor(imp[:, :, :], p4[:, :, :, 0], p4[:, :, :, 1], ALU.add))
                ch.link(nc.vector.tensor_tensor(imp[:, :, :], imp[:, :, :], p4[:, :, :, 2], ALU.add))
                ch.link(nc.vector.tensor_scalar(tail[:, :, :], p4[:, :, :, 3], 0.5, None, ALU.mult))
                ch.link(nc.vector.scalar_tensor_tensor(out=tail[:, :, :], in0=tail[:, :, :], scalar=TINY, in1=tail[:, :, :],
                                                       op0=ALU.is_ge, op1=ALU.mult))
                ch.link(nc.vector.tensor_tensor(imp[:, :, :], imp[:, :, :], tail[:, :, :], ALU.add))
                ch.link(nc.vector.tensor_tensor(imp[:, :, 1:NSLC], imp[:, :, 1:NSLC], tail[:, :, 0:NSLC - 1], ALU.add))
                ch.link(nc.vector.tensor_tensor(imp[:, :, :], imp[:, :, :], forced[:, :, :], ALU.add))
                for t in range(SEL_T):
                    ins = nc.vector.max(top8[:, t, :], imp[:, t, :])
                ch.link(ins)
                for t in range(SEL_T):
                    ins = nc.vector.match_replace(left[:, t, :], top8[:, t, :], imp[:, t, :], -BIG)
                ch.link(ins)
                nc.vector.tensor_tensor(unsel[:, :, 0:NSLC], left[:, :, :], imp[:, :, :], ALU.is_equal).then_inc(chosen, 1)

            def add_bias(c, n):
                w = len(tiles[n]) * P
                at = score_layout(len(tiles[n]))[0]
                r, br, qt = n // HU, n % HU // NT, n % NT
                if qt == 0:
                    dve.wait_ge((bf_in, bw_in)[br][r % 2], 32 * c + 16 * (r // 2 + 1))
                after(dve, turned, R * c + before[max(n - 1, 0)])
                dve.wait_ge(scored, UN * c + (n + 1))
                b = bf[:, r % 2, S - w:S] if br == 0 else bw[:, r % 2, CW - w:CW]
                nc.vector.tensor_tensor_reduce(out=pr[:, n % 2, 0:w], in0=sc[n % 2][:, at:at + w], in1=b,
                                               scale=-1.0, scalar=BIG, op0=ALU.add, op1=ALU.min,
                                               accum_out=nmax[:, br, qt:qt + 1]).then_inc(biased, 1)

            def low_part(c, n):
                for i, run in enumerate(runs[n]):
                    g = before[n] + i
                    dve.wait_ge(t_high, R * c + (g + 1))
                    k = len(run)
                    nc.vector.scalar_tensor_tensor(out=ptl[:, g % 4, 0:k, :], in0=tp[g % 2][:, 0:k, :], scalar=PSCALE,
                                                   in1=pth[:, g % 4, 0:k, :], op0=ALU.mult,
                                                   op1=ALU.subtract).then_inc(t_low, 1)

            def write_out(c, n, ch):
                r, br, qt = n // HU, n % HU // NT, n % NT
                dve.wait_ge(valued, R * c + before[n + 1])
                nc.vector.tensor_reduce(red[:, br, qt, :], ov[n % 2][:, 0:3 * HD].rearrange("p (t d) -> p d t", t=3),
                                        AX.X, ALU.add).then_inc(summed, 1)
                if qt < NT - 1:
                    return
                s = sums[:, r % 2, br, :]
                ch.link(nc.vector.reciprocal(s, s))
                ch.link(nc.vector.tensor_tensor(s.unsqueeze(2), s.unsqueeze(2), gate_of(c, r, br + 1), ALU.mult))
                dve.wait_ge(summed, UN * c + (n + 1))
                ch.link(nc.vector.tensor_tensor(red[:, br, :, :], red[:, br, :, :], over_blocks(s), ALU.mult))
                nc.vector.tensor_tensor(y_of(c, r), y_of(c, r), red[:, br, :, :], ALU.add).then_inc(headed, 1)
                dve.wait_ge(headed, 2 * RC * c + (2 * r + br + 1))

            for c in range(KV):
                ch = Chain(dve, chain, CH * c)
                stack(c, 0)
                shift(c, 0, ch)
                for r in range(RC):
                    stack(c, r + 1)
                    if r + 1 < RC:
                        shift(c, r + 1, ch)
                    norm(c, r, ch)
                    weigh(c, r, ch)
                stack(c, RC + 1)
                choose(c, ch)
                dve.wait_ge(c_turned, RC * (c + 1))
                add_bias(c, 0)
                for n in range(UN):
                    if n + 1 < UN:
                        add_bias(c, n + 1)
                    low_part(c, n)
                    if n >= 1:
                        write_out(c, n - 1, ch)
                write_out(c, UN - 1, ch)
                assert ch.n == CH, ch.n

        @block.tensor
        def _(pe):
            def cmp_scores(c, r):
                pe.wait_ge(stack_ready, LOADS * c + (r + 1))
                if r >= 2:
                    pe.wait_ge(c_shifted, RC * c + (r - 1))
                for qt in range(NT):
                    out = sc[r % 2][:, HD * qt:HD * (qt + 1)]
                    q = qs[:, r, qt * P:(qt + 1) * P]
                    nc.tensor.matmul(out, q, ck[:, 0, :], start=True, stop=False)
                    mm = nc.tensor.matmul(out, q, ck[:, 1, :], start=False, stop=True)
                mm.then_inc(c_scored, 1)

            def cmp_values(c, r):
                pe.wait_ge(c_normed, RC * c + (r + 1))
                if r >= 2:
                    pe.wait_ge(c_low, RC * c + (r - 1))
                for p in range(PAIRS):
                    mm = nc.tensor.transpose(tp[r % 2][:, p, :], pr[:, r % 2, P * p:P * (p + 1)], ident[:, :])
                mm.then_inc(c_turned, 1)
                pe.wait_ge(c_low, RC * c + (r + 1))
                for k in range(ROUNDS):
                    pe.wait_ge(c_summed, RC * ROUNDS * c + (ROUNDS * r + k))
                    for p, half in ((2 * k, 0), (2 * k, 1), (2 * k + 1, 0), (2 * k + 1, 1)):
                        rows = slice(HD * half, HD * (half + 1))
                        out = ov[half][:, 3 * HD * (p % 2):3 * HD * (p % 2 + 1)]
                        nc.tensor.matmul(out, pth[rows, r % 2, p, :], cv[rows, :], start=True, stop=False)
                        nc.tensor.matmul(out[:, 0:2 * HD], ptl[rows, r % 2, p, :], cv[rows, 0:2 * HD], start=False,
                                         stop=False)
                        mm = nc.tensor.matmul(out[:, 2 * HD:3 * HD], ptl[rows, r % 2, p, :], cv[rows, 2 * HD:3 * HD],
                                              start=False, stop=True)
                    mm.then_inc(c_valued, 1)

            def scores(c, n):
                r, br, qt = n // HU, n % HU // NT, n % NT
                if n == 0:
                    pe.wait_ge(stack_ready, LOADS * (c + 1))
                    pe.wait_ge(c_shifted, RC * (c + 1))
                elif n == 1:
                    pass
                else:
                    pe.wait_ge(biased, UN * c + (n - 1))
                q = qs[:, r, qt * P:(qt + 1) * P]
                first = tiles[n][0]
                masked = br == 0 and qt >= SEL_T
                for at, key, w in score_layout(max(len(tiles[n]), 2))[1]:
                    keys = slice(first * P + key, first * P + key + w)
                    out = sc[n % 2][:, at:at + w]
                    nc.tensor.matmul(out, q, kh[:, br, keys], start=True, stop=False)
                    mm = nc.tensor.matmul(out, q, kl[:, br, keys], start=False, stop=not masked)
                    if masked:
                        rows = slice(32 * (qt - SEL_T), 32 * (qt - SEL_T + 1))
                        mm = nc.tensor.matmul(out, unselT[rows, :], blk[rows, keys], start=False, stop=True)
                mm.then_inc(scored, 1)

            def turn(c, n):
                pe.wait_ge(exped, UN * c + (n + 1))
                for i, run in enumerate(runs[n]):
                    g = before[n] + i
                    after(pe, t_low, R * c + max(g - 1, 0))
                    transpose_run(pe, nc, tp[g % 2], pr[:, n % 2, :], run, tiles[n][0], ident).then_inc(turned, 1)

            def values(c, n):
                br = n % HU // NT
                after(pe, summed, UN * c + max(n - 1, 0))
                for i, run in enumerate(runs[n]):
                    g = before[n] + i
                    pe.wait_ge(t_low, R * c + (g + 1))
                    values_run(nc, ov[n % 2][:, 0:3 * HD], pth[:, g % 4], ptl[:, g % 4], run,
                               lambda kt: v3[:, kt, bass.ds(c + (A_H + KV + KV * br), 1), :, :].rearrange("p a t d -> p (a t d)"),
                               i == 0, i == len(runs[n]) - 1).then_inc(valued, 1)

            for c in range(KV):
                pe.wait_ge(cmp_copied, 3 * (c + 1))
                after(pe, biased, UN * c)
                after(pe, t_low, R * c)
                after(pe, summed, UN * c)
                cmp_scores(c, 0)
                for r in range(RC):
                    if r + 1 < RC:
                        cmp_scores(c, r + 1)
                    cmp_values(c, r)
                pe.wait_ge(chosen, c + 1)
                nc.tensor.transpose(tp[0][:, 0, :], unsel[:, :, :].rearrange("p t j -> p (t j)"), ident[:, :]).then_inc(chosen_turned, 1)
                pe.wait_ge(mask_ready, c + 2)
                pe.wait_ge(c_low, RC * (c + 1))
                pe.wait_ge(c_summed, RC * ROUNDS * (c + 1))
                scores(c, 0)
                for n in range(UN):
                    if n + 1 < UN:
                        scores(c, n + 1)
                    turn(c, n)
                    if n >= 1:
                        values(c, n - 1)
                values(c, UN - 1)


def out_phase(nc, x, w_out, gate_dram, subln, final_row, out, hT, y, ident, lam_size):
    AW = A_H * HD
    SLABS, W = 4, D // 4
    with ExitStack() as ctx:
        def sb(name, shape, dt):
            return ctx.enter_context(nc.sbuf_tensor(name, shape, dt))

        def sem(name):
            return ctx.enter_context(nc.semaphore(name))

        raw = hT[:, 0:4, :].rearrange("p (s a) n -> p s (a n)", s=2).rearrange("p s (k n) -> p s k n", k=KT)
        gates, xin, yg = hT[:, 4:6, :], hT[:, 6:8, :], hT[:, 8:10, :]
        res, fin, fn = hT[:, 10:12, :], hT[:, 12:14, :], hT[:, 14, :]
        wh = sb("o_w_high", [P, KT, D], F32R)
        wl = sb("o_w_low", [P, KT, D], F32R)
        yh = sb("o_yT_high", [P, 2, KT, P], F32R)
        yl = sb("o_yT_low", [P, 2, KT, P], F32R)
        sq = sb("o_squares", [P, AW], F32)
        sub = sb("o_subln", [P, HD], F32)
        small = sb("o_small", [P, 4], F32)
        arms = sb("o_a_rstd", [P, NT, A_H], F32)
        ss = sb("o_square_sums", [P, NT], F32)
        rs = sb("o_rstd", [P, NT], F32)
        tp = [ctx.enter_context(nc.psum_tensor(f"o_turned{i}", [P, 4, P], F32)) for i in range(2)]
        acc = [ctx.enter_context(nc.psum_tensor(f"o_acc{i}", [P, 512], F32)) for i in range(4)]

        row_in = sem("o_rows_in")
        w_in = [sem(f"o_w_in{i}") for i in range(2)]
        g_in = [sem(f"o_gates_in{i}") for i in range(2)]
        x_in = [sem(f"o_x_in{i}") for i in range(2)]
        w_high, w_low = sem("o_w_high_done"), sem("o_w_low_done")
        small_ready, a_summed, a_root, a_chain, gated = sem("o_small_ready"), sem("o_a_summed"), sem("o_a_root"), sem("o_a_chain"), sem("o_gated")
        turned, high, low = sem("o_turned"), sem("o_high"), sem("o_low")
        done, added, squares, roots, r_chain, normed = sem("o_done"), sem("o_added"), sem("o_squares_summed"), sem("o_roots"), sem("o_root_chain"), sem("o_normed")
        stored = [sem(f"o_stored{i}") for i in range(2)]
        block = ctx.enter_context(nc.Block())

        @block.sync
        def _(sp):
            sp.dma_start(fn, final_row.partition_broadcast(P)).then_inc(row_in, 16)
            sp.dma_start(sub[:, :], subln.partition_broadcast(P)).then_inc(row_in, 16)

            def load(i):
                if i >= 2:
                    sp.wait_ge(gated, i - 1)
                sp.dma_start(gates[:, i % 2, :], gate_dram[i * P:(i + 1) * P, :]).then_inc(g_in[i % 2], 16)
                if i >= 2:
                    sp.wait_ge(added, 2 * i - 2)
                sp.dma_start(xin[:, i % 2, :], x[i * P:(i + 1) * P, :]).then_inc(x_in[i % 2], 16)

            load(0)
            for s in range(SLABS):
                if s >= 2:
                    sp.wait_ge(w_low, s - 1)
                sp.dma_start(raw[:, s % 2], w_out[s]).then_inc(w_in[s % 2], 16)
            load(1)
            for i in range(NT):
                sp.wait_ge(normed, i + 1)
                sp.dma_start(out[i * P:(i + 1) * P, :], fin[:, i % 2, :]).then_inc(stored[i % 2], 16)
                if i + 2 < NT:
                    load(i + 2)
            for i in range(2):
                sp.wait_ge(stored[i], 16 * (NT // 2))

        @block.scalar
        def _(act):
            act.wait_ge(small_ready, 1)

            def a_rstd(i):
                act.wait_ge(a_summed, i + 1)
                nc.scalar.activation(arms[:, i, :], arms[:, i, :], ACT.Sqrt, scale=small[:, 1:2],
                                     bias=small[:, 2:3]).then_inc(a_root, 1)

            def high_part(i):
                for h in range(2):
                    act.wait_ge(turned, 2 * i + h + 1)
                    if i >= 2 and h == 0:
                        act.wait_ge(done, 2 * i - 2)
                    nc.scalar.copy(yh[:, i % 2, 4 * h:4 * h + 4, :], tp[h][:, :, :]).then_inc(high, 1)

            def square(i):
                act.wait_ge(added, 2 * i + 2)
                if i >= 2:
                    act.wait_ge(stored[i % 2], 16 * (i // 2))
                nc.scalar.activation(fin[:, i % 2, :], res[:, i % 2, :], ACT.Square, accum_out=ss[:, i:i + 1]).then_inc(squares, 1)
                act.wait_ge(squares, i + 1)
                nc.scalar.activation(rs[:, i:i + 1], ss[:, i:i + 1], ACT.Sqrt, scale=1.0 / D, bias=small[:, 2:3]).then_inc(roots, 1)

            a_rstd(0)
            for s in range(SLABS):
                act.wait_ge(w_in[s % 2], 16 * (s // 2 + 1))
                nc.scalar.copy(wh[:, :, s * W:(s + 1) * W], raw[:, s % 2]).then_inc(w_high, 1)
            high_part(0)
            for i in range(NT):
                if i + 1 < NT:
                    a_rstd(i + 1)
                    high_part(i + 1)
                square(i)

        @block.vector
        def _(dve):
            sc = Chain(dve, a_chain)
            sc.link(nc.vector.tensor_scalar(small[:, 0:1], lam_size[:, :], 1.0 / PSCALE, None, ALU.mult))
            sc.link(nc.vector.tensor_tensor(small[:, 1:2], small[:, 0:1], small[:, 0:1], ALU.mult))
            sc.link(nc.vector.tensor_scalar(small[:, 1:2], small[:, 1:2], 1.0 / HD, None, ALU.mult))
            sc.link(nc.vector.tensor_scalar(small[:, 3:4], small[:, 0:1], 1.0 - LAM_INIT, None, ALU.mult))
            nc.vector.memset(small[:, 2:3], EPS).then_inc(small_ready, 1)
            dve.wait_ge(row_in, 32)
            by_head = lambda t: t.rearrange("p (h d) -> p h d", d=HD)

            def a_squares(i):
                ya = y[:, i, 0:AW]
                sc.link(nc.vector.tensor_tensor(sq[:, :], ya, ya, ALU.mult))
                nc.vector.tensor_reduce(arms[:, i, :], by_head(sq[:, :]), AX.X, ALU.add).then_inc(a_summed, 1)

            def gate(i):
                ya = by_head(y[:, i, 0:AW])
                dve.wait_ge(a_root, i + 1)
                sc.link(nc.vector.reciprocal(arms[:, i, :], arms[:, i, :]))
                sc.link(nc.vector.tensor_scalar(arms[:, i, :], arms[:, i, :], small[:, 3:4], None, ALU.mult))
                sc.link(nc.vector.tensor_tensor(ya, ya, arms[:, i, :].unsqueeze(2).broadcast_to([P, A_H, HD]), ALU.mult))
                sc.link(nc.vector.tensor_tensor(ya, ya, sub[:, :].unsqueeze(1).broadcast_to([P, A_H, HD]), ALU.mult))
                dve.wait_ge(g_in[i % 2], 16 * (i // 2 + 1))
                if i >= 2:
                    dve.wait_ge(turned, 2 * i - 2)
                nc.vector.tensor_tensor(yg[:, i % 2, :], y[:, i, :], gates[:, i % 2, :], ALU.mult).then_inc(gated, 1)

            def low_part(i):
                for h in range(2):
                    dve.wait_ge(high, 2 * i + h + 1)
                    ks = slice(4 * h, 4 * h + 4)
                    nc.vector.tensor_tensor(yl[:, i % 2, ks, :], tp[h][:, :, :], yh[:, i % 2, ks, :].bitcast(F32),
                                            ALU.subtract).then_inc(low, 1)

            def residual(i):
                for h in range(2):
                    n = 2 * i + h
                    dve.wait_ge(done, n + 1)
                    if h == 0:
                        dve.wait_ge(x_in[i % 2], 16 * (i // 2 + 1))
                    cols = slice(512 * h, 512 * h + 512)
                    nc.vector.tensor_tensor(res[:, i % 2, cols], acc[n % 4][:, :], xin[:, i % 2, cols], ALU.add).then_inc(added, 1)

            def normalise(i):
                dve.wait_ge(roots, i + 1)
                nc.vector.reciprocal(rs[:, i:i + 1], rs[:, i:i + 1]).then_inc(r_chain, 1)
                dve.wait_ge(r_chain, i + 1)
                nc.vector.scalar_tensor_tensor(out=fin[:, i % 2, :], in0=res[:, i % 2, :], scalar=rs[:, i:i + 1], in1=fn,
                                               op0=ALU.mult, op1=ALU.mult).then_inc(normed, 1)

            a_squares(0)
            for s in range(SLABS):
                dve.wait_ge(w_high, s + 1)
                cols = slice(s * W, (s + 1) * W)
                nc.vector.tensor_tensor(wl[:, :, cols], raw[:, s % 2], wh[:, :, cols].bitcast(F32), ALU.subtract).then_inc(w_low, 1)
            gate(0)
            low_part(0)
            for i in range(NT):
                if i + 1 < NT:
                    a_squares(i + 1)
                    gate(i + 1)
                    low_part(i + 1)
                residual(i)
                normalise(i)

        @block.tensor
        def _(pe):
            def turn(i):
                pe.wait_ge(gated, i + 1)
                for h in range(2):
                    if i >= 1:
                        pe.wait_ge(low, 2 * i + h - 1)
                    for k in range(4):
                        mm = nc.tensor.transpose(tp[h][:, k, :], yg[:, i % 2, (4 * h + k) * P:(4 * h + k + 1) * P], ident[:, :])
                    mm.then_inc(turned, 1)

            def project(i):
                pe.wait_ge(low, 2 * i + 2)
                for h in range(2):
                    n = 2 * i + h
                    if n >= 4:
                        pe.wait_ge(added, n - 3)
                    cols = slice(512 * h, 512 * h + 512)
                    for k in range(KT):
                        nc.tensor.matmul(acc[n % 4][:, :], yh[:, i % 2, k, :], wh[:, k, cols], start=(k == 0), stop=False)
                        nc.tensor.matmul(acc[n % 4][:, :], yh[:, i % 2, k, :], wl[:, k, cols], start=False, stop=False)
                        mm = nc.tensor.matmul(acc[n % 4][:, :], yl[:, i % 2, k, :], wh[:, k, cols], start=False,
                                              stop=(k == KT - 1))
                    mm.then_inc(done, 1)

            turn(0)
            pe.wait_ge(w_low, SLABS)
            for i in range(NT):
                if i + 1 < NT:
                    turn(i + 1)
                project(i)


def decoder_trunk(nc, x, norm_row, w_feat, w_val, w_gate, w_out, lams, subln, sinks, pe_pairs, cmp_w1, cmp_w2k,
                  cmp_w2v, final_row, identity, bias_full, bias_win, bias_swa, bias_cmp, row_valid, force, blocks, out):
    gate_dram = nc.dram_tensor("silu_gates", (S, D), F32, kind="Internal").ap()
    with ExitStack() as ctx:
        def sb(name, shape, dt):
            return ctx.enter_context(nc.sbuf_tensor(name, shape, dt))

        ident = sb("identity", [P, P], F32)
        glog = sb("gate_logits", [P, NT, 3 * C_H], F32)
        kch = sb("cmp_keys_high", [P, KV, HD], F32R)
        kcl = sb("cmp_keys_low", [P, KV, HD], F32R)
        vc3 = sb("cmp_values", [P, KV, 3, HD], BF16)
        lam_size = sb("lam_size", [P, 1], F32)
        hT = sb("features", [P, TC, S], F32)
        with ExitStack() as attention:
            v3 = attention.enter_context(nc.sbuf_tensor("values", [P, NT, VH, 3, HD], BF16))
            load_identity(nc, ident, identity)
            with ExitStack() as projection:
                def proj(name, shape, dt):
                    return projection.enter_context(nc.sbuf_tensor(name, shape, dt))

                xh = proj("xT_high", [P, KT, S], F32R)
                xl = proj("xT_low", [P, KT, S], F32R)
                wr = proj("w_raw", [P, 4, KT * P], F32)
                wh = proj("w_high", [P, 4, KT * P], F32R)
                wl = proj("w_low", [P, 4, KT * P], F32R)
                norm_phase(nc, x, norm_row, ident, hT, xh, xl)
                values_phase(nc, w_val, w_gate, gate_dram, hT, xh, xl, wr, wh, wl, v3, glog)
                queries_phase(nc, w_feat, hT, xh, xl, wr, wh, wl)
            y = attention.enter_context(nc.sbuf_tensor("branches", [P, NT, D], F32))
            diff_phase(nc, hT, v3, y, ident, bias_full, lams, lam_size)
            swa_phase(nc, hT, v3, y, ident, bias_swa, sinks)
            compress_phase(nc, hT, cmp_w1, cmp_w2k, cmp_w2v, pe_pairs, kch, kcl, vc3)
            nsa_phase(nc, hT, v3, y, ident, kch, kcl, vc3, glog, bias_full, bias_win, bias_cmp, row_valid, force, blocks)
            out_phase(nc, x, w_out, gate_dram, subln, final_row, out, hT, y, ident, lam_size)


def load_identity(nc, ident, identity):
    with nc.semaphore("identity_in") as loaded, nc.Block() as block:
        @block.sync
        def _(sp):
            sp.dma_start(ident[:, :], identity).then_inc(loaded, 16)
            sp.wait_ge(loaded, 16)


def _columns():
    r = np.arange
    qa, ka, va, ga, qb, kb, vb, gb = 0, 256, 512, 768, 1024, 1280, 1408, 1536
    qc, kc, vc, ks, vs, kw, vw, gl, gc = 1792, 2304, 2432, 2560, 2688, 2816, 2944, 3072, 3096
    feat = [r(qa, qa + 128), r(qa + 128, qa + 256), r(ka, ka + 128), r(ka + 128, ka + 256)]
    feat += [r(qb + 128 * g, qb + 128 * g + 128) for g in range(KV)]
    feat += [np.r_[kb + 64 * g:kb + 64 * g + 64, ks + 64 * g:ks + 64 * g + 64] for g in range(KV)]
    feat += [np.r_[kw + 64 * g:kw + 64 * g + 64, kc + 64 * g:kc + 64 * g + 64] for g in range(KV)]
    feat += [r(qc + 128 * c, qc + 128 * c + 128) for c in range(4)] + [r(vc, vc + 128)]
    val = [r(va, va + 256), np.r_[vb:vb + 128, vs:vs + 128], np.r_[vw:vw + 128, gl:gl + 24, gl:gl + 24, gl:gl + 24, gl:gl + 24, gl:gl + 24, gl:gl + 8]]
    gate = [r(ga, ga + 256), r(gb, gb + 256), r(gc, gc + 256), r(gc + 256, gc + 512)]
    return feat, val, gate


def _constants():
    f32 = np.float32
    q = np.arange(P)[:, None]
    t = np.arange(S).reshape(NT, P).T[:, :, None]

    def bias(slope, dist, valid):
        return np.where(valid, -slope * dist, NEG).astype(f32)

    slopes8 = 2.0 ** -np.arange(1, C_H + 1)
    slopes4 = 2.0 ** (-2.0 * np.arange(1, B_H + 1))
    d = q + (S - P) - np.arange(S)[None]
    full = np.stack([bias(s, d, d >= 0) for s in slopes8])
    d = q + (CW - P) - np.arange(CW)[None]
    win = np.stack([bias(s, d, (d >= 0) & (d < 512)) for s in slopes8])
    d = q + (BW - P) - np.arange(BW)[None]
    swa = np.stack([bias(s, d, (d >= 0) & (d < 128)) for s in slopes4]).reshape(KV, 2, P, BW).transpose(0, 2, 1, 3)
    block = np.arange(HD)[None, None]
    d = t - (16 * block + 31)
    cmp = np.stack([bias(s, d, (d >= 0) & (block < NCMP)) for s in slopes8]).reshape(C_H, P, NT * HD)
    row_valid = (t[:, :, 0] >= 31).astype(f32)
    cur = t[:, SEL_T:] // 64
    j = np.arange(NSLC)[None, None]
    force = np.where(j > cur, NEG, np.where((j == 0) | (j == cur) | (j == cur - 1), -NEG, 0)).astype(f32)
    blocks = np.zeros((SEL_T, 32, S), f32)
    for b in range(NSLC):
        blocks[:, b, 64 * b:64 * b + 64] = NEG
    blocks = blocks.reshape(P, S)
    return {"identity": np.eye(P, dtype=f32), "bias_full": full, "bias_win": win, "bias_swa": swa, "bias_cmp": cmp,
            "row_valid": row_valid, "force": force, "blocks": blocks}


def _slab(w, columns):
    w = w if columns is None else w[:, columns]
    return w.reshape(KT, P, w.shape[1]).transpose(1, 0, 2)


def kernel(x, norm_w, w_in, w_out, diff_lq1, diff_lk1, diff_lq2, diff_lk2, diff_subln, sinks, cmp_pe_k, cmp_pe_v,
           cmp_wk1, cmp_wk2, cmp_wv1, cmp_wv2, final_norm):
    import concourse.bacc as bacc
    from concourse.bass_utils import run_bass_kernel_spmd

    feat, val, gate = _columns()
    w = w_in[0]
    pairs = lambda a: a.reshape(CPL, P, -1).transpose(1, 0, 2)
    arrays = {
        "x": x[0], "norm_row": norm_w,
        "w_feat": np.stack([_slab(w, c) for c in feat]),
        "w_val": np.stack([_slab(w, c) for c in val]),
        "w_gate": np.stack([_slab(w, c) for c in gate]),
        "w_out": np.stack([_slab(w_out[0][:, 256 * s:256 * s + 256], None) for s in range(4)]),
        "lams": np.concatenate([diff_lq1, diff_lk1, diff_lq2, diff_lk2]),
        "subln": diff_subln, "sinks": sinks.reshape(KV, 1, B_H // KV),
        "pe_pairs": np.stack([cmp_pe_k[0].reshape(CPL, P).T, cmp_pe_v[0].reshape(CPL, P).T], axis=1),
        "cmp_w1": np.stack([pairs(cmp_wk1[0]), pairs(cmp_wv1[0])], axis=1),
        "cmp_w2k": np.concatenate([cmp_wk2[0], cmp_wk2[0]], axis=1), "cmp_w2v": cmp_wv2[0],
        "final_row": final_norm.reshape(1, D),
    }
    arrays.update(_constants())
    arrays = {k: np.ascontiguousarray(v) for k, v in arrays.items()}
    nc = bacc.Bacc("TRN2", target_bir_lowering=False, num_devices=1)
    args = {k: nc.dram_tensor(f"in_{k}", v.shape, mybir.dt.from_np(v.dtype), kind="ExternalInput").ap() for k, v in arrays.items()}
    out = nc.dram_tensor("out", (S, D), F32, kind="ExternalOutput").ap()
    decoder_trunk(nc, **args, out=out)
    r = run_bass_kernel_spmd(nc, [{f"in_{k}": v for k, v in arrays.items()}], core_ids=[0])
    return r.results[0]["out"].reshape(1, S, D)
```

```python
from contextlib import ExitStack

import numpy as np

import concourse.bass as bass
from concourse import mybir

F32 = mybir.dt.float32
F32R = mybir.dt.float32r
F16 = mybir.dt.float16
BF16 = mybir.dt.bfloat16
ALU = mybir.AluOpType
ACT = mybir.ActivationFunctionType
AX = mybir.AxisListType

P = 128
D = 1024
S = 1024
KT = D // P
NT = S // P
HD = 64
A_QK = 32
EPS = 1e-6
NEG = -1e30
BIG = 3e38
TINY = 2.0 ** -126
PSCALE = 2.0 ** 14
A_H, B_H, C_H, KV = 4, 4, 8, 2
RC = C_H // KV
TC = 15
VH = A_H + 3 * KV
LAM_INIT = 0.2
QT_ORDER = (7, 0, 6, 1, 5, 2, 4, 3)
CW = 640
BW = 256
NCMP = 63
SEL_T = 4
NSLC = 16
CPL = 16


def score_layout(n_tiles):
    w = n_tiles * P
    if w <= 512:
        return 0, [(0, 0, w)]
    at = P if w == 640 else 0
    return at, [(at, 0, 512 - at), (512, 512 - at, w - 512 + at)]


def chunks_of(tiles):
    return [tiles[i:i + 4] for i in range(0, len(tiles), 4)]


def norm_phase(nc, x, norm_row, ident, hT, xh, xl):
    xin = hT[:, 0:2, :]
    xs = hT[:, 2:4, :]
    nw = hT[:, 4, :]
    junk = hT[:, 5, :]
    with ExitStack() as ctx:
        ss = ctx.enter_context(nc.sbuf_tensor("x_square_sums", [P, NT], F32))
        rs = ctx.enter_context(nc.sbuf_tensor("x_rstd", [P, NT], F32))
        ms = ctx.enter_context(nc.sbuf_tensor("x_mean_squares", [P, NT], F32))
        nt = ctx.enter_context(nc.sbuf_tensor("x_newton", [P, NT], F32))
        epsc = ctx.enter_context(nc.sbuf_tensor("norm_eps", [P, 1], F32))
        tp = [ctx.enter_context(nc.psum_tensor(f"x_transposed{i}", [P, 4, P], F32)) for i in range(4)]
        x_in = [ctx.enter_context(nc.semaphore(f"x_in{i}")) for i in range(2)]
        nw_in = ctx.enter_context(nc.semaphore("nw_in"))
        eps_set = ctx.enter_context(nc.semaphore("eps_set"))
        squares = ctx.enter_context(nc.semaphore("squares_summed"))
        roots = ctx.enter_context(nc.semaphore("roots_taken"))
        inverted = ctx.enter_context(nc.semaphore("roots_inverted"))
        scaled = ctx.enter_context(nc.semaphore("x_scaled"))
        turned = ctx.enter_context(nc.semaphore("x_turned"))
        high = ctx.enter_context(nc.semaphore("x_high_written"))
        low = ctx.enter_context(nc.semaphore("x_low_written"))
        block = ctx.enter_context(nc.Block())

        @block.sync
        def _(sp):
            sp.dma_start(nw, norm_row.partition_broadcast(P)).then_inc(nw_in, 16)
            for i in range(NT):
                if i >= 2:
                    sp.wait_ge(scaled, i - 1)
                sp.dma_start(xin[:, i % 2, :], x[i * P:(i + 1) * P, :]).then_inc(x_in[i % 2], 16)

        @block.scalar
        def _(act):
            act.wait_ge(eps_set, 1)

            def high_part(i):
                for h in range(2):
                    act.wait_ge(turned, 2 * i + h + 1)
                    nc.scalar.copy(xh[:, 4 * h:4 * h + 4, i * P:(i + 1) * P], tp[(2 * i + h) % 4][:, :, :]).then_inc(high, 1)

            for i in range(NT):
                act.wait_ge(x_in[i % 2], 16 * (i // 2 + 1))
                nc.scalar.activation(junk, xin[:, i % 2, :], ACT.Square, accum_out=ss[:, i:i + 1]).then_inc(squares, 1)
                act.wait_ge(squares, i + 1)
                nc.scalar.activation(rs[:, i:i + 1], ss[:, i:i + 1], ACT.Sqrt, scale=1.0 / D,
                                     bias=epsc[:, 0:1]).then_inc(roots, 1)
                if i >= 1:
                    high_part(i - 1)
            high_part(NT - 1)

        @block.vector
        def _(dve):
            nc.vector.memset(epsc[:, :], EPS).then_inc(eps_set, 1)
            dve.wait_ge(nw_in, 16)

            def low_part(i):
                for h in range(2):
                    dve.wait_ge(high, 2 * i + h + 1)
                    nc.vector.tensor_tensor(xl[:, 4 * h:4 * h + 4, i * P:(i + 1) * P], tp[(2 * i + h) % 4][:, :, :],
                                            xh[:, 4 * h:4 * h + 4, i * P:(i + 1) * P].bitcast(F32),
                                            ALU.subtract).then_inc(low, 1)

            steps = Chain(dve, inverted)
            for i in range(NT):
                dve.wait_ge(roots, i + 1)
                r, v, t = rs[:, i:i + 1], ms[:, i:i + 1], nt[:, i:i + 1]
                steps.link(nc.vector.tensor_scalar(v, ss[:, i:i + 1], 1.0 / D, EPS, ALU.mult, ALU.add))
                steps.link(nc.vector.reciprocal(r, r))
                steps.link(nc.vector.tensor_tensor(t, r, r, ALU.mult))
                steps.link(nc.vector.tensor_tensor(t, t, v, ALU.mult))
                steps.link(nc.vector.tensor_scalar(t, t, -0.5, 1.5, ALU.mult, ALU.add))
                steps.link(nc.vector.tensor_tensor(r, r, t, ALU.mult))
                if i >= 2:
                    dve.wait_ge(turned, 2 * i - 2)
                nc.vector.scalar_tensor_tensor(out=xs[:, i % 2, :], in0=xin[:, i % 2, :], scalar=rs[:, i:i + 1],
                                               in1=nw, op0=ALU.mult, op1=ALU.mult).then_inc(scaled, 1)
                if i >= 1:
                    low_part(i - 1)
            low_part(NT - 1)

        @block.tensor
        def _(pe):
            for i in range(NT):
                pe.wait_ge(scaled, i + 1)
                for h in range(2):
                    if 2 * i + h >= 4:
                        pe.wait_ge(low, 2 * i + h - 3)
                    for k in range(4):
                        mm = nc.tensor.transpose(tp[(2 * i + h) % 4][:, k, :],
                                                 xs[:, i % 2, (4 * h + k) * P:(4 * h + k + 1) * P], ident[:, :])
                    mm.then_inc(turned, 1)


def values_phase(nc, w_val, w_gate, gate_dram, hT, xh, xl, wr, wh, wl, v3, glog):
    rest = hT[:, 0, 0:512].rearrange("p (s n) -> p s n", s=2)
    e = hT[:, 1, 0:512].rearrange("p (s n) -> p s n", s=2)
    sg = hT[:, 2, :].rearrange("p (s n) -> p s n", s=4)
    NS, W = 3 + 4, 256
    with ExitStack() as ctx:
        acc = [ctx.enter_context(nc.psum_tensor(f"nat{i}", [P, 512], F32)) for i in range(4)]
        w_in = [ctx.enter_context(nc.semaphore(f"slab_in{i}")) for i in range(2)]
        high = ctx.enter_context(nc.semaphore("slab_high"))
        low = ctx.enter_context(nc.semaphore("slab_low"))
        done = ctx.enter_context(nc.semaphore("nat_done"))
        glog_copied = ctx.enter_context(nc.semaphore("gate_logits_copied"))
        v_first = ctx.enter_context(nc.semaphore("v_first_part"))
        v_rest = ctx.enter_context(nc.semaphore("v_rest"))
        v_second = ctx.enter_context(nc.semaphore("v_second_part"))
        v_third = ctx.enter_context(nc.semaphore("v_third_part"))
        g_exp = ctx.enter_context(nc.semaphore("gate_exp"))
        g_chain = ctx.enter_context(nc.semaphore("gate_chain"))
        g_ready = ctx.enter_context(nc.semaphore("gate_ready"))
        g_out = [ctx.enter_context(nc.semaphore(f"gate_out{i}")) for i in range(4)]
        block = ctx.enter_context(nc.Block())

        def slab(t, s):
            return t[:, 2 * (s % 2):2 * (s % 2) + 2, :].rearrange("p a n -> p (a n)").rearrange("p (k n) -> p k n", k=KT)

        def heads(s):
            return 4 if s < 2 else 2

        def first_head(s):
            return 4 * s

        def store(sp, s):
            if s < 3:
                return
            for i in range(NT):
                n = (s - 3) * NT + i
                sp.wait_ge(g_ready, n + 1)
                sp.dma_start(gate_dram[i * P:(i + 1) * P, (s - 3) * W:(s - 2) * W], sg[:, n % 4, :]).then_inc(g_out[n % 4], 16)

        @block.sync
        def _(sp):
            for s in range(NS):
                if s >= 2:
                    sp.wait_ge(low, s - 1)
                src = w_val[s] if s < 3 else w_gate[s - 3]
                sp.dma_start(slab(wr, s), src).then_inc(w_in[s % 2], 16)
                if s >= 3:
                    store(sp, s - 1)
            store(sp, NS - 1)
            for i in range(4):
                sp.wait_ge(g_out[i], 16 * 8)

        @block.scalar
        def _(act):
            def split(s):
                act.wait_ge(w_in[s % 2], 16 * (s // 2 + 1))
                if s >= 2:
                    act.wait_ge(done, NT * (s - 1))
                nc.scalar.copy(slab(wh, s), slab(wr, s)).then_inc(high, 1)

            split(0)
            split(1)
            for s in range(NS):
                for i in range(NT):
                    n = s * NT + i
                    act.wait_ge(done, n + 1)
                    if s < 3:
                        nh = heads(s)
                        ins = nc.scalar.copy(v3[:, i, first_head(s):first_head(s) + nh, 0, :],
                                             acc[n % 4][:, 0:nh * HD].rearrange("p (h d) -> p h d", d=HD))
                        ins.then_inc(v_first, 1)
                    else:
                        if n - 3 * NT >= 2:
                            act.wait_ge(g_ready, n - 3 * NT - 1)
                        nc.scalar.activation(e[:, n % 2, :], acc[n % 4][:, 0:W], ACT.Exp, scale=-1.0).then_inc(g_exp, 1)
                if s + 2 < NS:
                    split(s + 2)

        @block.vector
        def _(dve):
            def split(s):
                dve.wait_ge(high, s + 1)
                nc.vector.tensor_tensor(slab(wl, s), slab(wr, s), slab(wh, s).bitcast(F32), ALU.subtract).then_inc(low, 1)

            split(0)
            split(1)
            chain = 0
            for s in range(NS):
                for i in range(NT):
                    n = s * NT + i
                    if s < 3:
                        nh = heads(s)
                        dve.wait_ge(v_first, n + 1)
                        if n >= 2:
                            dve.wait_ge(v_third, n - 1)
                        ins = nc.vector.tensor_tensor(rest[:, n % 2, 0:nh * HD].rearrange("p (h d) -> p h d", d=HD),
                                                      acc[n % 4][:, 0:nh * HD].rearrange("p (h d) -> p h d", d=HD),
                                                      v3[:, i, first_head(s):first_head(s) + nh, 0, :], ALU.subtract)
                        ins.then_inc(v_rest, 1)
                        if s == 2:
                            ins = nc.vector.tensor_copy(glog[:, i, :], acc[n % 4][:, P:P + 3 * C_H])
                            ins.then_inc(glog_copied, 1)
                    else:
                        dve.wait_ge(g_exp, n - 3 * NT + 1)
                        nc.vector.tensor_scalar(e[:, n % 2, :], e[:, n % 2, :], 1.0, None, ALU.add).then_inc(g_chain, 1)
                        chain += 1
                        dve.wait_ge(g_chain, chain)
                        nc.vector.reciprocal(e[:, n % 2, :], e[:, n % 2, :]).then_inc(g_chain, 1)
                        chain += 1
                        dve.wait_ge(g_chain, chain)
                        m = n - 3 * NT
                        if m >= 4:
                            dve.wait_ge(g_out[n % 4], 16 * (m // 4))
                        nc.vector.tensor_tensor(sg[:, n % 4, :], acc[n % 4][:, 0:W], e[:, n % 2, :],
                                                ALU.mult).then_inc(g_ready, 1)
                if s + 2 < NS:
                    split(s + 2)

        @block.gpsimd
        def _(pool):
            for s in range(3):
                nh = heads(s)
                for i in range(NT):
                    n = s * NT + i
                    r = rest[:, n % 2, 0:nh * HD].rearrange("p (h d) -> p h d", d=HD)
                    vh = v3[:, i, first_head(s):first_head(s) + nh, :, :]
                    pool.wait_ge(v_rest, n + 1)
                    nc.gpsimd.tensor_copy(vh[:, :, 1, :], r).then_inc(v_second, 1)
                    pool.wait_ge(v_second, n + 1)
                    nc.gpsimd.tensor_tensor(vh[:, :, 2, :], r, vh[:, :, 1, :], ALU.subtract).then_inc(v_third, 1)

        @block.tensor
        def _(pe):
            for s in range(NS):
                pe.wait_ge(low, s + 1)
                a, b = slab(wh, s), slab(wl, s)
                n_cols = W if s != 2 else 192
                for i in range(NT):
                    n = s * NT + i
                    if n >= 4:
                        m = n - 4
                        if m < 3 * NT:
                            pe.wait_ge(v_rest, m + 1)
                            if m >= 2 * NT:
                                pe.wait_ge(glog_copied, m - 2 * NT + 1)
                        else:
                            pe.wait_ge(g_ready, m - 3 * NT + 1)
                    for k in range(KT):
                        rows = slice(i * P, (i + 1) * P)
                        nc.tensor.matmul(acc[n % 4][:, 0:n_cols], xh[:, k, rows], a[:, k, 0:n_cols], start=(k == 0), stop=False)
                        nc.tensor.matmul(acc[n % 4][:, 0:n_cols], xh[:, k, rows], b[:, k, 0:n_cols], start=False, stop=False)
                        mm = nc.tensor.matmul(acc[n % 4][:, 0:n_cols], xl[:, k, rows], a[:, k, 0:n_cols],
                                              start=False, stop=(k == KT - 1))
                    mm.then_inc(done, 1)


def queries_phase(nc, w_feat, hT, xh, xl, wr, wh, wl):
    U = 3
    TURNS = TC // U
    with ExitStack() as ctx:
        acc = [ctx.enter_context(nc.psum_tensor(f"feat{i}", [P, 512], F32)) for i in range(2 * U)]
        w_in = [ctx.enter_context(nc.semaphore(f"chunk_in{i}")) for i in range(U)]
        high = ctx.enter_context(nc.semaphore("chunk_high"))
        low = ctx.enter_context(nc.semaphore("chunk_low"))
        done = ctx.enter_context(nc.semaphore("feat_done"))
        left = ctx.enter_context(nc.semaphore("feat_left_copied"))
        right = ctx.enter_context(nc.semaphore("feat_right_copied"))
        block = ctx.enter_context(nc.Block())

        def chunk(t, j):
            return t[:, j, :].rearrange("p (k n) -> p k n", k=KT)

        @block.sync
        def _(sp):
            for j in range(U):
                sp.dma_start(chunk(wr, j), w_feat[j]).then_inc(w_in[j], 16)
            with sp.Fori(0, TURNS - 1) as it:
                for j in range(U):
                    sp.wait_ge(low, U * it + j + 1)
                    sp.dma_start(chunk(wr, j), w_feat[U * it + (j + U)]).then_inc(w_in[j], 16)

        @block.scalar
        def _(act):
            def split(j):
                nc.scalar.copy(chunk(wh, j), chunk(wr, j)).then_inc(high, 1)

            def evacuate(it, j):
                act.wait_ge(done, 2 * U * it + (2 * j + 1))
                nc.scalar.copy(hT[:, U * it + j, 0:512], acc[2 * j][:, :]).then_inc(left, 1)

            for j in range(U):
                act.wait_ge(w_in[j], 16)
                split(j)
            with act.Fori(0, TURNS - 1) as it:
                for j in range(U):
                    evacuate(it, j)
                    act.wait_ge(w_in[j], 16 * it + 32)
                    act.wait_ge(done, 2 * U * it + (2 * j + 2))
                    split(j)
            for j in range(U):
                evacuate(TURNS - 1, j)

        @block.vector
        def _(dve):
            def split(it, j):
                dve.wait_ge(high, U * it + (j + 1))
                nc.vector.tensor_tensor(chunk(wl, j), chunk(wr, j), chunk(wh, j).bitcast(F32),
                                        ALU.subtract).then_inc(low, 1)

            def evacuate(it, j):
                dve.wait_ge(done, 2 * U * it + (2 * j + 2))
                nc.vector.tensor_copy(hT[:, U * it + j, 512:1024], acc[2 * j + 1][:, :]).then_inc(right, 1)

            for j in range(U):
                split(0, j)
            with dve.Fori(0, TURNS - 1) as it:
                for j in range(U):
                    evacuate(it, j)
                    split(it + 1, j)
            for j in range(U):
                evacuate(TURNS - 1, j)

        @block.tensor
        def _(pe):
            def products(it, j, first):
                pe.wait_ge(low, U * it + (j + 1))
                a, b = chunk(wh, j), chunk(wl, j)
                for h, copied in ((0, left), (1, right)):
                    if not first:
                        pe.wait_ge(copied, U * it + (j + 1 - U))
                    cols = slice(512 * h, 512 * h + 512)
                    for k in range(KT):
                        nc.tensor.matmul(acc[2 * j + h][:, :], a[:, k, :], xh[:, k, cols], start=(k == 0), stop=False)
                        nc.tensor.matmul(acc[2 * j + h][:, :], a[:, k, :], xl[:, k, cols], start=False, stop=False)
                        mm = nc.tensor.matmul(acc[2 * j + h][:, :], b[:, k, :], xh[:, k, cols],
                                              start=False, stop=(k == KT - 1))
                    mm.then_inc(done, 1)

            for j in range(U):
                products(0, j, True)
            with pe.Fori(1, TURNS) as it:
                for j in range(U):
                    products(it, j, False)


def after(eng, sem, value):
    if value > 0:
        eng.wait_ge(sem, value)


class Chain:

    def __init__(self, eng, sem, start=0):
        self.eng, self.sem, self.start, self.n = eng, sem, start, 0

    def link(self, ins):
        ins.then_inc(self.sem, 1)
        self.n += 1
        self.eng.wait_ge(self.sem, self.start + self.n)


def softmax_chunks(tiles_of_unit):
    runs = [chunks_of(t) for t in tiles_of_unit]
    before = [0]
    for r in runs:
        before.append(before[-1] + len(r))
    return runs, before


def transpose_run(pe, nc, dst, src, run, first, ident):
    for j, kt in enumerate(run):
        c = (kt - first) * P
        mm = nc.tensor.transpose(dst[:, j, :], src[:, c:c + P], ident[:, :])
    return mm


def values_run(nc, out, ph, pl, run, v_of_tile, opens, closes):
    for j, kt in enumerate(run):
        v = v_of_tile(kt)
        for part in range(3):
            nc.tensor.matmul(out, ph[:, j, :], v[:, part, :], start=(opens and j == 0 and part == 0), stop=False)
        nc.tensor.matmul(out, pl[:, j, :], v[:, 0, :], start=False, stop=False)
        mm = nc.tensor.matmul(out, pl[:, j, :], v[:, 1, :], start=False, stop=(closes and j == len(run) - 1))
    return mm


def diff_phase(nc, hT, v3, y, ident, bias_full, lams, lam_size):
    HT = A_H // 2
    UN = 2 * NT
    tiles = [list(range(QT_ORDER[n % NT] + 1)) for n in range(UN)]
    runs, before = softmax_chunks(tiles)
    R = before[-1]
    LOADS = 8
    CH = 3
    with ExitStack() as ctx:
        def sb(name, shape, dt):
            return ctx.enter_context(nc.sbuf_tensor(name, shape, dt))

        def sem(name):
            return ctx.enter_context(nc.semaphore(name))

        raw = sb("a_raw", [P, 2, S], F32)
        qs = sb("a_queries", [P, 4, S], F32R)
        ks = sb("a_keys", [P, 4, S], F32R)
        bias = sb("a_bias", [P, 2, S], F32)
        pr = sb("a_probs", [P, 4, S], F32)
        pth = sb("a_probsT_high", [P, 4, 4, P], F16)
        ptl = sb("a_probsT_low", [P, 4, 4, P], F16)
        nmax = sb("a_negated_max", [P, 4], F32)
        sums = sb("a_sums", [P, 4], F32)
        lam_in = sb("a_lam_vectors", [P, 4, A_QK], F32)
        lam = sb("a_lam", [P, 8], F32)
        coef = lam[:, 6:8]
        sc = [ctx.enter_context(nc.psum_tensor(f"a_scores{i}", [P, S], F32)) for i in range(2)]
        tp = [ctx.enter_context(nc.psum_tensor(f"a_turned{i}", [P, 4, P], F32)) for i in range(2)]
        ov = [ctx.enter_context(nc.psum_tensor(f"a_out{i}", [P, 512], F32)) for i in range(2)]

        lam_loaded, lam_chain, lam_exp, lam_ready = sem("lam_loaded"), sem("lam_chain"), sem("lam_exp"), sem("lam_ready")
        raw_in = [sem(f"a_raw_in{i}") for i in range(2)]
        bias_in = [sem(f"a_bias_in{i}") for i in range(2)]
        stack_high, stack_ready = sem("a_stack_high"), sem("a_stack_ready")
        scored, biased, exped = sem("a_scored"), sem("a_biased"), sem("a_exped")
        chain, mixed = sem("a_mix_chain"), sem("a_mixed")
        turned, t_high, t_low = sem("a_turned"), sem("a_turned_high"), sem("a_turned_low")
        valued, summed = sem("a_valued"), sem("a_summed")
        block = ctx.enter_context(nc.Block())

        @block.sync
        def _(sp):
            for i in range(4):
                sp.dma_start(lam_in[:, i, :], lams[i:i + 1, :].partition_broadcast(P)).then_inc(lam_loaded, 16)
            for c in range(HT):
                for hh in range(2):
                    after(sp, biased, 2 * UN * c)
                    sp.dma_start(bias[:, hh, :], bias_full[4 * c + (2 * hh + 1)]).then_inc(bias_in[hh], 16)
                    for m in range(2):
                        for kind in range(2):
                            j = 4 * hh + 2 * m + kind
                            after(sp, stack_ready, LOADS * c + max(j - 1, 0))
                            src = hT[HD * hh + A_QK * m:HD * hh + A_QK * (m + 1), c + 2 * kind, :]
                            for band in range(4):
                                sp.dma_start(raw[A_QK * band:A_QK * (band + 1), j % 2, :], src).then_inc(raw_in[j % 2], 16)

        @block.scalar
        def _(act):
            act.wait_ge(lam_ready, 1)
            nc.scalar.activation(lam[:, 2:4], lam[:, 0:2], ACT.Exp).then_inc(lam_exp, 1)

            def stack(c, hh):
                for m in range(2):
                    for kind in range(2):
                        j = 4 * hh + 2 * m + kind
                        act.wait_ge(raw_in[j % 2], 256 * c + 64 * (j // 2 + 1))
                        dst = (qs, ks)[kind]
                        nc.scalar.activation(dst[:, 2 * hh + m, :], raw[:, j % 2, :], ACT.Copy,
                                             scale=A_QK ** -0.5 if kind == 0 else 1.0).then_inc(stack_high, 1)

            def exponentials(c, n):
                w = len(tiles[n]) * P
                for m in range(2):
                    act.wait_ge(biased, 2 * UN * c + (2 * n + m + 1))
                    s = 2 * (n % 2) + m
                    nc.scalar.activation(pr[:, s, 0:w], pr[:, s, 0:w], ACT.Exp, scale=-1.0, bias=nmax[:, s:s + 1],
                                         accum_out=sums[:, s:s + 1]).then_inc(exped, 1)

            def high_part(c, n):
                for r, run in enumerate(runs[n]):
                    g = before[n] + r
                    act.wait_ge(turned, R * c + (g + 1))
                    after(act, valued, R * c + max(g - 3, 0))
                    k = len(run)
                    nc.scalar.activation(pth[:, g % 4, 0:k, :], tp[g % 2][:, 0:k, :], ACT.Copy,
                                         scale=PSCALE).then_inc(t_high, 1)

            def write_out(c, hh):
                head = 2 * c + hh
                act.wait_ge(valued, R * c + before[NT * (hh + 1)])
                nc.scalar.copy(y[:, :, HD * head:HD * (head + 1)],
                               ov[head % 2][:, :].rearrange("p (q d) -> p q d", q=NT)).then_inc(summed, 1)

            for c in range(HT):
                after(act, scored, 2 * UN * c)
                stack(c, 0)
                exponentials(c, 0)
                for n in range(UN):
                    if n == 1:
                        stack(c, 1)
                    if n + 1 < UN:
                        exponentials(c, n + 1)
                    high_part(c, n)
                    if n == NT + 2:
                        write_out(c, 0)
                write_out(c, 1)

        @block.vector
        def _(dve):
            lc = Chain(dve, lam_chain)
            dve.wait_ge(lam_loaded, 64)
            for i in range(2):
                lc.link(nc.vector.tensor_tensor_reduce(out=lam_in[:, 2 * i, :], in0=lam_in[:, 2 * i, :],
                                                       in1=lam_in[:, 2 * i + 1, :], scale=1.0, scalar=0.0,
                                                       op0=ALU.mult, op1=ALU.add, accum_out=lam[:, i:i + 1]))
            nc.vector.tensor_copy(lam[:, 4:5], lam[:, 0:1]).then_inc(lam_ready, 1)
            dve.wait_ge(lam_exp, 1)
            lc.link(nc.vector.tensor_tensor(lam[:, 4:5], lam[:, 2:3], lam[:, 3:4], ALU.subtract))
            lc.link(nc.vector.tensor_scalar(lam[:, 4:5], lam[:, 4:5], LAM_INIT, None, ALU.add))
            lc.link(nc.vector.tensor_scalar(lam[:, 5:6], lam[:, 4:5], -1.0, None, ALU.mult))
            lc.link(nc.vector.tensor_tensor(lam[:, 5:6], lam[:, 5:6], lam[:, 4:5], ALU.max))
            lc.link(nc.vector.tensor_scalar(lam[:, 5:6], lam[:, 5:6], 1.0, None, ALU.add))
            lc.link(nc.vector.tensor_copy(lam_size[:, :], lam[:, 5:6]))
            lc.link(nc.vector.reciprocal(coef[:, 0:1], lam[:, 5:6]))
            lc.link(nc.vector.scalar_tensor_tensor(out=coef[:, 1:2], in0=lam[:, 4:5], scalar=-1.0, in1=coef[:, 0:1],
                                                   op0=ALU.mult, op1=ALU.mult))

            def stack(c, hh):
                for m in range(2):
                    for kind in range(2):
                        j = 4 * hh + 2 * m + kind
                        dve.wait_ge(stack_high, LOADS * c + (j + 1))
                        s = 2 * hh + m
                        if kind == 0:
                            low = qs[2 * A_QK:4 * A_QK, s, :]
                            ins = nc.vector.scalar_tensor_tensor(
                                out=low, in0=raw[2 * A_QK:4 * A_QK, j % 2, :], scalar=A_QK ** -0.5,
                                in1=low.bitcast(F32), op0=ALU.mult, op1=ALU.subtract)
                        else:
                            for band in (1, 2):
                                rows = slice(A_QK * band, A_QK * (band + 1))
                                ins = nc.vector.tensor_tensor(ks[rows, s, :], raw[rows, j % 2, :],
                                                              ks[rows, s, :].bitcast(F32), ALU.subtract)
                        ins.then_inc(stack_ready, 1)

            def add_bias(c, n):
                w = len(tiles[n]) * P
                at = score_layout(len(tiles[n]))[0]
                hh = n // NT
                if n % NT == 0:
                    dve.wait_ge(bias_in[hh], 16 * c + 16)
                after(dve, turned, R * c + before[max(n - 1, 0)])
                for m in range(2):
                    dve.wait_ge(scored, 2 * UN * c + (2 * n + m + 1))
                    s = 2 * (n % 2) + m
                    nc.vector.tensor_tensor_reduce(out=pr[:, s, 0:w], in0=sc[m][:, at:at + w], in1=bias[:, hh, S - w:S],
                                                   scale=-1.0, scalar=BIG, op0=ALU.add, op1=ALU.min,
                                                   accum_out=nmax[:, s:s + 1]).then_inc(biased, 1)

            def mix(c, n):
                w = len(tiles[n]) * P
                s = 2 * (n % 2)
                dve.wait_ge(exped, 2 * UN * c + (2 * n + 2))
                ch = Chain(dve, chain, CH * UN * c + CH * n)
                ch.link(nc.vector.reciprocal(sums[:, s:s + 2], sums[:, s:s + 2]))
                ch.link(nc.vector.tensor_tensor(sums[:, s:s + 2], sums[:, s:s + 2], coef, ALU.mult))
                ch.link(nc.vector.tensor_scalar(pr[:, s + 1, 0:w], pr[:, s + 1, 0:w], sums[:, s + 1:s + 2], None, ALU.mult))
                nc.vector.scalar_tensor_tensor(out=pr[:, s, 0:w], in0=pr[:, s, 0:w], scalar=sums[:, s:s + 1],
                                               in1=pr[:, s + 1, 0:w], op0=ALU.mult, op1=ALU.add).then_inc(mixed, 1)

            def low_part(c, n):
                for r, run in enumerate(runs[n]):
                    g = before[n] + r
                    dve.wait_ge(t_high, R * c + (g + 1))
                    k = len(run)
                    nc.vector.scalar_tensor_tensor(out=ptl[:, g % 4, 0:k, :], in0=tp[g % 2][:, 0:k, :], scalar=PSCALE,
                                                   in1=pth[:, g % 4, 0:k, :], op0=ALU.mult,
                                                   op1=ALU.subtract).then_inc(t_low, 1)

            for c in range(HT):
                stack(c, 0)
                add_bias(c, 0)
                mix(c, 0)
                for n in range(UN):
                    if n == 1:
                        stack(c, 1)
                    if n + 1 < UN:
                        add_bias(c, n + 1)
                    low_part(c, n)
                    if n + 1 < UN:
                        mix(c, n + 1)

        @block.tensor
        def _(pe):
            def scores(c, n):
                hh, qt = n // NT, QT_ORDER[n % NT]
                if n % NT == 0:
                    pe.wait_ge(stack_ready, LOADS * c + 4 * (hh + 1))
                after(pe, biased, 2 * UN * c + 2 * n)
                for m in range(2):
                    s = 2 * hh + m
                    for at, key, w in score_layout(max(qt + 1, 2))[1]:
                        mm = nc.tensor.matmul(sc[m][:, at:at + w], qs[:, s, qt * P:(qt + 1) * P], ks[:, s, key:key + w],
                                              start=True, stop=True)
                    mm.then_inc(scored, 1)

            def turn(c, n):
                pe.wait_ge(mixed, UN * c + (n + 1))
                for r, run in enumerate(runs[n]):
                    g = before[n] + r
                    after(pe, t_low, R * c + max(g - 1, 0))
                    transpose_run(pe, nc, tp[g % 2], pr[:, 2 * (n % 2), :], run, 0, ident).then_inc(turned, 1)

            def values(c, n):
                hh, qt = n // NT, QT_ORDER[n % NT]
                head = 2 * c + hh
                if n % NT == 0:
                    after(pe, summed, head - 1)
                for r, run in enumerate(runs[n]):
                    g = before[n] + r
                    pe.wait_ge(t_low, R * c + (g + 1))
                    values_run(nc, ov[head % 2][:, HD * qt:HD * (qt + 1)], pth[:, g % 4], ptl[:, g % 4], run,
                               lambda kt: v3[:, kt, head, :, :],
                               r == 0, r == len(runs[n]) - 1).then_inc(valued, 1)

            for c in range(HT):
                scores(c, 0)
                for n in range(UN):
                    if n + 1 < UN:
                        scores(c, n + 1)
                    turn(c, n)
                    if n >= 1:
                        values(c, n - 1)
                values(c, UN - 1)


def swa_phase(nc, hT, v3, y, ident, bias_swa, sinks):
    UN = 2 * NT
    tiles = [list(range(max(n % NT - 1, 0), n % NT + 1)) for n in range(UN)]
    LOADS = 3
    CH = 1 + 2 * 3
    with ExitStack() as ctx:
        def sb(name, shape, dt):
            return ctx.enter_context(nc.sbuf_tensor(name, shape, dt))

        def sem(name):
            return ctx.enter_context(nc.semaphore(name))

        raw = sb("b_raw", [P, 3, S], F32)
        qs = sb("b_queries", [P, 2, S], F32R)
        kh = sb("b_keys_high", [P, S], F32R)
        kl = sb("b_keys_low", [P, S], F32R)
        bias = sb("b_bias", [P, 2, BW], F32)
        pr = sb("b_probs", [P, 4, BW], F32)
        pth = sb("b_probsT_high", [P, 4, 2, P], F16)
        ptl = sb("b_probsT_low", [P, 4, 2, P], F16)
        nmax = sb("b_negated_max", [P, 2, NT], F32)
        sums = sb("b_sums", [P, 2, NT], F32)
        sink_exp = sb("b_sink_exp", [P, 2, NT], F32)
        sink = sb("b_sink", [P, 2], F32)
        nsink = sb("b_negated_sink", [P, 2], F32)
        sc = [ctx.enter_context(nc.psum_tensor(f"b_scores{i}", [P, 512], F32)) for i in range(4)]
        tp = [ctx.enter_context(nc.psum_tensor(f"b_turned{i}", [P, 4, P], F32)) for i in range(2)]
        ov = [ctx.enter_context(nc.psum_tensor(f"b_out{i}", [P, 512], F32)) for i in range(2)]

        raw_in = [sem(f"b_raw_in{i}") for i in range(LOADS)]
        bias_in, sink_in = sem("b_bias_in"), sem("b_sink_in")
        stack_high, stack_ready = sem("b_stack_high"), sem("b_stack_ready")
        scored, biased, exped, sink_exped = sem("b_scored"), sem("b_biased"), sem("b_exped"), sem("b_sink_exped")
        turned, t_high, t_low = sem("b_turned"), sem("b_turned_high"), sem("b_turned_low")
        valued, chain, headed = sem("b_valued"), sem("b_chain"), sem("b_headed")
        block = ctx.enter_context(nc.Block())

        @block.sync
        def _(sp):
            for c in range(KV):
                after(sp, headed, 2 * c)
                sp.dma_start(bias[:, :, :], bias_swa[c]).then_inc(bias_in, 16)
                sp.dma_start(sink[:, :], sinks[c].partition_broadcast(P)).then_inc(sink_in, 16)
                after(sp, stack_ready, LOADS * c)
                for j in range(LOADS):
                    src = hT[0:HD, c + 6, :] if j == 0 else hT[HD * (j - 1):HD * j, c + 4, :]
                    for band in range(2):
                        sp.dma_start(raw[HD * band:HD * (band + 1), j, :], src).then_inc(raw_in[j], 16)

        @block.scalar
        def _(act):
            def exponentials(c, n):
                w = len(tiles[n]) * P
                hh, qt = n // NT, n % NT
                act.wait_ge(biased, UN * c + (n + 1))
                nc.scalar.activation(pr[:, n % 4, 0:w], pr[:, n % 4, 0:w], ACT.Exp, scale=-1.0,
                                     bias=nmax[:, hh, qt:qt + 1], accum_out=sums[:, hh, qt:qt + 1]).then_inc(exped, 1)
                if qt == NT - 1:
                    nc.scalar.activation(sink_exp[:, hh, :], nmax[:, hh, :], ACT.Exp,
                                         bias=sink[:, hh:hh + 1]).then_inc(sink_exped, 1)

            def high_part(c, n):
                act.wait_ge(turned, UN * c + (n + 1))
                after(act, valued, UN * c + max(n - 3, 0))
                k = len(tiles[n])
                nc.scalar.activation(pth[:, n % 4, 0:k, :], tp[n % 2][:, 0:k, :], ACT.Copy,
                                     scale=PSCALE).then_inc(t_high, 1)

            for c in range(KV):
                after(act, scored, UN * c)
                for j in range(LOADS):
                    act.wait_ge(raw_in[j], 32 * c + 32)
                    if j == 0:
                        nc.scalar.copy(kh[:, :], raw[:, j, :]).then_inc(stack_high, 1)
                    else:
                        nc.scalar.activation(qs[:, j - 1, :], raw[:, j, :], ACT.Copy,
                                             scale=HD ** -0.5).then_inc(stack_high, 1)
                exponentials(c, 0)
                exponentials(c, 1)
                for n in range(UN):
                    if n + 2 < UN:
                        exponentials(c, n + 2)
                    high_part(c, n)

        @block.vector
        def _(dve):
            def add_bias(c, n):
                w = len(tiles[n]) * P
                hh, qt = n // NT, n % NT
                after(dve, turned, UN * c + max(n - 3, 0))
                dve.wait_ge(scored, UN * c + (n + 1))
                nc.vector.tensor_tensor_reduce(out=pr[:, n % 4, 0:w], in0=sc[n % 4][:, 0:w], in1=bias[:, hh, BW - w:BW],
                                               scale=-1.0, scalar=nsink[:, hh:hh + 1], op0=ALU.add, op1=ALU.min,
                                               accum_out=nmax[:, hh, qt:qt + 1]).then_inc(biased, 1)

            def low_part(c, n):
                dve.wait_ge(t_high, UN * c + (n + 1))
                k = len(tiles[n])
                nc.vector.scalar_tensor_tensor(out=ptl[:, n % 4, 0:k, :], in0=tp[n % 2][:, 0:k, :], scalar=PSCALE,
                                               in1=pth[:, n % 4, 0:k, :], op0=ALU.mult,
                                               op1=ALU.subtract).then_inc(t_low, 1)

            def write_out(c, hh, ch):
                head = 2 * c + hh
                dve.wait_ge(sink_exped, 2 * c + (hh + 1))
                s = sums[:, hh, :]
                ch.link(nc.vector.tensor_tensor(s, s, sink_exp[:, hh, :], ALU.add))
                ch.link(nc.vector.tensor_scalar(s, s, PSCALE, None, ALU.mult))
                ch.link(nc.vector.reciprocal(s, s))
                dve.wait_ge(valued, UN * c + NT * (hh + 1))
                nc.vector.tensor_tensor(y[:, :, HD * (A_H + head):HD * (A_H + head + 1)],
                                        ov[head % 2][:, :].rearrange("p (q d) -> p q d", q=NT),
                                        s.unsqueeze(2).broadcast_to([P, NT, HD]), ALU.mult).then_inc(headed, 1)

            for c in range(KV):
                ch = Chain(dve, chain, CH * c)
                for j in range(LOADS):
                    dve.wait_ge(stack_high, LOADS * c + (j + 1))
                    if j == 0:
                        ins = nc.vector.tensor_tensor(kl[:, :], raw[:, j, :], kh[:, :].bitcast(F32), ALU.subtract)
                    else:
                        low = qs[HD:P, j - 1, :]
                        ins = nc.vector.scalar_tensor_tensor(out=low, in0=raw[HD:P, j, :], scalar=HD ** -0.5,
                                                             in1=low.bitcast(F32), op0=ALU.mult, op1=ALU.subtract)
                    ins.then_inc(stack_ready, 1)
                dve.wait_ge(sink_in, 16 * c + 16)
                ch.link(nc.vector.tensor_scalar(nsink[:, :], sink[:, :], -1.0, None, ALU.mult))
                dve.wait_ge(bias_in, 16 * c + 16)
                add_bias(c, 0)
                add_bias(c, 1)
                for n in range(UN):
                    if n + 2 < UN:
                        add_bias(c, n + 2)
                    low_part(c, n)
                    if n == NT + 2:
                        write_out(c, 0, ch)
                write_out(c, 1, ch)
                assert ch.n == CH

        @block.tensor
        def _(pe):
            def scores(c, n):
                hh, qt = n // NT, n % NT
                if qt == 0:
                    pe.wait_ge(stack_ready, LOADS * c + (hh + 2))
                after(pe, biased, UN * c + max(n - 3, 0))
                q = qs[:, hh, qt * P:(qt + 1) * P]
                key = max(qt - 1, 0) * P
                nc.tensor.matmul(sc[n % 4][:, 0:BW], q, kh[:, key:key + BW], start=True, stop=False)
                nc.tensor.matmul(sc[n % 4][:, 0:BW], q, kl[:, key:key + BW], start=False, stop=True).then_inc(scored, 1)

            def turn(c, n):
                pe.wait_ge(exped, UN * c + (n + 1))
                after(pe, t_low, UN * c + max(n - 1, 0))
                transpose_run(pe, nc, tp[n % 2], pr[:, n % 4, :], tiles[n], tiles[n][0], ident).then_inc(turned, 1)

            def values(c, n):
                hh, qt = n // NT, n % NT
                head = 2 * c + hh
                if qt == 0:
                    after(pe, headed, head - 1)
                pe.wait_ge(t_low, UN * c + (n + 1))
                values_run(nc, ov[head % 2][:, HD * qt:HD * (qt + 1)], pth[:, n % 4], ptl[:, n % 4], tiles[n],
                           lambda kt: v3[:, kt, A_H + c, :, :],
                           True, True).then_inc(valued, 1)

            for c in range(KV):
                scores(c, 0)
                scores(c, 1)
                for n in range(UN):
                    if n + 2 < UN:
                        scores(c, n + 2)
                    turn(c, n)
                    if n >= 1:
                        values(c, n - 1)
                values(c, UN - 1)


def compress_phase(nc, hT, w1, w2k, w2v, pe_pairs, kch, kcl, vc3):
    NC2 = KV * NCMP
    with ExitStack() as ctx:
        def sb(name, shape, dt):
            return ctx.enter_context(nc.sbuf_tensor(name, shape, dt))

        def sem(name):
            return ctx.enter_context(nc.semaphore(name))

        cc = sb("c_pairs", [P, 2, KV + 1, S], F32)
        w1s = sb("c_w1", [P, 2, CPL, P], F32)
        w2ks = sb("c_w2k", [P, P], F32)
        w2vs = sb("c_w2v", [P, HD], F32)
        pes = sb("c_pe", [P, 2, CPL], F32)
        z = sb("c_hidden", [P, 2, NC2], F32)
        e = sb("c_hidden_exp", [P, 2, NC2], F32)
        rest = sb("c_value_rest", [P, KV, HD], F32)
        hid = [ctx.enter_context(nc.psum_tensor(f"c_hid{i}", [P, 512], F32)) for i in range(2)]
        kp = ctx.enter_context(nc.psum_tensor("c_key", [P, 512], F32))
        vp = [ctx.enter_context(nc.psum_tensor(f"c_value{g}", [P, 512], F32)) for g in range(KV)]
        w_in, w2_in, pe_in, cc_in = sem("c_w1_in"), sem("c_w2_in"), sem("c_pe_in"), [sem(f"c_pairs_in{i}") for i in range(2)]
        zeroed, placed, hidden, biased, exped = sem("c_zeroed"), sem("c_pe_placed"), sem("c_hidden_done"), sem("c_hid_biased"), sem("c_hid_exp")
        chain, act_ready, keyed, valued = sem("c_chain"), sem("c_silu"), sem("c_keyed"), sem("c_value_done")
        key_high, first = sem("c_key_high"), sem("c_value_first")
        block = ctx.enter_context(nc.Block())

        @block.sync
        def _(sp):
            sp.dma_start(w1s[:, :, :, :], w1).then_inc(w_in, 16)
            sp.dma_start(pes[:, :, :], pe_pairs).then_inc(pe_in, 16)
            for kv in range(2):
                for g in range(KV):
                    src = hT[HD:P, 8 + g, :] if kv == 0 else hT[HD * g:HD * (g + 1), 14, :]
                    sp.dma_start(cc[0:HD, kv, g, :], src).then_inc(cc_in[kv], 16)
                    sp.dma_start(cc[HD:P, kv, g, 0:S - 1], src[:, 1:S]).then_inc(cc_in[kv], 16)
            sp.dma_start(w2ks[:, :], w2k).then_inc(w2_in, 16)
            sp.dma_start(w2vs[:, :], w2v).then_inc(w2_in, 16)

        @block.scalar
        def _(act):
            for kv in range(2):
                act.wait_ge(biased, kv + 1)
                nc.scalar.activation(e[:, kv, :], z[:, kv, :], ACT.Exp, scale=-1.0).then_inc(exped, 1)
            act.wait_ge(keyed, 1)
            act.wait_ge(zeroed, 3)
            nc.scalar.copy(kch[:, :, 0:NCMP], kp[:, 0:NC2].rearrange("p (g n) -> p g n", g=KV)).then_inc(key_high, 1)
            for g in range(KV):
                act.wait_ge(valued, g + 1)
                for half in range(2):
                    rows = slice(HD * half, HD * half + NCMP)
                    nc.scalar.copy(vc3[rows, g, 0, :], vp[g][rows, 0:HD]).then_inc(first, 1)

        @block.vector
        def _(dve):
            nc.vector.memset(cc[:, :, KV, :], 0.0).then_inc(chain, 1)
            nc.vector.memset(kch[:, :, NCMP:HD].bitcast(F32), 0.0).then_inc(zeroed, 1)
            nc.vector.memset(kcl[:, :, NCMP:HD].bitcast(F32), 0.0).then_inc(zeroed, 1)
            nc.vector.memset(vc3[:, :, :, :], 0.0).then_inc(zeroed, 1)
            dve.wait_ge(chain, 1)
            ch = Chain(dve, chain, 1)
            dve.wait_ge(pe_in, 16)
            nc.vector.tensor_copy(cc[:, :, KV, 0:2 * CPL:2], pes[:, :, :]).then_inc(placed, 1)
            for kv in range(2):
                dve.wait_ge(hidden, kv + 1)
                nc.vector.tensor_scalar(z[:, kv, :], hid[kv][:, 0:NC2], hid[kv][:, NC2:NC2 + 1], None,
                                        ALU.add).then_inc(biased, 1)
            for kv in range(2):
                dve.wait_ge(exped, kv + 1)
                ch.link(nc.vector.tensor_scalar(e[:, kv, :], e[:, kv, :], 1.0, None, ALU.add))
                ch.link(nc.vector.reciprocal(e[:, kv, :], e[:, kv, :]))
                nc.vector.tensor_tensor(z[:, kv, :], z[:, kv, :], e[:, kv, :], ALU.mult).then_inc(act_ready, 1)
            dve.wait_ge(key_high, 1)
            ch.link(nc.vector.tensor_tensor(kcl[:, :, 0:NCMP], kp[:, 0:NC2].rearrange("p (g n) -> p g n", g=KV),
                                            kch[:, :, 0:NCMP].bitcast(F32), ALU.subtract))
            for g in range(KV):
                dve.wait_ge(first, 2 * g + 2)
                for half in range(2):
                    rows = slice(HD * half, HD * half + NCMP)
                    ch.link(nc.vector.tensor_tensor(rest[rows, g, :], vp[g][rows, 0:HD], vc3[rows, g, 0, :], ALU.subtract))
                    ch.link(nc.vector.tensor_copy(vc3[rows, g, 1, :], rest[rows, g, :]))
                    ch.link(nc.vector.tensor_tensor(vc3[rows, g, 2, :], rest[rows, g, :], vc3[rows, g, 1, :], ALU.subtract))

        @block.tensor
        def _(pe):
            pe.wait_ge(w_in, 16)
            pe.wait_ge(placed, 1)
            for kv in range(2):
                pe.wait_ge(cc_in[kv], 64)
                out = hid[kv][:, 0:(KV + 1) * NCMP].rearrange("p (g n) -> p g n", g=KV + 1)
                for lp in range(CPL):
                    mm = nc.tensor.matmul(out, w1s[:, kv, lp, :], cc[:, kv, :, 2 * lp:2 * lp + 16 * (NCMP - 1) + 1:16],
                                          start=(lp == 0), stop=(lp == CPL - 1))
                mm.then_inc(hidden, 1)
            pe.wait_ge(w2_in, 32)
            pe.wait_ge(act_ready, 1)
            nc.tensor.matmul(kp[:, 0:NC2], w2ks[:, :], z[:, 0, :], start=True, stop=True).then_inc(keyed, 1)
            pe.wait_ge(act_ready, 2)
            for g in range(KV):
                for half in range(2):
                    mm = nc.tensor.matmul(vp[g][HD * half:HD * half + NCMP, 0:HD], z[:, 1, NCMP * g:NCMP * (g + 1)],
                                          w2vs[:, :], start=True, stop=True)
                mm.then_inc(valued, 1)


def nsa_phase(nc, hT, v3, y, ident, kch, kcl, vc3, glog, bias_full, bias_win, bias_cmp, row_valid, force, blocks):
    HU = 2 * NT
    UN = RC * HU
    tiles = []
    for n in range(UN):
        qt = QT_ORDER[n % NT]
        tiles.append(list(range(qt + 1)) if n % HU < NT else list(range(max(qt - 4, 0), qt + 1)))
    runs, before = softmax_chunks(tiles)
    R = before[-1]
    AHEAD = 2
    PS, TS, OS, GS = 4, 2, 2, 6
    LOADS = RC + 2
    PAIRS = NT // 2
    CH = 7 * RC - 1 + 7 + 2 + 3 * 2 * RC
    with ExitStack() as ctx:
        def sb(name, shape, dt):
            return ctx.enter_context(nc.sbuf_tensor(name, shape, dt))

        def sem(name):
            return ctx.enter_context(nc.semaphore(name))

        raw = hT[:, 0:2, :]
        bf = hT[:, 2:4, :]
        blk_in = hT[:, 4, :]
        qs = sb("s_queries", [P, RC, S], F32R)
        kh = sb("s_keys_high", [P, 2, S], F32R)
        kl = sb("s_keys_low", [P, 2, S], F32R)
        ck = sb("s_cmp_keys", [P, 2, HD], F32R)
        cv = sb("s_cmp_values", [P, 3, HD], BF16)
        bw = sb("s_bias_window", [P, 2, CW], F32)
        bc = sb("s_bias_cmp", [P, 2, NT * HD], F32)
        pr = sb("s_probs", [P, PS, S], F32)
        pth = sb("s_probsT_high", [P, GS, 4, P], F16)
        ptl = sb("s_probsT_low", [P, GS, 4, P], F16)
        nmax = sb("s_negated_max", [P, 2, NT], F32)
        sums = sb("s_sums", [P, 2, 2, NT], F32)
        red = sb("s_out", [P, NT, HD], F32)
        cmax = sb("s_cmp_max", [P, RC, NT], F32)
        csum = sb("s_cmp_sums", [P, RC, NT], F32)
        pbar = sb("s_cmp_probs_sum", [P, 2, SEL_T * HD], F32)
        imp = sb("s_importance", [P, SEL_T, NSLC], F32)
        tail = sb("s_importance_tail", [P, SEL_T, NSLC], F32)
        left = sb("s_not_chosen_scores", [P, SEL_T, NSLC], F32)
        top8 = sb("s_top8", [P, SEL_T, 8], F32)
        unsel = sb("s_not_chosen", [P, SEL_T, 32], F32)
        unselT = sb("s_not_chosenT", [P, P], BF16)
        valid0 = sb("s_row_valid", [P, NT], F32)
        forced = sb("s_forced", [P, SEL_T, NSLC], F32)
        blk = sb("s_blocks", [P, S], BF16)
        gate = sb("s_gates", [P, NT, 3 * C_H], F32)
        sc = [ctx.enter_context(nc.psum_tensor(f"s_scores{i}", [P, S], F32)) for i in range(2)]
        tp = [ctx.enter_context(nc.psum_tensor(f"s_turned{i}", [P, 4, P], F32)) for i in range(2)]
        ov = [ctx.enter_context(nc.psum_tensor(f"s_out{i}", [P, 512], F32)) for i in range(2)]

        const_in, gate_exp, gate_chain = sem("s_const_in"), sem("s_gate_exp"), sem("s_gate_chain")
        raw_in = [sem(f"s_raw_in{i}") for i in range(2)]
        bc_in = [sem(f"s_bias_cmp_in{i}") for i in range(2)]
        bf_in = [sem(f"s_bias_full_in{i}") for i in range(2)]
        bw_in = [sem(f"s_bias_window_in{i}") for i in range(2)]
        stack_high, stack_ready, cmp_copied = sem("s_stack_high"), sem("s_stack_ready"), sem("s_cmp_copied")
        c_scored, c_shifted, c_exped, c_normed = sem("c_scored"), sem("c_shifted"), sem("c_exped"), sem("c_normed")
        c_turned, c_high, c_low, c_valued, c_summed = sem("c_turned"), sem("c_high"), sem("c_low"), sem("c_valued"), sem("c_summed")
        chosen, chosen_turned, mask_ready = sem("s_chosen"), sem("s_chosen_turned"), sem("s_mask_ready")
        scored, biased, exped = sem("s_scored"), sem("s_biased"), sem("s_exped")
        turned, t_high, t_low = sem("s_turned"), sem("s_turned_high"), sem("s_turned_low")
        valued, chain, headed = sem("s_valued"), sem("s_chain"), sem("s_headed")
        block = ctx.enter_context(nc.Block())

        def c_cols(r):
            return slice(PAIRS * HD * (r % 2), PAIRS * HD * (r % 2 + 1))

        def place(n):
            return n // HU, n % HU // NT, QT_ORDER[n % NT]

        @block.sync
        def _(sp):
            sp.dma_start(valid0[:, :], row_valid).then_inc(const_in, 16)
            sp.dma_start(forced[:, :, :], force).then_inc(const_in, 16)
            sp.dma_start(blk_in, blocks).then_inc(const_in, 16)
            for c in range(KV):
                for j in range(LOADS):
                    after(sp, stack_ready, LOADS * c + max(j - 1, 0))
                    if j < RC:
                        src = hT[HD * (j % 2):HD * (j % 2 + 1), 2 * c + (10 + j // 2), :]
                    else:
                        src = hT[HD:P, c + 6, :] if j == RC else hT[0:HD, c + 8, :]
                    for band in range(2):
                        sp.dma_start(raw[HD * band:HD * (band + 1), j % 2, :], src).then_inc(raw_in[j % 2], 16)
                    if j < RC:
                        after(sp, c_shifted, RC * c + max(j - 1, 0))
                        sp.dma_start(bc[:, j % 2, :], bias_cmp[RC * c + j]).then_inc(bc_in[j % 2], 16)
                for r in range(RC):
                    after(sp, biased, UN * c + max(r - 1, 0) * HU)
                    sp.dma_start(bf[:, r % 2, :], bias_full[RC * c + r]).then_inc(bf_in[r % 2], 16)
                    sp.dma_start(bw[:, r % 2, :], bias_win[RC * c + r]).then_inc(bw_in[r % 2], 16)

        @block.scalar
        def _(act):
            nc.scalar.activation(gate[:, :, :], glog[:, :, :], ACT.Exp, scale=-1.0).then_inc(gate_exp, 1)

            def stack(c, j):
                act.wait_ge(raw_in[j % 2], 96 * c + 32 * (j // 2 + 1))
                if j < RC:
                    nc.scalar.activation(qs[:, j, :], raw[:, j % 2, :], ACT.Copy, scale=HD ** -0.5).then_inc(stack_high, 1)
                else:
                    nc.scalar.copy(kh[:, j - RC, :], raw[:, j % 2, :]).then_inc(stack_high, 1)

            def exponentials(c, n):
                w = len(tiles[n]) * P
                r, br, qt = place(n)
                act.wait_ge(biased, UN * c + (n + 1))
                nc.scalar.activation(pr[:, n % PS, 0:w], pr[:, n % PS, 0:w], ACT.Exp, scale=-1.0,
                                     bias=nmax[:, br, qt:qt + 1],
                                     accum_out=sums[:, r % 2, br, qt:qt + 1]).then_inc(exped, 1)

            def high_part(c, n):
                for i, run in enumerate(runs[n]):
                    g = before[n] + i
                    act.wait_ge(turned, R * c + (g + 1))
                    after(act, valued, R * c + max(g + 1 - GS, 0))
                    k = len(run)
                    nc.scalar.activation(pth[:, g % GS, 0:k, :], tp[g % TS][:, 0:k, :], ACT.Copy,
                                         scale=PSCALE).then_inc(t_high, 1)

            for c in range(KV):
                after(act, scored, UN * c)
                after(act, c_valued, RC * c)
                nc.scalar.copy(ck[:, 0, :], kch[:, c, :].bitcast(F32)).then_inc(cmp_copied, 1)
                nc.scalar.copy(ck[:, 1, :], kcl[:, c, :].bitcast(F32)).then_inc(cmp_copied, 1)
                nc.scalar.copy(cv[:, :, :], vc3[:, c, :, :]).then_inc(cmp_copied, 1)
                stack(c, 0)
                for r in range(RC):
                    stack(c, r + 1)
                    act.wait_ge(c_shifted, RC * c + (r + 1))
                    nc.scalar.activation(pr[:, r % 2, 0:NT * HD], pr[:, r % 2, 0:NT * HD], ACT.Exp).then_inc(c_exped, 1)
                    act.wait_ge(c_turned, RC * c + (r + 1))
                    after(act, valued, R * c)
                    if r >= 2:
                        after(act, c_valued, RC * c + (r - 1))
                    nc.scalar.activation(pth[:, r % 2, :, :], tp[r % 2][:, :, :], ACT.Copy, scale=PSCALE).then_inc(c_high, 1)
                stack(c, RC + 1)
                if c == 0:
                    act.wait_ge(const_in, 48)
                    nc.scalar.copy(blk[:, :], blk_in).then_inc(mask_ready, 1)
                act.wait_ge(chosen_turned, c + 1)
                nc.scalar.copy(unselT[:, :], tp[0][:, 0, :]).then_inc(mask_ready, 1)
                exponentials(c, 0)
                act.wait_ge(c_valued, RC * (c + 1))
                for n in range(UN):
                    if n + 1 < UN:
                        exponentials(c, n + 1)
                    high_part(c, n)

        @block.vector
        def _(dve):
            gc = Chain(dve, gate_chain)
            dve.wait_ge(gate_exp, 1)
            gc.link(nc.vector.tensor_scalar(gate[:, :, :], gate[:, :, :], 1.0, PSCALE, ALU.add, ALU.mult))
            gc.link(nc.vector.reciprocal(gate[:, :, :], gate[:, :, :]))
            gc.link(nc.vector.memset(unsel[:, :, :], 0.0))
            dve.wait_ge(const_in, 48)

            def gate_of(c, r, br):
                return gate[:, :, 3 * (RC * c + r) + br:3 * (RC * c + r) + br + 1]

            def y_of(c, r):
                return y[:, :, HD * (A_H + B_H + RC * c + r):HD * (A_H + B_H + RC * c + r + 1)]

            def stack(c, j):
                dve.wait_ge(stack_high, LOADS * c + (j + 1))
                if j < RC:
                    low = qs[HD:P, j, :]
                    ins = nc.vector.scalar_tensor_tensor(out=low, in0=raw[HD:P, j % 2, :], scalar=HD ** -0.5,
                                                         in1=low.bitcast(F32), op0=ALU.mult, op1=ALU.subtract)
                else:
                    ins = nc.vector.tensor_tensor(kl[:, j - RC, :], raw[:, j % 2, :], kh[:, j - RC, :].bitcast(F32),
                                                  ALU.subtract)
                ins.then_inc(stack_ready, 1)

            def by_tile(r):
                return pr[:, r % 2, 0:NT * HD].rearrange("p (t n) -> p t n", t=NT)

            def over_blocks(v):
                return v.unsqueeze(2).broadcast_to([P, NT, HD])

            def shift(c, r, ch):
                dve.wait_ge(bc_in[r % 2], 32 * c + 16 * (r // 2 + 1))
                dve.wait_ge(c_scored, RC * c + (r + 1))
                after(dve, turned, R * c)
                if r >= 2:
                    dve.wait_ge(c_turned, RC * c + (r - 1))
                x = by_tile(r)
                ch.link(nc.vector.tensor_tensor(pr[:, r % 2, 0:NT * HD], sc[r % 2][:, 0:NT * HD], bc[:, r % 2, :], ALU.add))
                ch.link(nc.vector.tensor_reduce(cmax[:, r, :], x, AX.X, ALU.max))
                nc.vector.tensor_tensor(x, x, over_blocks(cmax[:, r, :]), ALU.subtract).then_inc(c_shifted, 1)

            def norm(c, r, ch):
                x = by_tile(r)
                dve.wait_ge(c_exped, RC * c + (r + 1))
                ch.link(nc.vector.tensor_reduce(csum[:, r, :], x, AX.X, ALU.add))
                ch.link(nc.vector.reciprocal(csum[:, r, :], csum[:, r, :]))
                ch.link(nc.vector.tensor_tensor(csum[:, r, :], csum[:, r, :], valid0[:, :], ALU.mult))
                nc.vector.tensor_tensor(x, x, over_blocks(csum[:, r, :]), ALU.mult).then_inc(c_normed, 1)
                dve.wait_ge(c_normed, RC * c + (r + 1))
                late = pr[:, r % 2, SEL_T * HD:NT * HD]
                flushed = pbar[:, 0, :] if r == 0 else pbar[:, 1, :]
                ch.link(nc.vector.scalar_tensor_tensor(out=flushed, in0=late, scalar=TINY, in1=late, op0=ALU.is_ge,
                                                       op1=ALU.mult))
                if r > 0:
                    ch.link(nc.vector.tensor_tensor(pbar[:, 0, :], pbar[:, 0, :], pbar[:, 1, :], ALU.add))

            def split_compressed(c, r):
                dve.wait_ge(c_high, RC * c + (r + 1))
                nc.vector.scalar_tensor_tensor(out=ptl[:, r % 2, :, :], in0=tp[r % 2][:, :, :], scalar=PSCALE,
                                               in1=pth[:, r % 2, :, :], op0=ALU.mult, op1=ALU.subtract).then_inc(c_low, 1)

            def write_compressed(c, r):
                dve.wait_ge(c_valued, RC * c + (r + 1))
                for half in range(2):
                    ins = nc.vector.tensor_tensor(y_of(c, r)[:, half:NT:2, :],
                                                  ov[half][:, c_cols(r)].rearrange("p (q d) -> p q d", q=PAIRS),
                                                  gate_of(c, r, 0)[:, half:NT:2, :].broadcast_to([P, PAIRS, HD]),
                                                  ALU.mult)
                ins.then_inc(c_summed, 1)

            def choose(c, ch):
                p4 = pbar[:, 0, :].rearrange("p (t j k) -> p t j k", t=SEL_T, k=4)
                ch.link(nc.vector.tensor_tensor(imp[:, :, :], p4[:, :, :, 0], p4[:, :, :, 1], ALU.add))
                ch.link(nc.vector.tensor_tensor(imp[:, :, :], imp[:, :, :], p4[:, :, :, 2], ALU.add))
                ch.link(nc.vector.tensor_scalar(tail[:, :, :], p4[:, :, :, 3], 0.5, None, ALU.mult))
                ch.link(nc.vector.scalar_tensor_tensor(out=tail[:, :, :], in0=tail[:, :, :], scalar=TINY, in1=tail[:, :, :],
                                                       op0=ALU.is_ge, op1=ALU.mult))
                ch.link(nc.vector.tensor_tensor(imp[:, :, :], imp[:, :, :], tail[:, :, :], ALU.add))
                ch.link(nc.vector.tensor_tensor(imp[:, :, 1:NSLC], imp[:, :, 1:NSLC], tail[:, :, 0:NSLC - 1], ALU.add))
                ch.link(nc.vector.tensor_tensor(imp[:, :, :], imp[:, :, :], forced[:, :, :], ALU.add))
                for t in range(SEL_T):
                    ins = nc.vector.max(top8[:, t, :], imp[:, t, :])
                ch.link(ins)
                for t in range(SEL_T):
                    ins = nc.vector.match_replace(left[:, t, :], top8[:, t, :], imp[:, t, :], -BIG)
                ch.link(ins)
                nc.vector.tensor_tensor(unsel[:, :, 0:NSLC], left[:, :, :], imp[:, :, :], ALU.is_equal).then_inc(chosen, 1)

            def add_bias(c, n):
                w = len(tiles[n]) * P
                at = score_layout(len(tiles[n]))[0]
                r, br, qt = place(n)
                if n % NT == 0:
                    dve.wait_ge((bf_in, bw_in)[br][r % 2], 32 * c + 16 * (r // 2 + 1))
                after(dve, turned, R * c + before[max(n + 1 - PS, 0)])
                dve.wait_ge(scored, UN * c + (n + 1))
                b = bf[:, r % 2, S - w:S] if br == 0 else bw[:, r % 2, CW - w:CW]
                nc.vector.tensor_tensor_reduce(out=pr[:, n % PS, 0:w], in0=sc[n % 2][:, at:at + w], in1=b,
                                               scale=-1.0, scalar=BIG, op0=ALU.add, op1=ALU.min,
                                               accum_out=nmax[:, br, qt:qt + 1]).then_inc(biased, 1)

            def low_part(c, n):
                for i, run in enumerate(runs[n]):
                    g = before[n] + i
                    dve.wait_ge(t_high, R * c + (g + 1))
                    k = len(run)
                    nc.vector.scalar_tensor_tensor(out=ptl[:, g % GS, 0:k, :], in0=tp[g % TS][:, 0:k, :], scalar=PSCALE,
                                                   in1=pth[:, g % GS, 0:k, :], op0=ALU.mult,
                                                   op1=ALU.subtract).then_inc(t_low, 1)

            def write_out(c, hb, ch):
                r, br = hb // 2, hb % 2
                s = sums[:, r % 2, br, :]
                ch.link(nc.vector.reciprocal(s, s))
                ch.link(nc.vector.tensor_tensor(s.unsqueeze(2), s.unsqueeze(2), gate_of(c, r, br + 1), ALU.mult))
                dve.wait_ge(valued, R * c + before[NT * (hb + 1)])
                ch.link(nc.vector.tensor_tensor(red[:, :, :], ov[hb % 2][:, :].rearrange("p (q d) -> p q d", q=NT),
                                                over_blocks(s), ALU.mult))
                nc.vector.tensor_tensor(y_of(c, r), y_of(c, r), red[:, :, :], ALU.add).then_inc(headed, 1)
                dve.wait_ge(headed, 2 * RC * c + hb + 1)

            for c in range(KV):
                ch = Chain(dve, chain, CH * c)
                stack(c, 0)
                shift(c, 0, ch)
                for r in range(RC):
                    stack(c, r + 1)
                    if r + 1 < RC:
                        shift(c, r + 1, ch)
                    norm(c, r, ch)
                    split_compressed(c, r)
                    write_compressed(c, r)
                stack(c, RC + 1)
                choose(c, ch)
                dve.wait_ge(c_turned, RC * (c + 1))
                for n in range(AHEAD):
                    add_bias(c, n)
                for n in range(UN):
                    if n + AHEAD < UN:
                        add_bias(c, n + AHEAD)
                    low_part(c, n)
                    if n % NT == 2 and n > NT:
                        write_out(c, n // NT - 1, ch)
                write_out(c, UN // NT - 1, ch)
                assert ch.n == CH, ch.n

        @block.tensor
        def _(pe):
            def cmp_scores(c, r):
                pe.wait_ge(stack_ready, LOADS * c + (r + 1))
                if r >= 2:
                    pe.wait_ge(c_shifted, RC * c + (r - 1))
                for qt in range(NT):
                    out = sc[r % 2][:, HD * qt:HD * (qt + 1)]
                    q = qs[:, r, qt * P:(qt + 1) * P]
                    nc.tensor.matmul(out, q, ck[:, 0, :], start=True, stop=False)
                    mm = nc.tensor.matmul(out, q, ck[:, 1, :], start=False, stop=True)
                mm.then_inc(c_scored, 1)

            def cmp_values(c, r):
                pe.wait_ge(c_normed, RC * c + (r + 1))
                if r >= 2:
                    pe.wait_ge(c_low, RC * c + (r - 1))
                for p in range(PAIRS):
                    mm = nc.tensor.transpose(tp[r % 2][:, p, :], pr[:, r % 2, P * p:P * (p + 1)], ident[:, :])
                mm.then_inc(c_turned, 1)
                pe.wait_ge(c_low, RC * c + (r + 1))
                after(pe, c_summed, RC * c + r - 1)
                for half in range(2):
                    for p in range(PAIRS):
                        rows = slice(HD * half, HD * (half + 1))
                        out = ov[half][:, c_cols(r)][:, HD * p:HD * (p + 1)]
                        mm = values_run(nc, out, pth[rows, r % 2, p:p + 1, :], ptl[rows, r % 2, p:p + 1, :], [0],
                                        lambda _: cv[rows, :, :], True, True)
                mm.then_inc(c_valued, 1)

            def scores(c, n):
                r, br, qt = place(n)
                if n == 0:
                    pe.wait_ge(stack_ready, LOADS * (c + 1))
                    pe.wait_ge(c_shifted, RC * (c + 1))
                elif n == 1:
                    pass
                else:
                    pe.wait_ge(biased, UN * c + (n - 1))
                q = qs[:, r, qt * P:(qt + 1) * P]
                first = tiles[n][0]
                masked = br == 0 and qt >= SEL_T
                for at, key, w in score_layout(max(len(tiles[n]), 2))[1]:
                    keys = slice(first * P + key, first * P + key + w)
                    out = sc[n % 2][:, at:at + w]
                    nc.tensor.matmul(out, q, kh[:, br, keys], start=True, stop=False)
                    mm = nc.tensor.matmul(out, q, kl[:, br, keys], start=False, stop=not masked)
                    if masked:
                        rows = slice(32 * (qt - SEL_T), 32 * (qt - SEL_T + 1))
                        mm = nc.tensor.matmul(out, unselT[rows, :], blk[rows, keys], start=False, stop=True)
                mm.then_inc(scored, 1)

            def turn(c, n):
                pe.wait_ge(exped, UN * c + (n + 1))
                for i, run in enumerate(runs[n]):
                    g = before[n] + i
                    after(pe, t_low, R * c + max(g + 1 - TS, 0))
                    transpose_run(pe, nc, tp[g % TS], pr[:, n % PS, :], run, tiles[n][0], ident).then_inc(turned, 1)

            def values(c, n):
                r, br, qt = place(n)
                hb = n // NT
                if n % NT == 0:
                    after(pe, headed, 2 * RC * c + hb - 1)
                for i, run in enumerate(runs[n]):
                    g = before[n] + i
                    pe.wait_ge(t_low, R * c + (g + 1))
                    values_run(nc, ov[hb % 2][:, HD * qt:HD * (qt + 1)], pth[:, g % GS], ptl[:, g % GS], run,
                               lambda kt: v3[:, kt, A_H + KV + KV * br + c, :, :],
                               i == 0, i == len(runs[n]) - 1).then_inc(valued, 1)

            for c in range(KV):
                pe.wait_ge(cmp_copied, 3 * (c + 1))
                after(pe, biased, UN * c)
                after(pe, t_low, R * c)
                after(pe, headed, 2 * RC * c)
                cmp_scores(c, 0)
                for r in range(RC):
                    if r + 1 < RC:
                        cmp_scores(c, r + 1)
                    cmp_values(c, r)
                pe.wait_ge(chosen, c + 1)
                nc.tensor.transpose(tp[0][:, 0, :], unsel[:, :, :].rearrange("p t j -> p (t j)"), ident[:, :]).then_inc(chosen_turned, 1)
                pe.wait_ge(mask_ready, c + 2)
                pe.wait_ge(c_low, RC * (c + 1))
                pe.wait_ge(c_summed, RC * (c + 1))
                for n in range(AHEAD):
                    scores(c, n)
                for n in range(UN):
                    if n + AHEAD < UN:
                        scores(c, n + AHEAD)
                    turn(c, n)
                    if n >= 1:
                        values(c, n - 1)
                values(c, UN - 1)


def out_phase(nc, x, w_out, gate_dram, subln, final_row, out, hT, y, ident, lam_size):
    AW = A_H * HD
    SLABS, W = 4, D // 4
    GS, XS = 2, 4
    with ExitStack() as ctx:
        def sb(name, shape, dt):
            return ctx.enter_context(nc.sbuf_tensor(name, shape, dt))

        def sem(name):
            return ctx.enter_context(nc.semaphore(name))

        raw = hT[:, 0:8, :].rearrange("p (s a) n -> p s (a n)", s=SLABS).rearrange("p s (k n) -> p s k n", k=KT)
        squared = hT[:, 0, :]
        gates, res, fn = hT[:, 8:10, :], hT[:, 10:14, :], hT[:, 14, :]
        wh = sb("o_w_high", [P, KT, D], F32R)
        wl = sb("o_w_low", [P, KT, D], F32R)
        yh = sb("o_yT_high", [P, 2, KT, P], F32R)
        yl = sb("o_yT_low", [P, 2, KT, P], F32R)
        sq = sb("o_squares", [P, AW], F32)
        sub = sb("o_subln", [P, HD], F32)
        small = sb("o_small", [P, 4], F32)
        arms = sb("o_a_rstd", [P, NT, A_H], F32)
        ss = sb("o_square_sums", [P, NT], F32)
        rs = sb("o_rstd", [P, NT], F32)
        tp = [ctx.enter_context(nc.psum_tensor(f"o_turned{i}", [P, 4, P], F32)) for i in range(2)]
        acc = [ctx.enter_context(nc.psum_tensor(f"o_acc{i}", [P, 512], F32)) for i in range(4)]

        row_in = sem("o_rows_in")
        w_in = [sem(f"o_w_in{i}") for i in range(SLABS)]
        g_in = [sem(f"o_gates_in{i}") for i in range(GS)]
        x_in = [sem(f"o_x_in{i}") for i in range(XS)]
        w_high, w_low = sem("o_w_high_done"), sem("o_w_low_done")
        small_ready, a_summed, a_root, a_chain, gated = sem("o_small_ready"), sem("o_a_summed"), sem("o_a_root"), sem("o_a_chain"), sem("o_gated")
        turned, high, low = sem("o_turned"), sem("o_high"), sem("o_low")
        done, added, squares, roots, r_chain, normed = sem("o_done"), sem("o_added"), sem("o_squares_summed"), sem("o_roots"), sem("o_root_chain"), sem("o_normed")
        stored = [sem(f"o_stored{i}") for i in range(XS)]
        block = ctx.enter_context(nc.Block())

        @block.sync
        def _(sp):
            sp.dma_start(fn, final_row.partition_broadcast(P)).then_inc(row_in, 16)
            sp.dma_start(sub[:, :], subln.partition_broadcast(P)).then_inc(row_in, 16)

            def load_gates(i):
                if i >= GS:
                    sp.wait_ge(gated, i + 1 - GS)
                sp.dma_start(gates[:, i % GS, :], gate_dram[i * P:(i + 1) * P, :]).then_inc(g_in[i % GS], 16)

            def load_x(i):
                if i >= XS:
                    sp.wait_ge(stored[i % XS], 16 * (i // XS))
                sp.dma_start(res[:, i % XS, :], x[i * P:(i + 1) * P, :]).then_inc(x_in[i % XS], 16)

            load_gates(0)
            for s in range(SLABS):
                sp.dma_start(raw[:, s], w_out[s]).then_inc(w_in[s], 16)
            load_gates(1)
            load_x(0)
            load_x(1)
            for i in range(NT):
                if i + GS < NT:
                    load_gates(i + GS)
                if i + 2 < NT:
                    load_x(i + 2)
                sp.wait_ge(normed, i + 1)
                sp.dma_start(out[i * P:(i + 1) * P, :], res[:, i % XS, :]).then_inc(stored[i % XS], 16)
            for i in range(XS):
                sp.wait_ge(stored[i], 16 * (NT // XS))

        @block.scalar
        def _(act):
            act.wait_ge(small_ready, 1)

            def a_rstd(i):
                act.wait_ge(a_summed, i + 1)
                nc.scalar.activation(arms[:, i, :], arms[:, i, :], ACT.Sqrt, scale=small[:, 1:2],
                                     bias=small[:, 2:3]).then_inc(a_root, 1)

            def high_part(i):
                for h in range(2):
                    act.wait_ge(turned, 2 * i + h + 1)
                    if i >= 2 and h == 0:
                        act.wait_ge(done, 2 * i - 2)
                    nc.scalar.copy(yh[:, i % 2, 4 * h:4 * h + 4, :], tp[h][:, :, :]).then_inc(high, 1)

            def square(i):
                act.wait_ge(added, 2 * i + 2)
                if i == 0:
                    act.wait_ge(w_low, 1)
                nc.scalar.activation(squared, res[:, i % XS, :], ACT.Square, accum_out=ss[:, i:i + 1]).then_inc(squares, 1)
                act.wait_ge(squares, i + 1)
                nc.scalar.activation(rs[:, i:i + 1], ss[:, i:i + 1], ACT.Sqrt, scale=1.0 / D, bias=small[:, 2:3]).then_inc(roots, 1)

            a_rstd(0)
            for s in range(SLABS):
                act.wait_ge(w_in[s], 16)
                nc.scalar.copy(wh[:, :, s * W:(s + 1) * W], raw[:, s]).then_inc(w_high, 1)
                if s == 0:
                    high_part(0)
            a_rstd(1)
            for i in range(NT):
                if i + 2 < NT:
                    a_rstd(i + 2)
                if i + 1 < NT:
                    high_part(i + 1)
                square(i)

        @block.vector
        def _(dve):
            sc = Chain(dve, a_chain)
            sc.link(nc.vector.tensor_scalar(small[:, 0:1], lam_size[:, :], 1.0 / PSCALE, None, ALU.mult))
            sc.link(nc.vector.tensor_tensor(small[:, 1:2], small[:, 0:1], small[:, 0:1], ALU.mult))
            sc.link(nc.vector.tensor_scalar(small[:, 1:2], small[:, 1:2], 1.0 / HD, None, ALU.mult))
            sc.link(nc.vector.tensor_scalar(small[:, 3:4], small[:, 0:1], 1.0 - LAM_INIT, None, ALU.mult))
            nc.vector.memset(small[:, 2:3], EPS).then_inc(small_ready, 1)
            dve.wait_ge(row_in, 32)
            by_head = lambda t: t.rearrange("p (h d) -> p h d", d=HD)

            def a_squares(i):
                ya = y[:, i, 0:AW]
                sc.link(nc.vector.tensor_tensor(sq[:, :], ya, ya, ALU.mult))
                nc.vector.tensor_reduce(arms[:, i, :], by_head(sq[:, :]), AX.X, ALU.add).then_inc(a_summed, 1)

            def gate(i):
                ya = by_head(y[:, i, 0:AW])
                dve.wait_ge(a_root, i + 1)
                sc.link(nc.vector.reciprocal(arms[:, i, :], arms[:, i, :]))
                sc.link(nc.vector.tensor_scalar(arms[:, i, :], arms[:, i, :], small[:, 3:4], None, ALU.mult))
                sc.link(nc.vector.tensor_tensor(ya, ya, arms[:, i, :].unsqueeze(2).broadcast_to([P, A_H, HD]), ALU.mult))
                sc.link(nc.vector.tensor_tensor(ya, ya, sub[:, :].unsqueeze(1).broadcast_to([P, A_H, HD]), ALU.mult))
                dve.wait_ge(g_in[i % GS], 16 * (i // GS + 1))
                nc.vector.tensor_tensor(y[:, i, :], y[:, i, :], gates[:, i % GS, :], ALU.mult).then_inc(gated, 1)

            def low_part(i):
                for h in range(2):
                    dve.wait_ge(high, 2 * i + h + 1)
                    ks = slice(4 * h, 4 * h + 4)
                    nc.vector.tensor_tensor(yl[:, i % 2, ks, :], tp[h][:, :, :], yh[:, i % 2, ks, :].bitcast(F32),
                                            ALU.subtract).then_inc(low, 1)

            def residual(i):
                for h in range(2):
                    n = 2 * i + h
                    dve.wait_ge(done, n + 1)
                    if h == 0:
                        dve.wait_ge(x_in[i % XS], 16 * (i // XS + 1))
                    cols = slice(512 * h, 512 * h + 512)
                    nc.vector.tensor_tensor(res[:, i % XS, cols], acc[n % 4][:, :], res[:, i % XS, cols], ALU.add).then_inc(added, 1)

            def normalise(i):
                dve.wait_ge(roots, i + 1)
                nc.vector.reciprocal(rs[:, i:i + 1], rs[:, i:i + 1]).then_inc(r_chain, 1)
                dve.wait_ge(r_chain, i + 1)
                nc.vector.scalar_tensor_tensor(out=res[:, i % XS, :], in0=res[:, i % XS, :], scalar=rs[:, i:i + 1], in1=fn,
                                               op0=ALU.mult, op1=ALU.mult).then_inc(normed, 1)

            a_squares(0)
            gate(0)
            for s in range(SLABS):
                dve.wait_ge(w_high, s + 1)
                cols = slice(s * W, (s + 1) * W)
                nc.vector.tensor_tensor(wl[:, :, cols], raw[:, s], wh[:, :, cols].bitcast(F32), ALU.subtract).then_inc(w_low, 1)
                if s == 0:
                    low_part(0)
            a_squares(1)
            gate(1)
            for i in range(NT):
                if i + 2 < NT:
                    a_squares(i + 2)
                    gate(i + 2)
                if i + 1 < NT:
                    low_part(i + 1)
                residual(i)
                normalise(i)

        @block.tensor
        def _(pe):
            def turn(i):
                pe.wait_ge(gated, i + 1)
                for h in range(2):
                    if i >= 1:
                        pe.wait_ge(low, 2 * i + h - 1)
                    for k in range(4):
                        mm = nc.tensor.transpose(tp[h][:, k, :], y[:, i, (4 * h + k) * P:(4 * h + k + 1) * P], ident[:, :])
                    mm.then_inc(turned, 1)

            def project(i):
                pe.wait_ge(low, 2 * i + 2)
                for h in range(2):
                    n = 2 * i + h
                    if n >= 4:
                        pe.wait_ge(added, n - 3)
                    if i == 0:
                        pe.wait_ge(w_low, SLABS // 2 * (h + 1))
                    cols = slice(512 * h, 512 * h + 512)
                    for k in range(KT):
                        nc.tensor.matmul(acc[n % 4][:, :], yh[:, i % 2, k, :], wh[:, k, cols], start=(k == 0), stop=False)
                        nc.tensor.matmul(acc[n % 4][:, :], yh[:, i % 2, k, :], wl[:, k, cols], start=False, stop=False)
                        mm = nc.tensor.matmul(acc[n % 4][:, :], yl[:, i % 2, k, :], wh[:, k, cols], start=False,
                                              stop=(k == KT - 1))
                    mm.then_inc(done, 1)

            turn(0)
            for i in range(NT):
                if i + 1 < NT:
                    turn(i + 1)
                project(i)


def decoder_trunk(nc, x, norm_row, w_feat, w_val, w_gate, w_out, lams, subln, sinks, pe_pairs, cmp_w1, cmp_w2k,
                  cmp_w2v, final_row, identity, bias_full, bias_win, bias_swa, bias_cmp, row_valid, force, blocks, out):
    gate_dram = nc.dram_tensor("silu_gates", (S, D), F32, kind="Internal").ap()
    with ExitStack() as ctx:
        def sb(name, shape, dt):
            return ctx.enter_context(nc.sbuf_tensor(name, shape, dt))

        ident = sb("identity", [P, P], F32)
        glog = sb("gate_logits", [P, NT, 3 * C_H], F32)
        kch = sb("cmp_keys_high", [P, KV, HD], F32R)
        kcl = sb("cmp_keys_low", [P, KV, HD], F32R)
        vc3 = sb("cmp_values", [P, KV, 3, HD], BF16)
        lam_size = sb("lam_size", [P, 1], F32)
        hT = sb("features", [P, TC, S], F32)
        with ExitStack() as attention:
            v3 = attention.enter_context(nc.sbuf_tensor("values", [P, NT, VH, 3, HD], BF16))
            load_identity(nc, ident, identity)
            with ExitStack() as projection:
                def proj(name, shape, dt):
                    return projection.enter_context(nc.sbuf_tensor(name, shape, dt))

                xh = proj("xT_high", [P, KT, S], F32R)
                xl = proj("xT_low", [P, KT, S], F32R)
                wr = proj("w_raw", [P, 4, KT * P], F32)
                wh = proj("w_high", [P, 4, KT * P], F32R)
                wl = proj("w_low", [P, 4, KT * P], F32R)
                norm_phase(nc, x, norm_row, ident, hT, xh, xl)
                values_phase(nc, w_val, w_gate, gate_dram, hT, xh, xl, wr, wh, wl, v3, glog)
                queries_phase(nc, w_feat, hT, xh, xl, wr, wh, wl)
            y = attention.enter_context(nc.sbuf_tensor("branches", [P, NT, D], F32))
            diff_phase(nc, hT, v3, y, ident, bias_full, lams, lam_size)
            swa_phase(nc, hT, v3, y, ident, bias_swa, sinks)
            compress_phase(nc, hT, cmp_w1, cmp_w2k, cmp_w2v, pe_pairs, kch, kcl, vc3)
            nsa_phase(nc, hT, v3, y, ident, kch, kcl, vc3, glog, bias_full, bias_win, bias_cmp, row_valid, force, blocks)
            out_phase(nc, x, w_out, gate_dram, subln, final_row, out, hT, y, ident, lam_size)


def load_identity(nc, ident, identity):
    with nc.semaphore("identity_in") as loaded, nc.Block() as block:
        @block.sync
        def _(sp):
            sp.dma_start(ident[:, :], identity).then_inc(loaded, 16)
            sp.wait_ge(loaded, 16)


def _columns():
    r = np.arange
    qa, ka, va, ga, qb, kb, vb, gb = 0, 256, 512, 768, 1024, 1280, 1408, 1536
    qc, kc, vc, ks, vs, kw, vw, gl, gc = 1792, 2304, 2432, 2560, 2688, 2816, 2944, 3072, 3096
    feat = [r(qa, qa + 128), r(qa + 128, qa + 256), r(ka, ka + 128), r(ka + 128, ka + 256)]
    feat += [r(qb + 128 * g, qb + 128 * g + 128) for g in range(KV)]
    feat += [np.r_[kb + 64 * g:kb + 64 * g + 64, ks + 64 * g:ks + 64 * g + 64] for g in range(KV)]
    feat += [np.r_[kw + 64 * g:kw + 64 * g + 64, kc + 64 * g:kc + 64 * g + 64] for g in range(KV)]
    feat += [r(qc + 128 * c, qc + 128 * c + 128) for c in range(4)] + [r(vc, vc + 128)]
    val = [r(va, va + 256), np.r_[vb:vb + 128, vs:vs + 128], np.r_[vw:vw + 128, gl:gl + 24, gl:gl + 24, gl:gl + 24, gl:gl + 24, gl:gl + 24, gl:gl + 8]]
    gate = [r(ga, ga + 256), r(gb, gb + 256), r(gc, gc + 256), r(gc + 256, gc + 512)]
    return feat, val, gate


def _constants():
    f32 = np.float32
    q = np.arange(P)[:, None]
    t = np.arange(S).reshape(NT, P).T[:, :, None]

    def bias(slope, dist, valid):
        return np.where(valid, -slope * dist, NEG).astype(f32)

    slopes8 = 2.0 ** -np.arange(1, C_H + 1)
    slopes4 = 2.0 ** (-2.0 * np.arange(1, B_H + 1))
    d = q + (S - P) - np.arange(S)[None]
    full = np.stack([bias(s, d, d >= 0) for s in slopes8])
    d = q + (CW - P) - np.arange(CW)[None]
    win = np.stack([bias(s, d, (d >= 0) & (d < 512)) for s in slopes8])
    d = q + (BW - P) - np.arange(BW)[None]
    swa = np.stack([bias(s, d, (d >= 0) & (d < 128)) for s in slopes4]).reshape(KV, 2, P, BW).transpose(0, 2, 1, 3)
    block = np.arange(HD)[None, None]
    d = t - (16 * block + 31)
    cmp = np.stack([bias(s, d, (d >= 0) & (block < NCMP)) for s in slopes8]).reshape(C_H, P, NT * HD)
    row_valid = (t[:, :, 0] >= 31).astype(f32)
    cur = t[:, SEL_T:] // 64
    j = np.arange(NSLC)[None, None]
    force = np.where(j > cur, NEG, np.where((j == 0) | (j == cur) | (j == cur - 1), -NEG, 0)).astype(f32)
    blocks = np.zeros((SEL_T, 32, S), f32)
    for b in range(NSLC):
        blocks[:, b, 64 * b:64 * b + 64] = NEG
    blocks = blocks.reshape(P, S)
    return {"identity": np.eye(P, dtype=f32), "bias_full": full, "bias_win": win, "bias_swa": swa, "bias_cmp": cmp,
            "row_valid": row_valid, "force": force, "blocks": blocks}


def _slab(w, columns):
    w = w if columns is None else w[:, columns]
    return w.reshape(KT, P, w.shape[1]).transpose(1, 0, 2)


def kernel(x, norm_w, w_in, w_out, diff_lq1, diff_lk1, diff_lq2, diff_lk2, diff_subln, sinks, cmp_pe_k, cmp_pe_v,
           cmp_wk1, cmp_wk2, cmp_wv1, cmp_wv2, final_norm):
    import concourse.bacc as bacc
    from concourse.bass_utils import run_bass_kernel_spmd

    feat, val, gate = _columns()
    w = w_in[0]
    pairs = lambda a: a.reshape(CPL, P, -1).transpose(1, 0, 2)
    arrays = {
        "x": x[0], "norm_row": norm_w,
        "w_feat": np.stack([_slab(w, c) for c in feat]),
        "w_val": np.stack([_slab(w, c) for c in val]),
        "w_gate": np.stack([_slab(w, c) for c in gate]),
        "w_out": np.stack([_slab(w_out[0][:, 256 * s:256 * s + 256], None) for s in range(4)]),
        "lams": np.concatenate([diff_lq1, diff_lk1, diff_lq2, diff_lk2]),
        "subln": diff_subln, "sinks": sinks.reshape(KV, 1, B_H // KV),
        "pe_pairs": np.stack([cmp_pe_k[0].reshape(CPL, P).T, cmp_pe_v[0].reshape(CPL, P).T], axis=1),
        "cmp_w1": np.stack([pairs(cmp_wk1[0]), pairs(cmp_wv1[0])], axis=1),
        "cmp_w2k": np.concatenate([cmp_wk2[0], cmp_wk2[0]], axis=1), "cmp_w2v": cmp_wv2[0],
        "final_row": final_norm.reshape(1, D),
    }
    arrays.update(_constants())
    arrays = {k: np.ascontiguousarray(v) for k, v in arrays.items()}
    nc = bacc.Bacc("TRN2", target_bir_lowering=False, num_devices=1)
    args = {k: nc.dram_tensor(f"in_{k}", v.shape, mybir.dt.from_np(v.dtype), kind="ExternalInput").ap() for k, v in arrays.items()}
    out = nc.dram_tensor("out", (S, D), F32, kind="ExternalOutput").ap()
    decoder_trunk(nc, **args, out=out)
    r = run_bass_kernel_spmd(nc, [{f"in_{k}": v for k, v in arrays.items()}], core_ids=[0])
    return r.results[0]["out"].reshape(1, S, D)
```

```python
from contextlib import ExitStack

import numpy as np

import concourse.bass as bass
from concourse import mybir

F32 = mybir.dt.float32
F32R = mybir.dt.float32r
F16 = mybir.dt.float16
BF16 = mybir.dt.bfloat16
ALU = mybir.AluOpType
ACT = mybir.ActivationFunctionType
AX = mybir.AxisListType

P = 128
D = 1024
S = 1024
KT = D // P
NT = S // P
HD = 64
A_QK = 32
EPS = 1e-6
NEG = -1e30
BIG = 3e38
TINY = 2.0 ** -126
PSCALE = 2.0 ** 14
A_H, B_H, C_H, KV = 4, 4, 8, 2
RC = C_H // KV
TC = 15
VH = A_H + 3 * KV
LAM_INIT = 0.2
QT_ORDER = (7, 3, 6, 2, 5, 1, 4, 0)
OUT_SLABS = (0, 4, 6, 8)
CW = 640
BW = 256
NCMP = 63
SEL_T = 4
NSLC = 16
CPL = 16


def score_layout(n_tiles):
    w = n_tiles * P
    if w <= 512:
        return 0, [(0, 0, w)]
    at = P if w == 640 else 0
    return at, [(at, 0, 512 - at), (512, 512 - at, w - 512 + at)]


def chunks_of(tiles):
    return [tiles[i:i + 4] for i in range(0, len(tiles), 4)]


def projection_phase(nc, x, norm_row, identity, w_val, w_gate, w_feat, gate_dram, ident, hT, xh, xl, wr, wh, wl, v3, glog):
    xin, xs, nw, junk = hT[:, 0:4, :], hT[:, 4:6, :], hT[:, 6, :], hT[:, 7, :]
    rest = hT[:, 12, 0:512].rearrange("p (s n) -> p s n", s=2)
    e = hT[:, 13, 0:512].rearrange("p (s n) -> p s n", s=2)
    sg = hT[:, 14, :].rearrange("p (s n) -> p s n", s=4)
    XS = 4
    NV, NS, W = 3, 3 + 4, 256
    U = 3
    TURNS = TC // U
    with ExitStack() as ctx:
        def sb(name, shape):
            return ctx.enter_context(nc.sbuf_tensor(name, shape, F32))

        def sem(name):
            return ctx.enter_context(nc.semaphore(name))

        ss, rs, ms, nt = sb("x_square_sums", [P, NT]), sb("x_rstd", [P, NT]), sb("x_mean_squares", [P, NT]), sb("x_newton", [P, NT])
        epsc = sb("norm_eps", [P, 1])
        nat = [ctx.enter_context(nc.psum_tensor(f"nat{i}", [P, 512], F32)) for i in range(4)]
        tp = [ctx.enter_context(nc.psum_tensor(f"x_transposed{i}", [P, 512], F32)) for i in range(4)]
        feat = tp + nat[0:2]
        rows_in, eps_set = sem("identity_and_norm_row_in"), sem("eps_set")
        x_in = [sem(f"x_in{i}") for i in range(XS)]
        squares, roots, inverted, scaled = sem("squares_summed"), sem("roots_taken"), sem("roots_inverted"), sem("x_scaled")
        turned, x_high, x_low = sem("x_turned"), sem("x_high_written"), sem("x_low_written")
        w_in = [sem(f"slab_in{i}") for i in range(2)]
        high, low, done = sem("slab_high"), sem("slab_low"), sem("nat_done")
        v_first, v_rest, v_second, v_third = sem("v_first_part"), sem("v_rest"), sem("v_second_part"), sem("v_third_part")
        glog_copied, g_exp, g_chain, g_ready = sem("gate_logits_copied"), sem("gate_exp"), sem("gate_chain"), sem("gate_ready")
        g_out = [sem(f"gate_out{i}") for i in range(4)]
        f_in = [sem(f"chunk_in{i}") for i in range(U)]
        f_high, f_low, f_done = sem("chunk_high"), sem("chunk_low"), sem("feat_done")
        left, right = sem("feat_left_copied"), sem("feat_right_copied")
        block = ctx.enter_context(nc.Block())

        def slab(t, s):
            return t[:, 2 * (s % 2):2 * (s % 2) + 2, :].rearrange("p a n -> p (a n)").rearrange("p (k n) -> p k n", k=KT)

        def chunk(t, j):
            return t[:, (j + 2) % 4, :].rearrange("p (k n) -> p k n", k=KT)

        def heads(s):
            return 4 if s < 2 else 2

        def by_head(t, s):
            return t[:, 0:heads(s) * HD].rearrange("p (h d) -> p h d", d=HD)

        def bank(i, h):
            return tp[(2 * i + h) % 4][:, :].rearrange("p (k n) -> p k n", k=4)

        @block.sync
        def _(sp):
            def load_x(i):
                if i >= XS:
                    sp.wait_ge(scaled, i + 1 - XS)
                sp.dma_start(xin[:, i % XS, :], x[i * P:(i + 1) * P, :]).then_inc(x_in[i % XS], 16)

            def load_slab(s):
                if s >= 2:
                    sp.wait_ge(low, s - 1)
                src = w_val[s] if s < NV else w_gate[s - NV]
                sp.dma_start(slab(wr, s), src).then_inc(w_in[s % 2], 16)

            def store(s):
                for i in range(NT):
                    n = (s - NV) * NT + i
                    sp.wait_ge(g_ready, n + 1)
                    sp.dma_start(gate_dram[i * P:(i + 1) * P, (s - NV) * W:(s - NV + 1) * W],
                                 sg[:, n % 4, :]).then_inc(g_out[n % 4], 16)

            load_x(0)
            sp.dma_start(nw, norm_row.partition_broadcast(P)).then_inc(rows_in, 16)
            sp.dma_start(ident[:, :], identity).then_inc(rows_in, 16)
            load_x(1)
            load_slab(0)
            load_x(2)
            load_x(3)
            load_slab(1)
            for i in range(XS, NT):
                load_x(i)
            for s in range(2, NS):
                load_slab(s)
            for s in range(NV, NS):
                store(s)
                if s == NV:
                    for j in range(2):
                        sp.wait_ge(low, NS - 1)
                        sp.dma_start(chunk(wr, j), w_feat[j]).then_inc(f_in[j], 16)
                if s == NV + 1:
                    sp.wait_ge(low, NS)
                    sp.dma_start(chunk(wr, 2), w_feat[2]).then_inc(f_in[2], 16)
            for i in range(4):
                sp.wait_ge(g_out[i], 16 * (NS - NV) * NT // 4)
            with sp.Fori(0, TURNS - 1) as it:
                for j in range(U):
                    sp.wait_ge(f_low, U * it + j + 1)
                    sp.dma_start(chunk(wr, j), w_feat[U * it + (j + U)]).then_inc(f_in[j], 16)

        @block.scalar
        def _(act):
            def x_high_part(i):
                for h in range(2):
                    act.wait_ge(turned, 2 * i + h + 1)
                    nc.scalar.copy(xh[:, 4 * h:4 * h + 4, i * P:(i + 1) * P], bank(i, h)).then_inc(x_high, 1)

            def root(i):
                act.wait_ge(x_in[i % XS], 16 * (i // XS + 1))
                nc.scalar.activation(junk, xin[:, i % XS, :], ACT.Square, accum_out=ss[:, i:i + 1]).then_inc(squares, 1)
                act.wait_ge(squares, i + 1)
                nc.scalar.activation(rs[:, i:i + 1], ss[:, i:i + 1], ACT.Sqrt, scale=1.0 / D,
                                     bias=epsc[:, 0:1]).then_inc(roots, 1)

            def split(s):
                act.wait_ge(w_in[s % 2], 16 * (s // 2 + 1))
                if s >= 2:
                    act.wait_ge(done, NT * (s - 1))
                nc.scalar.copy(slab(wh, s), slab(wr, s)).then_inc(high, 1)

            def split_chunk(j):
                nc.scalar.copy(chunk(wh, j), chunk(wr, j)).then_inc(f_high, 1)

            def first_chunk(j):
                act.wait_ge(f_in[j], 16)
                act.wait_ge(done, NT * (NS - 1) if j < 2 else NT * NS)
                split_chunk(j)

            def first_part(n):
                s, i = n // NT, n % NT
                act.wait_ge(done, n + 1)
                nc.scalar.copy(v3[:, i, 4 * s:4 * s + heads(s), 0, :], by_head(nat[n % 4], s)).then_inc(v_first, 1)

            def gate_exp(n):
                m = n - NV * NT
                act.wait_ge(done, n + 1)
                if m >= 2:
                    act.wait_ge(g_ready, m - 1)
                nc.scalar.activation(e[:, n % 2, :], nat[n % 4][:, 0:W], ACT.Exp, scale=-1.0).then_inc(g_exp, 1)

            def evacuate(it, j):
                act.wait_ge(f_done, 2 * U * it + (2 * j + 1))
                nc.scalar.copy(hT[:, U * it + j, 0:512], feat[2 * j][:, :]).then_inc(left, 1)

            act.wait_ge(eps_set, 1)
            root(0)
            root(1)
            for i in range(NT):
                x_high_part(i)
                if i == 0:
                    split(0)
                if i == 2:
                    split(1)
                if i + 2 < NT:
                    root(i + 2)
                if i >= 1:
                    first_part(i - 1)
            first_part(NT - 1)
            split(2)
            for s in range(1, NS):
                for i in range(NT):
                    if s < NV:
                        first_part(s * NT + i)
                    else:
                        gate_exp(s * NT + i)
                if s + 2 < NS:
                    split(s + 2)
                elif s == NS - 2:
                    first_chunk(0)
                    first_chunk(1)
            first_chunk(2)
            act.wait_ge(v_third, NV * NT)
            act.wait_ge(g_ready, (NS - NV) * NT)
            with act.Fori(0, TURNS - 1) as it:
                for j in range(U):
                    evacuate(it, j)
                    act.wait_ge(f_in[j], 16 * it + 32)
                    act.wait_ge(f_done, 2 * U * it + (2 * j + 2))
                    split_chunk(j)
            for j in range(U):
                evacuate(TURNS - 1, j)

        @block.vector
        def _(dve):
            steps = Chain(dve, inverted)
            gates = Chain(dve, g_chain)

            def x_low_part(i):
                for h in range(2):
                    dve.wait_ge(x_high, 2 * i + h + 1)
                    nc.vector.tensor_tensor(xl[:, 4 * h:4 * h + 4, i * P:(i + 1) * P], bank(i, h),
                                            xh[:, 4 * h:4 * h + 4, i * P:(i + 1) * P].bitcast(F32),
                                            ALU.subtract).then_inc(x_low, 1)

            def scale_x(i):
                dve.wait_ge(roots, i + 1)
                r, v, t = rs[:, i:i + 1], ms[:, i:i + 1], nt[:, i:i + 1]
                steps.link(nc.vector.tensor_scalar(v, ss[:, i:i + 1], 1.0 / D, EPS, ALU.mult, ALU.add))
                steps.link(nc.vector.reciprocal(r, r))
                steps.link(nc.vector.tensor_tensor(t, r, r, ALU.mult))
                steps.link(nc.vector.tensor_tensor(t, t, v, ALU.mult))
                steps.link(nc.vector.tensor_scalar(t, t, -0.5, 1.5, ALU.mult, ALU.add))
                steps.link(nc.vector.tensor_tensor(r, r, t, ALU.mult))
                if i >= 2:
                    dve.wait_ge(turned, 2 * i - 2)
                nc.vector.scalar_tensor_tensor(out=xs[:, i % 2, :], in0=xin[:, i % XS, :], scalar=rs[:, i:i + 1],
                                               in1=nw, op0=ALU.mult, op1=ALU.mult).then_inc(scaled, 1)

            def split(s):
                dve.wait_ge(high, s + 1)
                nc.vector.tensor_tensor(slab(wl, s), slab(wr, s), slab(wh, s).bitcast(F32), ALU.subtract).then_inc(low, 1)

            def split_chunk(it, j):
                dve.wait_ge(f_high, U * it + (j + 1))
                nc.vector.tensor_tensor(chunk(wl, j), chunk(wr, j), chunk(wh, j).bitcast(F32),
                                        ALU.subtract).then_inc(f_low, 1)

            def value_rest(n):
                s, i = n // NT, n % NT
                dve.wait_ge(v_first, n + 1)
                if n >= 2:
                    dve.wait_ge(v_third, n - 1)
                nc.vector.tensor_tensor(by_head(rest[:, n % 2, :], s), by_head(nat[n % 4], s),
                                        v3[:, i, 4 * s:4 * s + heads(s), 0, :], ALU.subtract).then_inc(v_rest, 1)
                if s == 2:
                    nc.vector.tensor_copy(glog[:, i, :], nat[n % 4][:, P:P + 3 * C_H]).then_inc(glog_copied, 1)

            def silu(n):
                m = n - NV * NT
                dve.wait_ge(g_exp, m + 1)
                gates.link(nc.vector.tensor_scalar(e[:, n % 2, :], e[:, n % 2, :], 1.0, None, ALU.add))
                gates.link(nc.vector.reciprocal(e[:, n % 2, :], e[:, n % 2, :]))
                if m >= 4:
                    dve.wait_ge(g_out[n % 4], 16 * (m // 4))
                nc.vector.tensor_tensor(sg[:, n % 4, :], nat[n % 4][:, 0:W], e[:, n % 2, :], ALU.mult).then_inc(g_ready, 1)

            def evacuate(it, j):
                dve.wait_ge(f_done, 2 * U * it + (2 * j + 2))
                nc.vector.tensor_copy(hT[:, U * it + j, 512:1024], feat[2 * j + 1][:, :]).then_inc(right, 1)

            nc.vector.memset(epsc[:, :], EPS).then_inc(eps_set, 1)
            dve.wait_ge(rows_in, 32)
            scale_x(0)
            for i in range(NT):
                if i + 1 < NT:
                    scale_x(i + 1)
                x_low_part(i)
                if i == 0:
                    split(0)
                if i == 2:
                    split(1)
                if i >= 1:
                    value_rest(i - 1)
            value_rest(NT - 1)
            split(2)
            for s in range(1, NS):
                for i in range(NT):
                    if s < NV:
                        value_rest(s * NT + i)
                    else:
                        silu(s * NT + i)
                if s + 2 < NS:
                    split(s + 2)
                elif s == NS - 2:
                    split_chunk(0, 0)
                    split_chunk(0, 1)
            split_chunk(0, 2)
            dve.wait_ge(v_third, NV * NT)
            with dve.Fori(0, TURNS - 1) as it:
                for j in range(U):
                    evacuate(it, j)
                    split_chunk(it + 1, j)
            for j in range(U):
                evacuate(TURNS - 1, j)

        @block.gpsimd
        def _(pool):
            for n in range(NV * NT):
                s, i = n // NT, n % NT
                r = by_head(rest[:, n % 2, :], s)
                vh = v3[:, i, 4 * s:4 * s + heads(s), :, :]
                pool.wait_ge(v_rest, n + 1)
                nc.gpsimd.tensor_copy(vh[:, :, 1, :], r).then_inc(v_second, 1)
                pool.wait_ge(v_second, n + 1)
                nc.gpsimd.tensor_tensor(vh[:, :, 2, :], r, vh[:, :, 1, :], ALU.subtract).then_inc(v_third, 1)

        @block.tensor
        def _(pe):
            def turn(i):
                pe.wait_ge(scaled, i + 1)
                for h in range(2):
                    if i >= 2:
                        pe.wait_ge(x_low, 2 * i + h - 3)
                    for k in range(4):
                        mm = nc.tensor.transpose(bank(i, h)[:, k, :],
                                                 xs[:, i % 2, (4 * h + k) * P:(4 * h + k + 1) * P], ident[:, :])
                    mm.then_inc(turned, 1)

            def natural(n):
                s, i = n // NT, n % NT
                a, b = slab(wh, s), slab(wl, s)
                cols = W if s != 2 else 192
                m = n - 4
                if 0 <= m < NV * NT:
                    pe.wait_ge(v_rest, m + 1)
                    if m >= 2 * NT:
                        pe.wait_ge(glog_copied, m - 2 * NT + 1)
                elif m >= NV * NT:
                    pe.wait_ge(g_ready, m - NV * NT + 1)
                rows = slice(i * P, (i + 1) * P)
                for k in range(KT):
                    nc.tensor.matmul(nat[n % 4][:, 0:cols], xh[:, k, rows], a[:, k, 0:cols], start=(k == 0), stop=False)
                    nc.tensor.matmul(nat[n % 4][:, 0:cols], xh[:, k, rows], b[:, k, 0:cols], start=False, stop=False)
                    mm = nc.tensor.matmul(nat[n % 4][:, 0:cols], xl[:, k, rows], a[:, k, 0:cols],
                                          start=False, stop=(k == KT - 1))
                mm.then_inc(done, 1)

            def features(it, j, first):
                pe.wait_ge(f_low, U * it + (j + 1))
                a, b = chunk(wh, j), chunk(wl, j)
                for h, copied in ((0, left), (1, right)):
                    if not first:
                        pe.wait_ge(copied, U * it + (j + 1 - U))
                    cols = slice(512 * h, 512 * h + 512)
                    for k in range(KT):
                        nc.tensor.matmul(feat[2 * j + h][:, :], a[:, k, :], xh[:, k, cols], start=(k == 0), stop=False)
                        nc.tensor.matmul(feat[2 * j + h][:, :], a[:, k, :], xl[:, k, cols], start=False, stop=False)
                        mm = nc.tensor.matmul(feat[2 * j + h][:, :], b[:, k, :], xh[:, k, cols],
                                              start=False, stop=(k == KT - 1))
                    mm.then_inc(f_done, 1)

            pe.wait_ge(rows_in, 32)
            turn(0)
            for i in range(NT):
                if i + 1 < NT:
                    turn(i + 1)
                pe.wait_ge(x_low, 2 * i + 2)
                if i == 0:
                    pe.wait_ge(low, 1)
                natural(i)
            for s in range(1, NS):
                pe.wait_ge(low, s + 1)
                for i in range(NT):
                    natural(s * NT + i)
            for j in range(U):
                if j == 2:
                    pe.wait_ge(g_ready, (NS - NV) * NT)
                features(0, j, True)
            with pe.Fori(1, TURNS) as it:
                for j in range(U):
                    features(it, j, False)


class Chain:

    def __init__(self, eng, sem, start=0):
        self.eng, self.sem, self.start, self.n = eng, sem, start, 0

    def link(self, ins):
        ins.then_inc(self.sem, 1)
        self.n += 1
        self.eng.wait_ge(self.sem, self.start + self.n)


def softmax_chunks(tiles_of_unit):
    runs = [chunks_of(t) for t in tiles_of_unit]
    before = [0]
    for r in runs:
        before.append(before[-1] + len(r))
    return runs, before


def transpose_run(pe, nc, dst, src, run, first, ident):
    for j, kt in enumerate(run):
        c = (kt - first) * P
        mm = nc.tensor.transpose(dst[:, j, :], src[:, c:c + P], ident[:, :])
    return mm


def values_run(nc, out, ph, pl, run, v_of_tile, opens, closes):
    for j, kt in enumerate(run):
        v = v_of_tile(kt)
        for part in range(3):
            nc.tensor.matmul(out, ph[:, j, :], v[:, part, :], start=(opens and j == 0 and part == 0), stop=False)
        nc.tensor.matmul(out, pl[:, j, :], v[:, 0, :], start=False, stop=False)
        mm = nc.tensor.matmul(out, pl[:, j, :], v[:, 1, :], start=False, stop=(closes and j == len(run) - 1))
    return mm


def diff_phase(nc, hT, v3, y, ident, bias_full, lams, lam_size):
    UN = A_H * NT
    tiles = [list(range(QT_ORDER[n % NT] + 1)) for n in range(UN)]
    runs, before = softmax_chunks(tiles)
    LOADS = 4
    PS, GS = 3, 4
    K = 3 * A_QK
    with ExitStack() as ctx:
        def sb(name, shape, dt):
            return ctx.enter_context(nc.sbuf_tensor(name, shape, dt))

        def sem(name):
            return ctx.enter_context(nc.semaphore(name))

        raw = sb("a_raw", [K, 2, S], F32)
        qs = sb("a_queries", [K, 4, S], F32R)
        ks = sb("a_keys", [K, 4, S], F32R)
        bias = sb("a_bias", [P, 2, S], F32)
        pr = sb("a_probs", [P, 2 * PS, S], F32)
        pth = sb("a_probsT_high", [P, GS, 4, P], F16)
        ptl = sb("a_probsT_low", [P, GS, 4, P], F16)
        nmax = sb("a_negated_max", [P, 2 * PS], F32)
        sums = sb("a_sums", [P, 2 * PS], F32)
        lam_in = sb("a_lam_vectors", [P, 4, A_QK], F32)
        lam = sb("a_lam", [P, 8], F32)
        coef = lam[:, 6:8]
        sc = [ctx.enter_context(nc.psum_tensor(f"a_scores{i}", [P, S], F32)) for i in range(2)]
        tp = [ctx.enter_context(nc.psum_tensor(f"a_turned{i}", [P, 4, P], F32)) for i in range(2)]
        ov = [ctx.enter_context(nc.psum_tensor(f"a_out{i}", [P, 512], F32)) for i in range(2)]

        lam_loaded, lam_chain, lam_exp, lam_ready = sem("lam_loaded"), sem("lam_chain"), sem("lam_exp"), sem("lam_ready")
        raw_in = [sem(f"a_raw_in{i}") for i in range(3)]
        bias_in = [sem(f"a_bias_in{i}") for i in range(2)]
        stack_high, q_ready, k_ready = sem("a_stack_high"), sem("a_queries_ready"), sem("a_keys_ready")
        scored, biased, exped = sem("a_scored"), sem("a_biased"), sem("a_exped")
        chain, mixed = sem("a_mix_chain"), sem("a_mixed")
        turned, t_high, t_low = sem("a_turned"), sem("a_turned_high"), sem("a_turned_low")
        valued, copied = sem("a_valued"), sem("a_copied")
        block = ctx.enter_context(nc.Block())

        def raw_of(j):
            return pr[0:K, 2 * PS - 4 + j, :] if j in (2, 3) else raw[:, j % 2, :]

        @block.sync
        def _(sp):
            for h in range(A_H):
                for m in range(2):
                    for kind in range(2):
                        j = LOADS * h + 2 * m + kind
                        if j >= 4:
                            sp.wait_ge((q_ready, k_ready)[kind], j // 2)
                        src = hT[HD * (h % 2) + A_QK * m:HD * (h % 2) + A_QK * (m + 1), h // 2 + 2 * kind, :]
                        for band in range(3):
                            sp.dma_start(raw_of(j)[A_QK * band:A_QK * (band + 1), :], src).then_inc(raw_in[2 if j in (2, 3) else j % 2], 16)
                if h >= 2:
                    sp.wait_ge(biased, 2 * NT * (h - 1))
                sp.dma_start(bias[:, h % 2, :], bias_full[2 * h + 1]).then_inc(bias_in[h % 2], 16)
                if h == 0:
                    for i in range(4):
                        sp.dma_start(lam_in[:, i, :], lams[i:i + 1, :].partition_broadcast(P)).then_inc(lam_loaded, 16)

        @block.scalar
        def _(act):
            def stack(j):
                h, m, kind = j // LOADS, j % LOADS // 2, j % 2
                if j in (2, 3):
                    act.wait_ge(raw_in[2], 96)
                else:
                    act.wait_ge(raw_in[j % 2], 48 * max(j // 2, 1))
                if h >= 2:
                    act.wait_ge(scored, 2 * NT * (h - 1))
                dst = (qs, ks)[kind]
                nc.scalar.activation(dst[:, 2 * (h % 2) + m, :], raw_of(j), ACT.Copy,
                                     scale=A_QK ** -0.5 if kind == 0 else 1.0).then_inc(stack_high, 1)

            def exponential(n, m):
                w = len(tiles[n]) * P
                act.wait_ge(biased, 2 * n + m + 1)
                s = 2 * (n % PS) + m
                nc.scalar.activation(pr[:, s, 0:w], pr[:, s, 0:w], ACT.Exp, scale=-1.0, bias=nmax[:, s:s + 1],
                                     accum_out=sums[:, s:s + 1]).then_inc(exped, 1)

            def high_part(n):
                for r, run in enumerate(runs[n]):
                    g = before[n] + r
                    act.wait_ge(turned, g + 1)
                    if g >= GS:
                        act.wait_ge(valued, g + 1 - GS)
                    k = len(run)
                    nc.scalar.activation(pth[:, g % GS, 0:k, :], tp[g % 2][:, 0:k, :], ACT.Copy,
                                         scale=PSCALE).then_inc(t_high, 1)

            def write_out(h):
                act.wait_ge(valued, before[NT * (h + 1)])
                nc.scalar.copy(y[:, :, HD * h:HD * (h + 1)],
                               ov[h % 2][:, :].rearrange("p (q d) -> p q d", q=NT)).then_inc(copied, 1)

            for j in range(LOADS):
                stack(j)
            act.wait_ge(lam_ready, 1)
            nc.scalar.activation(lam[:, 2:4], lam[:, 0:2], ACT.Exp).then_inc(lam_exp, 1)
            for m in range(2):
                exponential(0, m)
            for n in range(UN):
                h, pos = n // NT, n % NT
                if n + 1 < UN:
                    exponential(n + 1, 0)
                high_part(n)
                if n + 1 < UN:
                    exponential(n + 1, 1)
                if 1 <= pos <= LOADS and h + 1 < A_H:
                    stack(LOADS * (h + 1) + pos - 1)
                if pos == 2 and h >= 1:
                    write_out(h - 1)
            write_out(A_H - 1)

        @block.vector
        def _(dve):
            def stack(j):
                h, m = j // LOADS, j % LOADS // 2
                dve.wait_ge(stack_high, j + 1)
                low = qs[A_QK:2 * A_QK, 2 * (h % 2) + m, :]
                nc.vector.scalar_tensor_tensor(out=low, in0=raw_of(j)[A_QK:2 * A_QK, :], scalar=A_QK ** -0.5,
                                               in1=low.bitcast(F32), op0=ALU.mult, op1=ALU.subtract).then_inc(q_ready, 1)

            def add_bias(n, m):
                w = len(tiles[n]) * P
                at = score_layout(len(tiles[n]))[0]
                h = n // NT
                if n % NT == 0 and m == 0:
                    dve.wait_ge(bias_in[h % 2], 16 * (h // 2 + 1))
                if n >= PS and m == 0:
                    dve.wait_ge(turned, before[n + 1 - PS])
                if n == PS - 1:
                    dve.wait_ge(k_ready, LOADS // 2)
                dve.wait_ge(scored, 2 * n + m + 1)
                s = 2 * (n % PS) + m
                nc.vector.tensor_tensor_reduce(out=pr[:, s, 0:w], in0=sc[m][:, at:at + w], in1=bias[:, h % 2, S - w:S],
                                               scale=-1.0, scalar=BIG, op0=ALU.add, op1=ALU.min,
                                               accum_out=nmax[:, s:s + 1]).then_inc(biased, 1)

            def mix(n):
                w = len(tiles[n]) * P
                s = 2 * (n % PS)
                dve.wait_ge(exped, 2 * n + 2)
                both = sums[:, s:s + 2]
                mc.link(nc.vector.reciprocal(both, both))
                mc.link(nc.vector.tensor_tensor(both, both, coef, ALU.mult))
                mc.link(nc.vector.tensor_scalar(pr[:, s + 1, 0:w], pr[:, s + 1, 0:w], sums[:, s + 1:s + 2], None, ALU.mult))
                nc.vector.scalar_tensor_tensor(out=pr[:, s, 0:w], in0=pr[:, s, 0:w], scalar=sums[:, s:s + 1],
                                               in1=pr[:, s + 1, 0:w], op0=ALU.mult, op1=ALU.add).then_inc(mixed, 1)

            def low_part(n):
                for r, run in enumerate(runs[n]):
                    g = before[n] + r
                    dve.wait_ge(t_high, g + 1)
                    k = len(run)
                    nc.vector.scalar_tensor_tensor(out=ptl[:, g % GS, 0:k, :], in0=tp[g % 2][:, 0:k, :], scalar=PSCALE,
                                                   in1=pth[:, g % GS, 0:k, :], op0=ALU.mult,
                                                   op1=ALU.subtract).then_inc(t_low, 1)

            stack(0)
            stack(2)
            lc = Chain(dve, lam_chain)
            dve.wait_ge(lam_loaded, 64)
            for i in range(2):
                lc.link(nc.vector.tensor_tensor_reduce(out=lam_in[:, 2 * i, :], in0=lam_in[:, 2 * i, :],
                                                       in1=lam_in[:, 2 * i + 1, :], scale=1.0, scalar=0.0,
                                                       op0=ALU.mult, op1=ALU.add, accum_out=lam[:, i:i + 1]))
            nc.vector.tensor_copy(lam[:, 4:5], lam[:, 0:1]).then_inc(lam_ready, 1)
            for m in range(2):
                add_bias(0, m)
            dve.wait_ge(lam_exp, 1)
            lc.link(nc.vector.tensor_tensor(lam[:, 4:5], lam[:, 2:3], lam[:, 3:4], ALU.subtract))
            lc.link(nc.vector.tensor_scalar(lam[:, 4:5], lam[:, 4:5], LAM_INIT, None, ALU.add))
            lc.link(nc.vector.tensor_scalar(lam[:, 5:6], lam[:, 4:5], -1.0, None, ALU.mult))
            lc.link(nc.vector.tensor_tensor(lam[:, 5:6], lam[:, 5:6], lam[:, 4:5], ALU.max))
            lc.link(nc.vector.tensor_scalar(lam[:, 5:6], lam[:, 5:6], 1.0, None, ALU.add))
            lc.link(nc.vector.tensor_copy(lam_size[:, :], lam[:, 5:6]))
            lc.link(nc.vector.reciprocal(coef[:, 0:1], lam[:, 5:6]))
            lc.link(nc.vector.scalar_tensor_tensor(out=coef[:, 1:2], in0=lam[:, 4:5], scalar=-1.0, in1=coef[:, 0:1],
                                                   op0=ALU.mult, op1=ALU.mult))
            mc = Chain(dve, chain)
            mix(0)
            for m in range(2):
                add_bias(1, m)
            for n in range(UN):
                h, pos = n // NT, n % NT
                if n + 2 < UN:
                    add_bias(n + 2, 0)
                low_part(n)
                if n + 1 < UN:
                    mix(n + 1)
                if n + 2 < UN:
                    add_bias(n + 2, 1)
                if pos in range(1, LOADS, 2) and h + 1 < A_H:
                    stack(LOADS * (h + 1) + pos - 1)

        @block.gpsimd
        def _(pool):
            for j in range(1, LOADS * A_H, 2):
                h, m = j // LOADS, j % LOADS // 2
                pool.wait_ge(stack_high, j + 1)
                low = ks[2 * A_QK:K, 2 * (h % 2) + m, :]
                nc.gpsimd.tensor_tensor(low, raw_of(j)[2 * A_QK:K, :], low.bitcast(F32), ALU.subtract).then_inc(k_ready, 1)

        @block.tensor
        def _(pe):
            def scores(n, m):
                h, qt = n // NT, QT_ORDER[n % NT]
                if n % NT == 0 and m == 0:
                    pe.wait_ge(q_ready, LOADS // 2 * (h + 1))
                    pe.wait_ge(k_ready, LOADS // 2 * (h + 1))
                if n >= 1:
                    pe.wait_ge(biased, 2 * (n - 1) + m + 1)
                s = 2 * (h % 2) + m
                for at, key, w in score_layout(max(qt + 1, 2))[1]:
                    mm = nc.tensor.matmul(sc[m][:, at:at + w], qs[:, s, qt * P:(qt + 1) * P], ks[:, s, key:key + w],
                                          start=True, stop=True)
                mm.then_inc(scored, 1)

            def turn(n):
                pe.wait_ge(mixed, n + 1)
                for r, run in enumerate(runs[n]):
                    g = before[n] + r
                    if g >= 2:
                        pe.wait_ge(t_low, g - 1)
                    transpose_run(pe, nc, tp[g % 2], pr[:, 2 * (n % PS), :], run, 0, ident).then_inc(turned, 1)

            def values(n):
                h, qt = n // NT, QT_ORDER[n % NT]
                if n % NT == 0 and h >= 2:
                    pe.wait_ge(copied, h - 1)
                for r, run in enumerate(runs[n]):
                    g = before[n] + r
                    pe.wait_ge(t_low, g + 1)
                    values_run(nc, ov[h % 2][:, HD * qt:HD * (qt + 1)], pth[:, g % GS], ptl[:, g % GS], run,
                               lambda kt: v3[:, kt, h, :, :], r == 0, r == len(runs[n]) - 1).then_inc(valued, 1)

            for n in range(2):
                for m in range(2):
                    scores(n, m)
            for n in range(UN):
                if n + 2 < UN:
                    scores(n + 2, 0)
                turn(n)
                if n >= 1:
                    values(n - 1)
                if n + 2 < UN:
                    scores(n + 2, 1)
            values(UN - 1)


def swa_compress_phase(nc, hT, v3, y, ident, bias_swa, sinks, w1, w2k, w2v, pe_pairs, kch, kcl, vc3):
    UN = B_H * NT
    RB = B_H // KV
    tiles = [list(range(max(n % NT - 1, 0), n % NT + 1)) for n in range(UN)]
    LOADS = 1 + RB
    SS, TS, GS = 3, 2, 4
    NC2 = KV * NCMP
    DATA = (slice(0, NC2), slice(NCMP, NCMP + NC2))
    PE_AT = (NC2, 32)
    FROM = NT
    with ExitStack() as ctx:
        def sb(name, shape, dt):
            return ctx.enter_context(nc.sbuf_tensor(name, shape, dt))

        def sem(name):
            return ctx.enter_context(nc.semaphore(name))

        raw = sb("b_raw", [P, LOADS, S], F32)
        qs = sb("b_queries", [P, B_H, S], F32R)
        kh = sb("b_keys_high", [P, KV, S], F32R)
        kl = sb("b_keys_low", [P, KV, S], F32R)
        bias = sb("b_bias", [P, KV, RB, BW], F32)
        pr = sb("b_probs", [P, GS, BW], F32)
        pth = sb("b_probsT_high", [P, GS, 2, P], F16)
        ptl = sb("b_probsT_low", [P, GS, 2, P], F16)
        nmax = sb("b_negated_max", [P, B_H, NT], F32)
        sums = sb("b_sums", [P, B_H, NT], F32)
        sink_exp = sb("b_sink_exp", [P, B_H, NT], F32)
        sink = sb("b_sink", [P, B_H], F32)
        nsink = sb("b_negated_sink", [P, B_H], F32)
        sc = [ctx.enter_context(nc.psum_tensor(f"b_scores{i}", [P, 512], F32)) for i in range(SS)]
        tp = [ctx.enter_context(nc.psum_tensor(f"b_turned{i}", [P, 4, P], F32)) for i in range(TS)]
        ov = [ctx.enter_context(nc.psum_tensor(f"b_out{i}", [P, 512], F32)) for i in range(2)]

        cc = sb("c_pairs", [P, 2 * KV + 1, S], F32)
        w1s = hT[:, 0:4, :].rearrange("p a n -> p (a n)").rearrange("p (v l n) -> p v l n", v=2, l=CPL)
        w2ks = sb("c_w2k", [P, P], F32)
        w2vs = sb("c_w2v", [P, HD], F32)
        pes = sb("c_pe", [P, 2, CPL], F32)
        z = sb("c_hidden", [P, 2, NC2], F32)
        e = sb("c_hidden_exp", [P, 2, NC2], F32)
        rest = sb("c_value_rest", [P, KV, HD], F32)
        hid = ctx.enter_context(nc.psum_tensor("c_hidden_sums", [P, 2, (KV + 1) * NCMP], F32))
        kp, vp = sc[0], tp
        w_in, w2_in, pe_in, cc_in = sem("c_w1_in"), sem("c_w2_in"), sem("c_pe_in"), sem("c_pairs_in")
        zeroed, placed, hidden, c_biased, c_exped = sem("c_zeroed"), sem("c_pe_placed"), sem("c_hidden_done"), sem("c_hid_biased"), sem("c_hid_exp")
        act_ready, keyed, c_valued = sem("c_silu"), sem("c_keyed"), sem("c_value_done")
        key_high, first, rested, second = sem("c_key_high"), sem("c_value_first"), sem("c_value_rest_done"), sem("c_value_second")

        next_in = sem("next_queries_in")
        raw_in = [sem(f"b_raw_in{i}") for i in range(LOADS)]
        bias_in, sink_in = sem("b_bias_in"), sem("b_sink_in")
        stack_high, stack_ready = sem("b_stack_high"), sem("b_stack_ready")
        scored, biased, exped, sink_exped = sem("b_scored"), sem("b_biased"), sem("b_exped"), sem("b_sink_exped")
        turned, t_high, t_low = sem("b_turned"), sem("b_turned_high"), sem("b_turned_low")
        valued, chain, headed = sem("b_valued"), sem("b_chain"), sem("b_headed")
        block = ctx.enter_context(nc.Block())

        def stack_at(n):
            return {2 * i + 1: LOADS + i for i in range(LOADS)}.get(n)

        @block.sync
        def _(sp):
            for j in range(LOADS * KV):
                c, i = j // LOADS, j % LOADS
                if c > 0:
                    sp.wait_ge(stack_ready, i + 1)
                src = hT[0:HD, c + 6, :] if i == 0 else hT[HD * (i - 1):HD * i, c + 4, :]
                for band in range(2):
                    sp.dma_start(raw[HD * band:HD * (band + 1), i, :], src).then_inc(raw_in[i], 16)
                if j == 1:
                    for g in range(KV):
                        sp.dma_start(sink[:, RB * g:RB * (g + 1)], sinks[g].partition_broadcast(P)).then_inc(sink_in, 16)
                        sp.dma_start(bias[:, g, :, :], bias_swa[g]).then_inc(bias_in, 16)
                if j == LOADS - 1:
                    sp.dma_start(pes[:, :, :], pe_pairs).then_inc(pe_in, 16)
                    sp.dma_start(w1s, w1).then_inc(w_in, 16)
            for kv in range(2):
                for g in range(KV):
                    src = hT[HD:P, 8 + g, :] if kv == 0 else hT[HD * g:HD * (g + 1), 14, :]
                    group = (KV + 1) * kv + g
                    sp.dma_start(cc[0:HD, group, :], src).then_inc(cc_in, 16)
                    sp.dma_start(cc[HD:P, group, 0:S - 1], src[:, 1:S]).then_inc(cc_in, 16)
            sp.dma_start(w2ks[:, :], w2k).then_inc(w2_in, 16)
            sp.dma_start(w2vs[:, :], w2v).then_inc(w2_in, 16)
            sp.wait_ge(stack_ready, LOADS * KV)
            for j in range(2):
                for band in range(2):
                    sp.dma_start(hT[HD * band:HD * (band + 1), 4 + j, :], hT[HD * j:HD * (j + 1), 10, :]).then_inc(next_in, 16)
            sp.wait_ge(next_in, 64)

        @block.scalar
        def _(act):
            def stack(j):
                c, i = j // LOADS, j % LOADS
                act.wait_ge(raw_in[i], 32 * (c + 1))
                if i == 0:
                    nc.scalar.copy(kh[:, c, :], raw[:, i, :]).then_inc(stack_high, 1)
                else:
                    nc.scalar.activation(qs[:, RB * c + i - 1, :], raw[:, i, :], ACT.Copy,
                                         scale=HD ** -0.5).then_inc(stack_high, 1)

            def exponentials(n):
                w = len(tiles[n]) * P
                h, qt = n // NT, n % NT
                act.wait_ge(biased, n + 1)
                nc.scalar.activation(pr[:, n % GS, 0:w], pr[:, n % GS, 0:w], ACT.Exp, scale=-1.0,
                                     bias=nmax[:, h, qt:qt + 1], accum_out=sums[:, h, qt:qt + 1]).then_inc(exped, 1)
                if qt == NT - 1:
                    nc.scalar.activation(sink_exp[:, h, :], nmax[:, h, :], ACT.Exp,
                                         bias=sink[:, h:h + 1]).then_inc(sink_exped, 1)

            def high_part(n):
                act.wait_ge(turned, n + 1)
                if n >= GS:
                    act.wait_ge(valued, n + 1 - GS)
                k = len(tiles[n])
                nc.scalar.activation(pth[:, n % GS, 0:k, :], tp[n % TS][:, 0:k, :], ACT.Copy,
                                     scale=PSCALE).then_inc(t_high, 1)

            for j in range(LOADS):
                stack(j)
            exponentials(0)
            exponentials(1)
            for n in range(UN):
                if n + 2 < UN:
                    exponentials(n + 2)
                high_part(n)
                if stack_at(n):
                    stack(stack_at(n))
            for kv in range(2):
                act.wait_ge(c_biased, kv + 1)
                nc.scalar.activation(e[:, kv, :], z[:, kv, :], ACT.Exp, scale=-1.0).then_inc(c_exped, 1)
            act.wait_ge(keyed, 1)
            act.wait_ge(zeroed, 3)
            nc.scalar.activation(kch[:, :, 0:NCMP], kp[:, 0:NC2].rearrange("p (g n) -> p g n", g=KV), ACT.Copy,
                                 scale=HD ** -0.5).then_inc(key_high, 1)
            for g in range(KV):
                act.wait_ge(c_valued, g + 1)
                for half in range(2):
                    rows = slice(HD * half, HD * half + NCMP)
                    nc.scalar.copy(vc3[rows, g, 0, :], vp[g][rows, 0, 0:HD]).then_inc(first, 1)

        @block.vector
        def _(dve):
            ch = Chain(dve, chain)

            def stack(j):
                c, i = j // LOADS, j % LOADS
                dve.wait_ge(stack_high, j + 1)
                if i == 0:
                    nc.vector.tensor_tensor(kl[:, c, :], raw[:, i, :], kh[:, c, :].bitcast(F32),
                                            ALU.subtract).then_inc(stack_ready, 1)
                else:
                    low = qs[HD:P, RB * c + i - 1, :]
                    nc.vector.scalar_tensor_tensor(out=low, in0=raw[HD:P, i, :], scalar=HD ** -0.5, in1=low.bitcast(F32),
                                                   op0=ALU.mult, op1=ALU.subtract).then_inc(stack_ready, 1)

            def add_bias(n):
                w = len(tiles[n]) * P
                h, qt = n // NT, n % NT
                if n >= GS:
                    dve.wait_ge(turned, n + 1 - GS)
                dve.wait_ge(scored, n + 1)
                nc.vector.tensor_tensor_reduce(out=pr[:, n % GS, 0:w], in0=sc[n % SS][:, 0:w],
                                               in1=bias[:, h // RB, h % RB, BW - w:BW],
                                               scale=-1.0, scalar=nsink[:, h:h + 1], op0=ALU.add, op1=ALU.min,
                                               accum_out=nmax[:, h, qt:qt + 1]).then_inc(biased, 1)

            def low_part(n):
                dve.wait_ge(t_high, n + 1)
                k = len(tiles[n])
                nc.vector.scalar_tensor_tensor(out=ptl[:, n % GS, 0:k, :], in0=tp[n % TS][:, 0:k, :], scalar=PSCALE,
                                               in1=pth[:, n % GS, 0:k, :], op0=ALU.mult,
                                               op1=ALU.subtract).then_inc(t_low, 1)

            def write_out(h):
                dve.wait_ge(sink_exped, h + 1)
                s = sums[:, h, :]
                ch.link(nc.vector.tensor_tensor(s, s, sink_exp[:, h, :], ALU.add))
                ch.link(nc.vector.tensor_scalar(s, s, PSCALE, None, ALU.mult))
                ch.link(nc.vector.reciprocal(s, s))
                dve.wait_ge(valued, NT * (h + 1))
                nc.vector.tensor_tensor(y[:, :, HD * (A_H + h):HD * (A_H + h + 1)],
                                        ov[h % 2][:, :].rearrange("p (q d) -> p q d", q=NT),
                                        s.unsqueeze(2).broadcast_to([P, NT, HD]), ALU.mult).then_inc(headed, 1)

            ch.link(nc.vector.memset(cc[:, KV, :], 0.0))
            nc.vector.memset(kch[:, :, NCMP:HD].bitcast(F32), 0.0).then_inc(zeroed, 1)
            nc.vector.memset(kcl[:, :, NCMP:HD].bitcast(F32), 0.0).then_inc(zeroed, 1)
            nc.vector.memset(vc3[:, :, :, :], 0.0).then_inc(zeroed, 1)
            for j in range(LOADS):
                stack(j)
            dve.wait_ge(sink_in, 16 * KV)
            ch.link(nc.vector.tensor_scalar(nsink[:, :], sink[:, :], -1.0, None, ALU.mult))
            dve.wait_ge(bias_in, 16 * KV)
            add_bias(0)
            add_bias(1)
            add_bias(2)
            for n in range(UN):
                if n + 3 < UN:
                    add_bias(n + 3)
                if n == FROM - 2:
                    dve.wait_ge(pe_in, 16)
                    for kv in range(2):
                        nc.vector.tensor_copy(cc[:, KV, 512 * kv:512 * kv + 2 * CPL:2], pes[:, kv, :]).then_inc(placed, 1)
                low_part(n)
                if stack_at(n):
                    stack(stack_at(n))
                if n % NT == 3 and n > NT:
                    write_out(n // NT - 1)
            write_out(B_H - 1)
            for kv in range(2):
                dve.wait_ge(hidden, 2)
                nc.vector.tensor_scalar(z[:, kv, :], hid[:, kv, DATA[kv]], hid[:, kv, PE_AT[kv]:PE_AT[kv] + 1], None,
                                        ALU.add).then_inc(c_biased, 1)
            for kv in range(2):
                dve.wait_ge(c_exped, kv + 1)
                ch.link(nc.vector.tensor_scalar(e[:, kv, :], e[:, kv, :], 1.0, None, ALU.add))
                ch.link(nc.vector.reciprocal(e[:, kv, :], e[:, kv, :]))
                nc.vector.tensor_tensor(z[:, kv, :], z[:, kv, :], e[:, kv, :], ALU.mult).then_inc(act_ready, 1)
            dve.wait_ge(key_high, 1)
            ch.link(nc.vector.scalar_tensor_tensor(out=kcl[:, :, 0:NCMP], scalar=HD ** -0.5,
                                                   in0=kp[:, 0:NC2].rearrange("p (g n) -> p g n", g=KV),
                                                   in1=kch[:, :, 0:NCMP].bitcast(F32), op0=ALU.mult, op1=ALU.subtract))
            for g in range(KV):
                dve.wait_ge(first, 2 * g + 2)
                for half in range(2):
                    rows = slice(HD * half, HD * half + NCMP)
                    nc.vector.tensor_tensor(rest[rows, g, :], vp[g][rows, 0, 0:HD], vc3[rows, g, 0, :],
                                            ALU.subtract).then_inc(rested, 1)
            for g in range(KV):
                for half in range(2):
                    rows = slice(HD * half, HD * half + NCMP)
                    dve.wait_ge(rested, 2 * g + half + 1)
                    nc.vector.tensor_copy(vc3[rows, g, 1, :], rest[rows, g, :]).then_inc(second, 1)
            for g in range(KV):
                for half in range(2):
                    rows = slice(HD * half, HD * half + NCMP)
                    dve.wait_ge(second, 2 * g + half + 1)
                    nc.vector.tensor_tensor(vc3[rows, g, 2, :], rest[rows, g, :], vc3[rows, g, 1, :], ALU.subtract)

        @block.tensor
        def _(pe):
            def scores(n):
                h, qt = n // NT, n % NT
                if qt == 0:
                    pe.wait_ge(stack_ready, LOADS * (h // RB) + h % RB + 2)
                if n >= SS:
                    pe.wait_ge(biased, n + 1 - SS)
                q = qs[:, h, qt * P:(qt + 1) * P]
                keys = slice(max(qt - 1, 0) * P, max(qt - 1, 0) * P + BW)
                nc.tensor.matmul(sc[n % SS][:, 0:BW], q, kh[:, h // RB, keys], start=True, stop=False)
                nc.tensor.matmul(sc[n % SS][:, 0:BW], q, kl[:, h // RB, keys], start=False, stop=True).then_inc(scored, 1)

            def turn(n):
                pe.wait_ge(exped, n + 1)
                if n >= TS:
                    pe.wait_ge(t_low, n + 1 - TS)
                transpose_run(pe, nc, tp[n % TS], pr[:, n % GS, :], tiles[n], tiles[n][0], ident).then_inc(turned, 1)

            def values(n):
                h, qt = n // NT, n % NT
                if qt == 0 and h >= 2:
                    pe.wait_ge(headed, h - 1)
                pe.wait_ge(t_low, n + 1)
                values_run(nc, ov[h % 2][:, HD * qt:HD * (qt + 1)], pth[:, n % GS], ptl[:, n % GS], tiles[n],
                           lambda kt: v3[:, kt, A_H + h // RB, :, :], True, True).then_inc(valued, 1)

            def compress(at):
                kv, lp = at // CPL, at % CPL
                out = hid[:, kv, :].rearrange("p (g n) -> p g n", g=KV + 1)
                groups = slice(KV * kv, KV * kv + KV + 1)
                mm = nc.tensor.matmul(out, w1s[:, kv, lp, :], cc[:, groups, 2 * lp:2 * lp + 16 * (NCMP - 1) + 1:16],
                                      start=(lp == 0), stop=(lp == CPL - 1))
                if lp == CPL - 1:
                    mm.then_inc(hidden, 1)

            scores(0)
            scores(1)
            scores(2)
            for n in range(UN):
                if n + 3 < UN:
                    scores(n + 3)
                turn(n)
                if n >= 2:
                    values(n - 2)
                if n == FROM:
                    pe.wait_ge(w_in, 16)
                    pe.wait_ge(placed, 2)
                    pe.wait_ge(cc_in, 16 * 4 * KV)
                if n >= FROM:
                    for at in range(2 * CPL * (n - FROM) // (UN - FROM), 2 * CPL * (n + 1 - FROM) // (UN - FROM)):
                        compress(at)
            values(UN - 2)
            values(UN - 1)
            pe.wait_ge(w2_in, 32)
            pe.wait_ge(act_ready, 1)
            pe.wait_ge(biased, UN)
            pe.wait_ge(t_low, UN)
            nc.tensor.matmul(kp[:, 0:NC2], w2ks[:, :], z[:, 0, :], start=True, stop=True).then_inc(keyed, 1)
            pe.wait_ge(act_ready, 2)
            for g in range(KV):
                for half in range(2):
                    mm = nc.tensor.matmul(vp[g][HD * half:HD * half + NCMP, 0, 0:HD], z[:, 1, NCMP * g:NCMP * (g + 1)],
                                          w2vs[:, :], start=True, stop=True)
                mm.then_inc(c_valued, 1)


def nsa_phase(nc, hT, v3, y, ident, kch, kcl, vc3, glog, bias_full, bias_win, bias_cmp, row_valid, force, blocks,
              w_out, final_row):
    HU = 2 * NT
    UN = C_H * HU
    tiles = []
    for n in range(UN):
        qt = QT_ORDER[n % NT]
        tiles.append(list(range(max(qt - 4, 0), qt + 1)) if n % HU < NT else list(range(qt + 1)))
    runs, before = softmax_chunks(tiles)
    AHEAD = 2
    PS, TS, GS = 4, 3, 6
    PAIRS = NT // 2
    GU = RC * HU
    with ExitStack() as ctx:
        def sb(name, shape, dt):
            return ctx.enter_context(nc.sbuf_tensor(name, shape, dt))

        def sem(name):
            return ctx.enter_context(nc.semaphore(name))

        raw = hT[:, 4:6, :]
        bf = [hT[:, 3, :], hT[:, 2, :]]
        bc = hT[:, 2, :].rearrange("p (s n) -> p s n", s=2)
        cp = hT[:, 0, :].rearrange("p (s n) -> p s n", s=2)
        blk_in = hT[:, 1, :]
        pr = hT[:, 10:10 + PS, :]
        qs = sb("s_queries", [P, C_H, S], F32R)
        kh = sb("s_keys_high", [P, 2, S], F32R)
        kl = sb("s_keys_low", [P, 2, S], F32R)
        bw = sb("s_bias_window", [P, 2, CW], F32)
        pth = sb("s_probsT_high", [P, GS, 4, P], F16)
        ptl = sb("s_probsT_low", [P, GS, 4, P], F16)
        nmax = sb("s_negated_max", [P, 4, NT], F32)
        sums = sb("s_sums", [P, 4, NT], F32)
        red = sb("s_out", [P, 2, NT, HD], F32)
        cmax = sb("s_cmp_max", [P, C_H, NT], F32)
        csum = sb("s_cmp_sums", [P, C_H, NT], F32)
        pbar = sb("s_cmp_probs_sum", [P, 2, SEL_T * HD], F32)
        imp = sb("s_importance", [P, SEL_T, NSLC], F32)
        tail = sb("s_importance_tail", [P, SEL_T, NSLC], F32)
        left = sb("s_not_chosen_scores", [P, SEL_T, NSLC], F32)
        top8 = sb("s_top8", [P, SEL_T, 8], F32)
        unsel = sb("s_not_chosen", [P, KV, SEL_T, 32], F32)
        unselT = sb("s_not_chosenT", [P, KV, P], BF16)
        valid0 = sb("s_row_valid", [P, NT], F32)
        forced = sb("s_forced", [P, SEL_T, NSLC], F32)
        blk = sb("s_blocks", [P, S], BF16)
        gate = sb("s_gates", [P, NT, 3 * C_H], F32)
        sc = [ctx.enter_context(nc.psum_tensor(f"s_scores{i}", [P, (2 - i) * 512], F32)) for i in range(2)]
        tp = [ctx.enter_context(nc.psum_tensor(f"s_turned{i}", [P, 4, P], F32)) for i in range(TS)]
        ov = [ctx.enter_context(nc.psum_tensor(f"s_out{i}", [P, 512], F32)) for i in range(2)]

        const_in, gate_exp = sem("s_const_in"), sem("s_gate_exp")
        raw_in = [sem(f"s_raw_in{i}") for i in range(2)]
        bc_in = [sem(f"s_bias_cmp_in{i}") for i in range(2)]
        bf_in = [sem(f"s_bias_full_in{i}") for i in range(2)]
        bw_in = [sem(f"s_bias_window_in{i}") for i in range(2)]
        stack_high, q_ready, k_ready = sem("s_stack_high"), sem("s_queries_ready"), sem("s_keys_ready")
        c_scored, c_shifted, c_exped, c_normed = sem("c_scored"), sem("c_shifted"), sem("c_exped"), sem("c_normed")
        c_turned, c_high, c_low, c_valued, c_summed = sem("c_turned"), sem("c_high"), sem("c_low"), sem("c_valued"), sem("c_summed")
        w_loaded = sem("w_out_loaded")
        chosen, chosen_turned, mask_ready = sem("s_chosen"), sem("s_chosen_turned"), sem("s_mask_ready")
        scored, biased, exped = sem("s_scored"), sem("s_biased"), sem("s_exped")
        turned, t_high, t_low = sem("s_turned"), sem("s_turned_high"), sem("s_turned_low")
        valued, chain, headed, added = sem("s_valued"), sem("s_chain"), sem("s_headed"), sem("s_added")
        block = ctx.enter_context(nc.Block())

        def c_out(h, half):
            if h % 2 == 0:
                return ov[half][:, 0:PAIRS * HD]
            return sc[1][:, 0:PAIRS * HD] if half == 0 else tp[2][:, 0:2, :].rearrange("p a n -> p (a n)")

        def place(n):
            return n // HU, n % HU // NT, QT_ORDER[n % NT]

        def y_of(h):
            return y[:, :, HD * (A_H + B_H + h):HD * (A_H + B_H + h + 1)]

        def key_stack_at(n):
            return {GU - NT + 2: C_H + 2, GU + 2: C_H + 3}.get(n)

        @block.sync
        def _(sp):
            sp.dma_start(valid0[:, :], row_valid).then_inc(const_in, 16)

            def load_stack(j):
                if j < C_H + 2:
                    sp.wait_ge(q_ready, j - 1)
                else:
                    sp.wait_ge(k_ready, j - 1 - C_H)
                if j < C_H:
                    src = hT[HD * (j % 2):HD * (j % 2 + 1), 10 + j // 2, :]
                else:
                    g = (j - C_H) // 2
                    src = hT[0:HD, 8 + g, :] if j % 2 == 0 else hT[HD:P, 6 + g, :]
                for band in range(2):
                    sp.dma_start(raw[HD * band:HD * (band + 1), j % 2, :], src).then_inc(raw_in[j % 2], 16)

            def load_bias(h):
                if h == 1:
                    sp.wait_ge(c_shifted, C_H)
                if h >= 2:
                    sp.wait_ge(biased, HU * (h - 1))
                sp.dma_start(bf[h % 2], bias_full[h]).then_inc(bf_in[h % 2], 16)
                sp.dma_start(bw[:, h % 2, :], bias_win[h]).then_inc(bw_in[h % 2], 16)

            for j in range(C_H):
                if j >= 2:
                    load_stack(j)
                    sp.wait_ge(c_shifted, j - 1)
                sp.dma_start(bc[:, j % 2, :], bias_cmp[j]).then_inc(bc_in[j % 2], 16)
                if j == 0:
                    sp.dma_start(forced[:, :, :], force).then_inc(const_in, 16)
                    sp.dma_start(blk_in, blocks).then_inc(const_in, 16)
                if j == 2:
                    load_bias(0)
            load_stack(C_H)
            load_stack(C_H + 1)
            load_bias(1)
            load_stack(C_H + 2)
            load_stack(C_H + 3)
            for h in range(2, C_H):
                load_bias(h)
                if h == RC + 1:
                    sp.wait_ge(k_ready, 4)
                    for s, at in enumerate(OUT_SLABS):
                        sp.dma_start(hT[:, at:at + 2, :].rearrange("p a n -> p (a n)"), w_out[s]).then_inc(w_loaded, 16)
                    sp.dma_start(hT[:, 14, :], final_row.partition_broadcast(P)).then_inc(w_loaded, 16)
            sp.wait_ge(w_loaded, 16 * (len(OUT_SLABS) + 1))

        @block.scalar
        def _(act):
            nc.scalar.activation(gate[:, :, :], glog[:, :, :], ACT.Exp, scale=-1.0).then_inc(gate_exp, 1)

            def stack(j):
                if j >= 2:
                    act.wait_ge(raw_in[j % 2], 32 * (j // 2))
                if j < C_H:
                    nc.scalar.copy(qs[:, j, :], raw[:, j % 2, :]).then_inc(stack_high, 1)
                else:
                    if j >= C_H + 2:
                        act.wait_ge(scored, GU - NT if j % 2 == 0 else GU)
                    nc.scalar.activation(kh[:, j % 2, :], raw[:, j % 2, :], ACT.Copy, scale=HD ** -0.5).then_inc(stack_high, 1)

            def c_exponential(h):
                act.wait_ge(c_shifted, h + 1)
                nc.scalar.activation(cp[:, h % 2, :], cp[:, h % 2, :], ACT.Exp).then_inc(c_exped, 1)

            def c_high_part(h):
                act.wait_ge(c_turned, h + 1)
                if h >= 2:
                    act.wait_ge(c_valued, h - 1)
                nc.scalar.activation(pth[:, h % 2, :, :], tp[h % 2][:, :, :], ACT.Copy, scale=PSCALE).then_inc(c_high, 1)

            def exponentials(n):
                w = len(tiles[n]) * P
                hb, qt = n // NT, QT_ORDER[n % NT]
                act.wait_ge(biased, n + 1)
                nc.scalar.activation(pr[:, n % PS, 0:w], pr[:, n % PS, 0:w], ACT.Exp, scale=-1.0,
                                     bias=nmax[:, hb % 4, qt:qt + 1], accum_out=sums[:, hb % 4, qt:qt + 1]).then_inc(exped, 1)

            def high_part(n):
                for i, run in enumerate(runs[n]):
                    g = before[n] + i
                    act.wait_ge(turned, g + 1)
                    if g >= GS:
                        act.wait_ge(valued, g + 1 - GS)
                    k = len(run)
                    nc.scalar.activation(pth[:, g % GS, 0:k, :], tp[g % TS][:, 0:k, :], ACT.Copy,
                                         scale=PSCALE).then_inc(t_high, 1)

            stack(0)
            stack(1)
            stack(2)
            c_exponential(0)
            for h in range(C_H):
                if h + 1 < C_H:
                    c_exponential(h + 1)
                if h + 3 < C_H + 2:
                    stack(h + 3)
                c_high_part(h)
            exponentials(0)
            act.wait_ge(const_in, 48)
            nc.scalar.copy(blk[:, :], blk_in).then_inc(mask_ready, 1)
            act.wait_ge(chosen_turned, 1)
            nc.scalar.copy(unselT[:, :, :], tp[0][:, 0:KV, :]).then_inc(mask_ready, 1)
            act.wait_ge(c_valued, C_H)
            for n in range(UN):
                if n + 1 < UN:
                    exponentials(n + 1)
                high_part(n)
                if key_stack_at(n):
                    stack(key_stack_at(n))

        @block.vector
        def _(dve):
            ch = Chain(dve, chain)

            def gate_of(h, br):
                return gate[:, :, 3 * h + br:3 * h + br + 1]

            def stack(j):
                dve.wait_ge(stack_high, j + 1)
                nc.vector.scalar_tensor_tensor(out=kl[:, j % 2, :], in0=raw[:, j % 2, :], scalar=HD ** -0.5,
                                               in1=kh[:, j % 2, :].bitcast(F32), op0=ALU.mult,
                                               op1=ALU.subtract).then_inc(k_ready, 1)

            def by_tile(h):
                return cp[:, h % 2, :].rearrange("p (t n) -> p t n", t=NT)

            def over_blocks(v):
                return v.unsqueeze(2).broadcast_to([P, NT, HD])

            def shift(h):
                dve.wait_ge(bc_in[h % 2], 16 * (h // 2 + 1))
                dve.wait_ge(c_scored, h + 1)
                if h >= 2:
                    dve.wait_ge(c_turned, h - 1)
                x = by_tile(h)
                ch.link(nc.vector.tensor_tensor(cp[:, h % 2, :], sc[0][:, 512 * (h % 2):512 * (h % 2 + 1)],
                                                bc[:, h % 2, :], ALU.add))
                ch.link(nc.vector.tensor_reduce(cmax[:, h, :], x, AX.X, ALU.max))
                nc.vector.tensor_tensor(x, x, over_blocks(cmax[:, h, :]), ALU.subtract).then_inc(c_shifted, 1)

            def norm(h):
                x = by_tile(h)
                dve.wait_ge(c_exped, h + 1)
                ch.link(nc.vector.tensor_reduce(csum[:, h, :], x, AX.X, ALU.add))
                ch.link(nc.vector.reciprocal(csum[:, h, :], csum[:, h, :]))
                ch.link(nc.vector.tensor_tensor(csum[:, h, :], csum[:, h, :], valid0[:, :], ALU.mult))
                nc.vector.tensor_tensor(x, x, over_blocks(csum[:, h, :]), ALU.mult).then_inc(c_normed, 1)
                dve.wait_ge(c_normed, h + 1)
                late = cp[:, h % 2, SEL_T * HD:NT * HD]
                flushed = pbar[:, 0, :] if h % RC == 0 else pbar[:, 1, :]
                ch.link(nc.vector.scalar_tensor_tensor(out=flushed, in0=late, scalar=TINY, in1=late, op0=ALU.is_ge,
                                                       op1=ALU.mult))
                if h % RC > 0:
                    ch.link(nc.vector.tensor_tensor(pbar[:, 0, :], pbar[:, 0, :], pbar[:, 1, :], ALU.add))

            def c_low_part(h):
                dve.wait_ge(c_high, h + 1)
                nc.vector.scalar_tensor_tensor(out=ptl[:, h % 2, :, :], in0=tp[h % 2][:, :, :], scalar=PSCALE,
                                               in1=pth[:, h % 2, :, :], op0=ALU.mult, op1=ALU.subtract).then_inc(c_low, 1)

            def c_write_out(h):
                dve.wait_ge(c_valued, h + 1)
                for half in range(2):
                    ins = nc.vector.tensor_tensor(y_of(h)[:, half:NT:2, :],
                                                  c_out(h, half).rearrange("p (q d) -> p q d", q=PAIRS),
                                                  gate_of(h, 0)[:, half:NT:2, :].broadcast_to([P, PAIRS, HD]), ALU.mult)
                ins.then_inc(c_summed, 1)

            def choose(g):
                p4 = pbar[:, 0, :].rearrange("p (t j k) -> p t j k", t=SEL_T, k=4)
                ch.link(nc.vector.tensor_tensor(imp[:, :, :], p4[:, :, :, 0], p4[:, :, :, 1], ALU.add))
                ch.link(nc.vector.tensor_tensor(imp[:, :, :], imp[:, :, :], p4[:, :, :, 2], ALU.add))
                ch.link(nc.vector.tensor_scalar(tail[:, :, :], p4[:, :, :, 3], 0.5, None, ALU.mult))
                ch.link(nc.vector.scalar_tensor_tensor(out=tail[:, :, :], in0=tail[:, :, :], scalar=TINY, in1=tail[:, :, :],
                                                       op0=ALU.is_ge, op1=ALU.mult))
                ch.link(nc.vector.tensor_tensor(imp[:, :, :], imp[:, :, :], tail[:, :, :], ALU.add))
                ch.link(nc.vector.tensor_tensor(imp[:, :, 1:NSLC], imp[:, :, 1:NSLC], tail[:, :, 0:NSLC - 1], ALU.add))
                ch.link(nc.vector.tensor_tensor(imp[:, :, :], imp[:, :, :], forced[:, :, :], ALU.add))
                for t in range(SEL_T):
                    ins = nc.vector.max(top8[:, t, :], imp[:, t, :])
                ch.link(ins)
                for t in range(SEL_T):
                    ins = nc.vector.match_replace(left[:, t, :], top8[:, t, :], imp[:, t, :], -BIG)
                ch.link(ins)
                nc.vector.tensor_tensor(unsel[:, g, :, 0:NSLC], left[:, :, :], imp[:, :, :],
                                        ALU.is_equal).then_inc(chosen, 1)
                dve.wait_ge(chosen, g + 1)

            def add_bias(n):
                w = len(tiles[n]) * P
                at = score_layout(len(tiles[n]))[0]
                h, br, qt = place(n)
                if n % NT == 0:
                    dve.wait_ge((bw_in, bf_in)[br][h % 2], 16 * (h // 2 + 1))
                if n == 0:
                    dve.wait_ge(q_ready, C_H)
                if n >= PS:
                    dve.wait_ge(turned, before[n + 1 - PS])
                dve.wait_ge(scored, n + 1)
                b = bw[:, h % 2, CW - w:CW] if br == 0 else bf[h % 2][:, S - w:S]
                nc.vector.tensor_tensor_reduce(out=pr[:, n % PS, 0:w], in0=sc[n % 2][:, at:at + w], in1=b,
                                               scale=-1.0, scalar=BIG, op0=ALU.add, op1=ALU.min,
                                               accum_out=nmax[:, n // NT % 4, qt:qt + 1]).then_inc(biased, 1)

            def low_part(n):
                for i, run in enumerate(runs[n]):
                    g = before[n] + i
                    dve.wait_ge(t_high, g + 1)
                    k = len(run)
                    nc.vector.scalar_tensor_tensor(out=ptl[:, g % GS, 0:k, :], in0=tp[g % TS][:, 0:k, :], scalar=PSCALE,
                                                   in1=pth[:, g % GS, 0:k, :], op0=ALU.mult,
                                                   op1=ALU.subtract).then_inc(t_low, 1)

            def write_out(hb):
                h, br = hb // 2, hb % 2
                s = sums[:, hb % 4, :]
                ch.link(nc.vector.reciprocal(s, s))
                ch.link(nc.vector.tensor_tensor(s.unsqueeze(2), s.unsqueeze(2), gate_of(h, 2 - br), ALU.mult))
                dve.wait_ge(valued, before[NT * (hb + 1)])
                if hb >= 2:
                    dve.wait_ge(added, hb - 1)
                nc.vector.tensor_tensor(red[:, hb % 2, :, :], ov[hb % 2][:, :].rearrange("p (q d) -> p q d", q=NT),
                                        over_blocks(s), ALU.mult).then_inc(headed, 1)

            dve.wait_ge(gate_exp, 1)
            ch.link(nc.vector.tensor_scalar(gate[:, :, :], gate[:, :, :], 1.0, PSCALE, ALU.add, ALU.mult))
            ch.link(nc.vector.reciprocal(gate[:, :, :], gate[:, :, :]))
            ch.link(nc.vector.memset(unsel[:, :, :, :], 0.0))
            dve.wait_ge(const_in, 48)
            shift(0)
            for h in range(C_H):
                if h + 1 < C_H:
                    shift(h + 1)
                if h >= 1:
                    c_low_part(h - 1)
                norm(h)
                if C_H <= h + 3 < C_H + 2:
                    stack(h + 3)
                if h >= 2:
                    c_write_out(h - 2)
                if h == RC - 1:
                    choose(0)
            add_bias(0)
            c_low_part(C_H - 1)
            choose(1)
            c_write_out(C_H - 2)
            c_write_out(C_H - 1)
            add_bias(1)
            dve.wait_ge(c_summed, C_H)
            for n in range(UN):
                if n + AHEAD < UN:
                    add_bias(n + AHEAD)
                low_part(n)
                if key_stack_at(n):
                    stack(key_stack_at(n))
                if n % NT == 2 and n > NT:
                    write_out(n // NT - 1)
            write_out(UN // NT - 1)

        @block.gpsimd
        def _(pool):
            for j in range(C_H):
                pool.wait_ge(stack_high, j + 1)
                low = qs[HD:P, j, :]
                nc.gpsimd.tensor_tensor(low, raw[HD:P, j % 2, :], low.bitcast(F32), ALU.subtract).then_inc(q_ready, 1)
            pool.wait_ge(c_summed, C_H)
            for hb in range(UN // NT):
                pool.wait_ge(headed, hb + 1)
                if hb % 2 == 1:
                    pool.wait_ge(added, hb)
                out = y_of(hb // 2)
                nc.gpsimd.tensor_tensor(out, out, red[:, hb % 2, :, :], ALU.add).then_inc(added, 1)

        @block.tensor
        def _(pe):
            def c_scores(h):
                pe.wait_ge(q_ready, h + 1)
                if h >= 2:
                    pe.wait_ge(c_shifted, h - 1)
                for qt in range(NT):
                    at = 512 * (h % 2) + HD * qt
                    out = sc[0][:, at:at + HD]
                    q = qs[:, h, qt * P:(qt + 1) * P]
                    nc.tensor.matmul(out, q, kch[:, h // RC, :], start=True, stop=False)
                    mm = nc.tensor.matmul(out, q, kcl[:, h // RC, :], start=False, stop=True)
                mm.then_inc(c_scored, 1)

            def c_turn(h):
                pe.wait_ge(c_normed, h + 1)
                if h >= 2:
                    pe.wait_ge(c_low, h - 1)
                for p in range(PAIRS):
                    mm = nc.tensor.transpose(tp[h % 2][:, p, :], cp[:, h % 2, P * p:P * (p + 1)], ident[:, :])
                mm.then_inc(c_turned, 1)

            def c_values(h):
                pe.wait_ge(c_low, h + 1)
                if h >= 2:
                    pe.wait_ge(c_summed, h - 1)
                for half in range(2):
                    for p in range(PAIRS):
                        rows = slice(HD * half, HD * (half + 1))
                        out = c_out(h, half)[:, HD * p:HD * (p + 1)]
                        mm = values_run(nc, out, pth[rows, h % 2, p:p + 1, :], ptl[rows, h % 2, p:p + 1, :], [0],
                                        lambda _: vc3[rows, h // RC, :, :], True, True)
                mm.then_inc(c_valued, 1)

            def scores(n):
                h, br, qt = place(n)
                c = h // RC
                if n % GU in (0, NT):
                    pe.wait_ge(k_ready, 2 * c + br + 1)
                if n < 2:
                    pe.wait_ge(c_shifted, C_H)
                else:
                    pe.wait_ge(biased, n - 1)
                if n == NT:
                    pe.wait_ge(mask_ready, 2)
                q = qs[:, h, qt * P:(qt + 1) * P]
                first = tiles[n][0]
                masked = br == 1 and qt >= SEL_T
                for at, key, w in score_layout(max(len(tiles[n]), 2))[1]:
                    keys = slice(first * P + key, first * P + key + w)
                    out = sc[n % 2][:, at:at + w]
                    nc.tensor.matmul(out, q, kh[:, br, keys], start=True, stop=False)
                    mm = nc.tensor.matmul(out, q, kl[:, br, keys], start=False, stop=not masked)
                    if masked:
                        rows = slice(32 * (qt - SEL_T), 32 * (qt - SEL_T + 1))
                        mm = nc.tensor.matmul(out, unselT[rows, c, :], blk[rows, keys], start=False, stop=True)
                mm.then_inc(scored, 1)

            def turn(n):
                pe.wait_ge(exped, n + 1)
                for i, run in enumerate(runs[n]):
                    g = before[n] + i
                    if g >= TS:
                        pe.wait_ge(t_low, g + 1 - TS)
                    transpose_run(pe, nc, tp[g % TS], pr[:, n % PS, :], run, tiles[n][0], ident).then_inc(turned, 1)

            def values(n):
                h, br, qt = place(n)
                hb = n // NT
                if n % NT == 0 and hb >= 2:
                    pe.wait_ge(headed, hb - 1)
                for i, run in enumerate(runs[n]):
                    g = before[n] + i
                    pe.wait_ge(t_low, g + 1)
                    values_run(nc, ov[hb % 2][:, HD * qt:HD * (qt + 1)], pth[:, g % GS], ptl[:, g % GS], run,
                               lambda kt: v3[:, kt, A_H + KV * (2 - br) + h // RC, :, :],
                               i == 0, i == len(runs[n]) - 1).then_inc(valued, 1)

            c_scores(0)
            c_scores(1)
            for h in range(C_H):
                if h + 2 < C_H:
                    c_scores(h + 2)
                c_turn(h)
                if h >= 1:
                    c_values(h - 1)
            scores(0)
            c_values(C_H - 1)
            pe.wait_ge(chosen, KV)
            for g in range(KV):
                mm = nc.tensor.transpose(tp[0][:, g, :], unsel[:, g, :, :].rearrange("p t j -> p (t j)"), ident[:, :])
            mm.then_inc(chosen_turned, 1)
            pe.wait_ge(mask_ready, 2)
            pe.wait_ge(c_summed, C_H)
            scores(1)
            for n in range(UN):
                if n + AHEAD < UN:
                    scores(n + AHEAD)
                turn(n)
                if n >= 2:
                    values(n - 2)
            values(UN - 2)
            values(UN - 1)


def out_phase(nc, x, gate_dram, subln, out, hT, y, ident, lam_size):
    AW = A_H * HD
    SLABS, W = 4, D // 4
    GS, XS = 2, 4
    with ExitStack() as ctx:
        def sb(name, shape, dt):
            return ctx.enter_context(nc.sbuf_tensor(name, shape, dt))

        def sem(name):
            return ctx.enter_context(nc.semaphore(name))

        raw = [hT[:, at:at + 2, :].rearrange("p a n -> p (a n)").rearrange("p (k n) -> p k n", k=KT) for at in OUT_SLABS]
        squared = hT[:, 0, :]
        gates, res, fn = hT[:, 2:4, :], hT[:, 10:14, :], hT[:, 14, :]
        wh = sb("o_w_high", [P, KT, D], F32R)
        wl = sb("o_w_low", [P, KT, D], F32R)
        yh = sb("o_yT_high", [P, 2, KT, P], F32R)
        yl = sb("o_yT_low", [P, 2, KT, P], F32R)
        sq = sb("o_squares", [P, AW], F32)
        sub = sb("o_subln", [P, HD], F32)
        small = sb("o_small", [P, 4], F32)
        arms = sb("o_a_rstd", [P, NT, A_H], F32)
        ss = sb("o_square_sums", [P, NT], F32)
        rs = sb("o_rstd", [P, NT], F32)
        tp = [ctx.enter_context(nc.psum_tensor(f"o_turned{i}", [P, 4, P], F32)) for i in range(2)]
        acc = [ctx.enter_context(nc.psum_tensor(f"o_acc{i}", [P, 512], F32)) for i in range(4)]

        row_in = sem("o_rows_in")
        g_in = [sem(f"o_gates_in{i}") for i in range(GS)]
        x_in = [sem(f"o_x_in{i}") for i in range(XS)]
        w_high, w_low = sem("o_w_high_done"), sem("o_w_low_done")
        small_ready, a_summed, a_root, a_chain, gated = sem("o_small_ready"), sem("o_a_summed"), sem("o_a_root"), sem("o_a_chain"), sem("o_gated")
        turned, high, low = sem("o_turned"), sem("o_high"), sem("o_low")
        done, added, squares, roots, r_chain, normed = sem("o_done"), sem("o_added"), sem("o_squares_summed"), sem("o_roots"), sem("o_root_chain"), sem("o_normed")
        stored = [sem(f"o_stored{i}") for i in range(XS)]
        block = ctx.enter_context(nc.Block())

        @block.sync
        def _(sp):
            def load_gates(i):
                if i >= GS:
                    sp.wait_ge(gated, i + 1 - GS)
                sp.dma_start(gates[:, i % GS, :], gate_dram[i * P:(i + 1) * P, :]).then_inc(g_in[i % GS], 16)

            def load_x(i):
                if i >= XS:
                    sp.wait_ge(stored[i % XS], 16 * (i // XS))
                sp.dma_start(res[:, i % XS, :], x[i * P:(i + 1) * P, :]).then_inc(x_in[i % XS], 16)

            sp.dma_start(sub[:, :], subln.partition_broadcast(P)).then_inc(row_in, 16)
            load_gates(0)
            load_gates(1)
            load_x(0)
            load_x(1)
            for i in range(NT):
                if i + GS < NT:
                    load_gates(i + GS)
                if i + 2 < NT:
                    load_x(i + 2)
                sp.wait_ge(normed, i + 1)
                sp.dma_start(out[i * P:(i + 1) * P, :], res[:, i % XS, :]).then_inc(stored[i % XS], 16)
            for i in range(XS):
                sp.wait_ge(stored[i], 16 * (NT // XS))

        @block.scalar
        def _(act):
            def a_rstd(i):
                act.wait_ge(small_ready, 1)
                act.wait_ge(a_summed, i + 1)
                nc.scalar.activation(arms[:, i, :], arms[:, i, :], ACT.Sqrt, scale=small[:, 1:2],
                                     bias=small[:, 2:3]).then_inc(a_root, 1)

            def high_part(i):
                for h in range(2):
                    act.wait_ge(turned, 2 * i + h + 1)
                    if i >= 2 and h == 0:
                        act.wait_ge(done, 2 * i - 2)
                    nc.scalar.copy(yh[:, i % 2, 4 * h:4 * h + 4, :], tp[h][:, :, :]).then_inc(high, 1)

            def square(i):
                act.wait_ge(added, 2 * i + 2)
                if i == 0:
                    act.wait_ge(w_low, 1)
                nc.scalar.activation(squared, res[:, i % XS, :], ACT.Square, accum_out=ss[:, i:i + 1]).then_inc(squares, 1)
                act.wait_ge(squares, i + 1)
                nc.scalar.activation(rs[:, i:i + 1], ss[:, i:i + 1], ACT.Sqrt, scale=1.0 / D, bias=small[:, 2:3]).then_inc(roots, 1)

            for s in range(SLABS):
                nc.scalar.copy(wh[:, :, s * W:(s + 1) * W], raw[s]).then_inc(w_high, 1)
                if s == 0:
                    a_rstd(0)
                if s == 1:
                    high_part(0)
            a_rstd(1)
            for i in range(NT):
                if i + 2 < NT:
                    a_rstd(i + 2)
                if i + 1 < NT:
                    high_part(i + 1)
                square(i)

        @block.vector
        def _(dve):
            sc = Chain(dve, a_chain)
            sc.link(nc.vector.tensor_scalar(small[:, 0:1], lam_size[:, :], 1.0 / PSCALE, None, ALU.mult))
            sc.link(nc.vector.tensor_tensor(small[:, 1:2], small[:, 0:1], small[:, 0:1], ALU.mult))
            sc.link(nc.vector.tensor_scalar(small[:, 1:2], small[:, 1:2], 1.0 / HD, None, ALU.mult))
            sc.link(nc.vector.tensor_scalar(small[:, 3:4], small[:, 0:1], 1.0 - LAM_INIT, None, ALU.mult))
            nc.vector.memset(small[:, 2:3], EPS).then_inc(small_ready, 1)
            dve.wait_ge(row_in, 16)
            by_head = lambda t: t.rearrange("p (h d) -> p h d", d=HD)

            def a_squares(i):
                ya = y[:, i, 0:AW]
                sc.link(nc.vector.tensor_tensor(sq[:, :], ya, ya, ALU.mult))
                nc.vector.tensor_reduce(arms[:, i, :], by_head(sq[:, :]), AX.X, ALU.add).then_inc(a_summed, 1)

            def gate(i):
                ya = by_head(y[:, i, 0:AW])
                dve.wait_ge(a_root, i + 1)
                sc.link(nc.vector.reciprocal(arms[:, i, :], arms[:, i, :]))
                sc.link(nc.vector.tensor_scalar(arms[:, i, :], arms[:, i, :], small[:, 3:4], None, ALU.mult))
                sc.link(nc.vector.tensor_tensor(ya, ya, arms[:, i, :].unsqueeze(2).broadcast_to([P, A_H, HD]), ALU.mult))
                sc.link(nc.vector.tensor_tensor(ya, ya, sub[:, :].unsqueeze(1).broadcast_to([P, A_H, HD]), ALU.mult))
                dve.wait_ge(g_in[i % GS], 16 * (i // GS + 1))
                nc.vector.tensor_tensor(y[:, i, :], y[:, i, :], gates[:, i % GS, :], ALU.mult).then_inc(gated, 1)

            def low_part(i):
                for h in range(2):
                    dve.wait_ge(high, 2 * i + h + 1)
                    ks = slice(4 * h, 4 * h + 4)
                    nc.vector.tensor_tensor(yl[:, i % 2, ks, :], tp[h][:, :, :], yh[:, i % 2, ks, :].bitcast(F32),
                                            ALU.subtract).then_inc(low, 1)

            def residual(i):
                for h in range(2):
                    n = 2 * i + h
                    dve.wait_ge(done, n + 1)
                    if h == 0:
                        dve.wait_ge(x_in[i % XS], 16 * (i // XS + 1))
                    cols = slice(512 * h, 512 * h + 512)
                    nc.vector.tensor_tensor(res[:, i % XS, cols], acc[n % 4][:, :], res[:, i % XS, cols], ALU.add).then_inc(added, 1)

            def normalise(i):
                dve.wait_ge(roots, i + 1)
                nc.vector.reciprocal(rs[:, i:i + 1], rs[:, i:i + 1]).then_inc(r_chain, 1)
                dve.wait_ge(r_chain, i + 1)
                nc.vector.scalar_tensor_tensor(out=res[:, i % XS, :], in0=res[:, i % XS, :], scalar=rs[:, i:i + 1], in1=fn,
                                               op0=ALU.mult, op1=ALU.mult).then_inc(normed, 1)

            a_squares(0)
            for s in range(SLABS):
                dve.wait_ge(w_high, s + 1)
                cols = slice(s * W, (s + 1) * W)
                nc.vector.tensor_tensor(wl[:, :, cols], raw[s], wh[:, :, cols].bitcast(F32), ALU.subtract).then_inc(w_low, 1)
                if s == 0:
                    gate(0)
                if s == 1:
                    low_part(0)
            a_squares(1)
            gate(1)
            for i in range(NT):
                if i + 2 < NT:
                    a_squares(i + 2)
                    gate(i + 2)
                if i + 1 < NT:
                    low_part(i + 1)
                residual(i)
                normalise(i)

        @block.tensor
        def _(pe):
            def turn(i):
                pe.wait_ge(gated, i + 1)
                for h in range(2):
                    if i >= 1:
                        pe.wait_ge(low, 2 * i + h - 1)
                    for k in range(4):
                        mm = nc.tensor.transpose(tp[h][:, k, :], y[:, i, (4 * h + k) * P:(4 * h + k + 1) * P], ident[:, :])
                    mm.then_inc(turned, 1)

            def project(i, halves):
                pe.wait_ge(low, 2 * i + 2)
                for h in halves:
                    n = 2 * i + h
                    if n >= 4:
                        pe.wait_ge(added, n - 3)
                    if i == 0:
                        pe.wait_ge(w_low, SLABS // 2 * (h + 1))
                    cols = slice(512 * h, 512 * h + 512)
                    for k in range(KT):
                        nc.tensor.matmul(acc[n % 4][:, :], yh[:, i % 2, k, :], wh[:, k, cols], start=(k == 0), stop=False)
                        nc.tensor.matmul(acc[n % 4][:, :], yh[:, i % 2, k, :], wl[:, k, cols], start=False, stop=False)
                        mm = nc.tensor.matmul(acc[n % 4][:, :], yl[:, i % 2, k, :], wh[:, k, cols], start=False,
                                              stop=(k == KT - 1))
                    mm.then_inc(done, 1)

            turn(0)
            project(0, (0,))
            turn(1)
            project(0, (1,))
            for i in range(1, NT):
                if i + 1 < NT:
                    turn(i + 1)
                project(i, (0, 1))


def decoder_trunk(nc, x, norm_row, w_feat, w_val, w_gate, w_out, lams, subln, sinks, pe_pairs, cmp_w1, cmp_w2k,
                  cmp_w2v, final_row, identity, bias_full, bias_win, bias_swa, bias_cmp, row_valid, force, blocks, out):
    gate_dram = nc.dram_tensor("silu_gates", (S, D), F32, kind="Internal").ap()
    with ExitStack() as ctx:
        def sb(name, shape, dt):
            return ctx.enter_context(nc.sbuf_tensor(name, shape, dt))

        ident = sb("identity", [P, P], F32)
        glog = sb("gate_logits", [P, NT, 3 * C_H], F32)
        kch = sb("cmp_keys_high", [P, KV, HD], F32R)
        kcl = sb("cmp_keys_low", [P, KV, HD], F32R)
        vc3 = sb("cmp_values", [P, KV, 3, HD], BF16)
        lam_size = sb("lam_size", [P, 1], F32)
        hT = sb("features", [P, TC, S], F32)
        with ExitStack() as attention:
            v3 = attention.enter_context(nc.sbuf_tensor("values", [P, NT, VH, 3, HD], BF16))
            with ExitStack() as projection:
                def proj(name, shape, dt):
                    return projection.enter_context(nc.sbuf_tensor(name, shape, dt))

                xh = proj("xT_high", [P, KT, S], F32R)
                xl = proj("xT_low", [P, KT, S], F32R)
                wr = proj("w_raw", [P, 4, KT * P], F32)
                wh = proj("w_high", [P, 4, KT * P], F32R)
                wl = proj("w_low", [P, 4, KT * P], F32R)
                projection_phase(nc, x, norm_row, identity, w_val, w_gate, w_feat, gate_dram, ident, hT, xh, xl,
                                 wr, wh, wl, v3, glog)
            y = attention.enter_context(nc.sbuf_tensor("branches", [P, NT, D], F32))
            diff_phase(nc, hT, v3, y, ident, bias_full, lams, lam_size)
            swa_compress_phase(nc, hT, v3, y, ident, bias_swa, sinks, cmp_w1, cmp_w2k, cmp_w2v, pe_pairs, kch, kcl, vc3)
            nsa_phase(nc, hT, v3, y, ident, kch, kcl, vc3, glog, bias_full, bias_win, bias_cmp, row_valid, force, blocks,
                      w_out, final_row)
            out_phase(nc, x, gate_dram, subln, out, hT, y, ident, lam_size)


def _columns():
    r = np.arange
    qa, ka, va, ga, qb, kb, vb, gb = 0, 256, 512, 768, 1024, 1280, 1408, 1536
    qc, kc, vc, ks, vs, kw, vw, gl, gc = 1792, 2304, 2432, 2560, 2688, 2816, 2944, 3072, 3096
    feat = [r(qa, qa + 128), r(qa + 128, qa + 256), r(ka, ka + 128), r(ka + 128, ka + 256)]
    feat += [r(qb + 128 * g, qb + 128 * g + 128) for g in range(KV)]
    feat += [np.r_[kb + 64 * g:kb + 64 * g + 64, ks + 64 * g:ks + 64 * g + 64] for g in range(KV)]
    feat += [np.r_[kw + 64 * g:kw + 64 * g + 64, kc + 64 * g:kc + 64 * g + 64] for g in range(KV)]
    feat += [r(qc + 128 * c, qc + 128 * c + 128) for c in range(4)] + [r(vc, vc + 128)]
    val = [r(va, va + 256), np.r_[vb:vb + 128, vs:vs + 128], np.r_[vw:vw + 128, gl:gl + 24, gl:gl + 24, gl:gl + 24, gl:gl + 24, gl:gl + 24, gl:gl + 8]]
    gate = [r(ga, ga + 256), r(gb, gb + 256), r(gc, gc + 256), r(gc + 256, gc + 512)]
    return feat, val, gate


def _constants():
    f32 = np.float32
    q = np.arange(P)[:, None]
    t = np.arange(S).reshape(NT, P).T[:, :, None]

    def bias(slope, dist, valid):
        return np.where(valid, -slope * dist, NEG).astype(f32)

    slopes8 = 2.0 ** -np.arange(1, C_H + 1)
    slopes4 = 2.0 ** (-2.0 * np.arange(1, B_H + 1))
    d = q + (S - P) - np.arange(S)[None]
    full = np.stack([bias(s, d, d >= 0) for s in slopes8])
    d = q + (CW - P) - np.arange(CW)[None]
    win = np.stack([bias(s, d, (d >= 0) & (d < 512)) for s in slopes8])
    d = q + (BW - P) - np.arange(BW)[None]
    swa = np.stack([bias(s, d, (d >= 0) & (d < 128)) for s in slopes4]).reshape(KV, 2, P, BW).transpose(0, 2, 1, 3)
    block = np.arange(HD)[None, None]
    d = t - (16 * block + 31)
    cmp = np.stack([bias(s, d, (d >= 0) & (block < NCMP)) for s in slopes8]).reshape(C_H, P, NT * HD)
    row_valid = (t[:, :, 0] >= 31).astype(f32)
    cur = t[:, SEL_T:] // 64
    j = np.arange(NSLC)[None, None]
    force = np.where(j > cur, NEG, np.where((j == 0) | (j == cur) | (j == cur - 1), -NEG, 0)).astype(f32)
    blocks = np.zeros((SEL_T, 32, S), f32)
    for b in range(NSLC):
        blocks[:, b, 64 * b:64 * b + 64] = NEG
    blocks = blocks.reshape(P, S)
    return {"identity": np.eye(P, dtype=f32), "bias_full": full, "bias_win": win, "bias_swa": swa, "bias_cmp": cmp,
            "row_valid": row_valid, "force": force, "blocks": blocks}


def _slab(w, columns):
    w = w if columns is None else w[:, columns]
    return w.reshape(KT, P, w.shape[1]).transpose(1, 0, 2)


def kernel(x, norm_w, w_in, w_out, diff_lq1, diff_lk1, diff_lq2, diff_lk2, diff_subln, sinks, cmp_pe_k, cmp_pe_v,
           cmp_wk1, cmp_wk2, cmp_wv1, cmp_wv2, final_norm):
    import concourse.bacc as bacc
    from concourse.bass_utils import run_bass_kernel_spmd

    feat, val, gate = _columns()
    w = w_in[0]
    pairs = lambda a: a.reshape(CPL, P, -1).transpose(1, 0, 2)
    arrays = {
        "x": x[0], "norm_row": norm_w,
        "w_feat": np.stack([_slab(w, c) for c in feat]),
        "w_val": np.stack([_slab(w, c) for c in val]),
        "w_gate": np.stack([_slab(w, c) for c in gate]),
        "w_out": np.stack([_slab(w_out[0][:, 256 * s:256 * s + 256], None).reshape(P, -1) for s in range(4)]),
        "lams": np.concatenate([diff_lq1, diff_lk1, diff_lq2, diff_lk2]),
        "subln": diff_subln, "sinks": sinks.reshape(KV, 1, B_H // KV),
        "pe_pairs": np.stack([cmp_pe_k[0].reshape(CPL, P).T, cmp_pe_v[0].reshape(CPL, P).T], axis=1),
        "cmp_w1": np.stack([pairs(cmp_wk1[0]), pairs(cmp_wv1[0])], axis=1),
        "cmp_w2k": np.concatenate([cmp_wk2[0], cmp_wk2[0]], axis=1), "cmp_w2v": cmp_wv2[0],
        "final_row": final_norm.reshape(1, D),
    }
    arrays.update(_constants())
    arrays = {k: np.ascontiguousarray(v) for k, v in arrays.items()}
    nc = bacc.Bacc("TRN2", target_bir_lowering=False, num_devices=1)
    args = {k: nc.dram_tensor(f"in_{k}", v.shape, mybir.dt.from_np(v.dtype), kind="ExternalInput").ap() for k, v in arrays.items()}
    out = nc.dram_tensor("out", (S, D), F32, kind="ExternalOutput").ap()
    decoder_trunk(nc, **args, out=out)
    r = run_bass_kernel_spmd(nc, [{f"in_{k}": v for k, v in arrays.items()}], core_ids=[0])
    return r.results[0]["out"].reshape(1, S, D)
```
